# Optimizing a Trainium2 kernel written in Bass

```python
import math
import jax, jax.numpy as jnp
from jax import lax
import numpy as np

D_MODEL = 1024
BATCH = 1
SEQ = 128
DEPTH = 2
DEC_BATCH = 1
DEC_SEQ = 128
PAST_LEN = 128

GRID_W = 64
Q_BLOCK = 128
ROPE_BASE = 10000.0
NORM_EPS = 1e-6

MLA_HEADS = 8
MLA_NOPE = 64
MLA_ROPE = 32
MLA_QK = MLA_NOPE + MLA_ROPE
MLA_V = 64
Q_LORA = 384
KV_LORA = 256
D_RNN = 512
LRU_BLOCKS = 8
LRU_BW = D_RNN // LRU_BLOCKS
CONV_W = 4
CONV_LEFT = 2
LRU_C = 8.0
DIFF_HEADS = 4
DIFF_DH = 64
DIFF_DV = 2 * DIFF_DH
N_EXPERTS = 32
TOP_K = 4
D_EXPERT = 512
SWIGLU_LIMIT = 7.0
SWIGLU_ALPHA = 1.702
N_BRANCH = 3

OFF_QA = 0
OFF_KVA = OFF_QA + Q_LORA
OFF_LRU_X = OFF_KVA + KV_LORA + MLA_ROPE
OFF_LRU_G = OFF_LRU_X + D_RNN
OFF_DQ = OFF_LRU_G + D_RNN
OFF_DK = OFF_DQ + DIFF_HEADS * 2 * DIFF_DH
OFF_DV = OFF_DK + DIFF_HEADS * 2 * DIFF_DH
IN_COLS = OFF_DV + DIFF_HEADS * DIFF_DV

kernel_name = 'hybrid_mla_rglru_diffattn_moe_dit_step'

def _rmsnorm(x, g):
    xf = x.astype(jnp.float32)
    y = xf * lax.rsqrt(jnp.mean(xf * xf, axis=-1, keepdims=True) + NORM_EPS)
    return (y * g.astype(jnp.float32)).astype(x.dtype)

def _modulation(cond, w, b):
    m = jax.nn.silu(cond) @ w + b
    return jnp.split(m[:, None, :], 6, axis=-1)

def _modulate(x, g, shift, scale):
    return _rmsnorm(x, g) * (1.0 + scale) + shift

def _rot_half(x):
    x1, x2 = jnp.split(x, 2, axis=-1)
    return jnp.concatenate([-x2, x1], axis=-1)

def _axial_rope_tables(n_tokens, dim):
    rows = n_tokens // GRID_W
    row = jnp.repeat(jnp.arange(rows), GRID_W)
    col = jnp.tile(jnp.arange(GRID_W), rows)
    half = dim // 2
    inv = 1.0 / (ROPE_BASE ** (jnp.arange(0, half, 2, dtype=jnp.float32) / half))

    def axis_angles(pos):
        ang = pos.astype(jnp.float32)[:, None] * inv[None, :]
        return jnp.concatenate([ang, ang], axis=-1)

    ang = jnp.concatenate([axis_angles(row), axis_angles(col)], axis=-1)
    return jnp.cos(ang), jnp.sin(ang)

def _apply_rope(x, cos, sin):
    shape = (x.shape[1],) + (1,) * (x.ndim - 3) + (x.shape[-1],)
    cos = cos.reshape(shape).astype(x.dtype)
    sin = sin.reshape(shape).astype(x.dtype)
    half = x.shape[-1] // 2
    rot = jnp.concatenate([_rot_half(x[..., :half]), _rot_half(x[..., half:])], axis=-1)
    return x * cos + rot * sin

def _rope_tail(x, cos, sin, n_plain):
    return jnp.concatenate([x[..., :n_plain], _apply_rope(x[..., n_plain:], cos, sin)], axis=-1)

def _over_query_blocks(fn, q):
    b, s = q.shape[0], q.shape[1]
    nb = s // Q_BLOCK
    qb = jnp.moveaxis(q.reshape((b, nb, Q_BLOCK) + q.shape[2:]), 1, 0)
    out = jnp.moveaxis(lax.map(fn, qb), 0, 1)
    return out.reshape((b, s) + out.shape[3:])

def _mla_attend(q, k, v):
    scale = MLA_QK ** -0.5

    def block(qb):
        s = jnp.einsum('bqhd,bkhd->bhqk', qb, k).astype(jnp.float32) * scale
        p = jax.nn.softmax(s, axis=-1).astype(v.dtype)
        return jnp.einsum('bhqk,bkhe->bqhe', p, v)

    return _over_query_blocks(block, q)

def _diff_attend(q, k, v, lam):
    scale = DIFF_DH ** -0.5

    def block(qb):
        s = jnp.einsum('bqhcd,bkhcd->bhcqk', qb, k).astype(jnp.float32) * scale
        p = jax.nn.softmax(s, axis=-1)
        pd = (p[:, :, 0] - lam * p[:, :, 1]).astype(v.dtype)
        return jnp.einsum('bhqk,bkhe->bqhe', pd, v)

    return _over_query_blocks(block, q)

def _mla_query(proj, p):
    b, n = proj.shape[:2]
    q_a = _rmsnorm(proj[..., OFF_QA:OFF_KVA], p['mla_qa_norm'])
    q = (q_a @ p['w_q_b']).reshape(b, n, MLA_HEADS, MLA_QK)
    return _rmsnorm(q, p['mla_qn'])

def _mla_compress(proj, p):
    kv_a = proj[..., OFF_KVA:OFF_LRU_X]
    c_kv = _rmsnorm(kv_a[..., :KV_LORA], p['mla_kva_norm'])
    return c_kv, kv_a[..., KV_LORA:]

def _mla_expand(c_kv, k_rope, p):
    b, n = c_kv.shape[:2]
    kv = (c_kv @ p['w_kv_b']).reshape(b, n, MLA_HEADS, MLA_NOPE + MLA_V)
    k_pe = jnp.broadcast_to(k_rope[:, :, None, :], (b, n, MLA_HEADS, MLA_ROPE))
    k = _rmsnorm(jnp.concatenate([kv[..., :MLA_NOPE], k_pe], axis=-1), p['mla_kn'])
    return k, kv[..., MLA_NOPE:]

def _mla_out(o, p):
    b, n = o.shape[:2]
    return o.reshape(b, n, MLA_HEADS * MLA_V) @ p['w_o_mla']

def _centred_dwconv(x, w, bias):
    n = x.shape[1]
    xp = jnp.pad(x, ((0, 0), (CONV_LEFT, CONV_W - 1 - CONV_LEFT), (0, 0)))
    out = bias
    for j in range(CONV_W):
        out = out + xp[:, j:j + n] * w[j]
    return out

def _linear_scan(a, bx, h0, reverse):
    def step(h, inp):
        a_t, b_t = inp
        h = a_t * h + b_t
        return h, h

    h_last, hs = lax.scan(step, h0, (jnp.swapaxes(a, 0, 1), jnp.swapaxes(bx, 0, 1)), reverse=reverse)
    return jnp.swapaxes(hs, 0, 1), h_last

def _rglru(x, p, h0):
    b, n = x.shape[:2]
    xf = x.astype(jnp.float32)
    xb = xf.reshape(b, n, LRU_BLOCKS, LRU_BW)
    outs, finals = [], []
    for d in range(2):
        gates = jnp.einsum('bnkc,gkcd->gbnkd', xb, p['lru_gate_w'][d].astype(jnp.float32))
        gates = gates.reshape(2, b, n, D_RNN) + p['lru_gate_b'][d].astype(jnp.float32)[:, None, None, :]
        r = jax.nn.sigmoid(gates[0])
        i = jax.nn.sigmoid(gates[1])
        log_a = -LRU_C * r * jax.nn.softplus(-p['lru_lambda'][d].astype(jnp.float32))
        a = jnp.exp(log_a)
        bx = jnp.sqrt(-jnp.expm1(2.0 * log_a)) * (i * xf)
        h, h_last = _linear_scan(a, bx, h0[:, d].astype(jnp.float32), reverse=(d == 1))
        outs.append(h)
        finals.append(h_last)
    return (outs[0] + outs[1]).astype(x.dtype), jnp.stack(finals, axis=1).astype(x.dtype)

def _lru_out(y_r, proj, p):
    return (y_r * jax.nn.gelu(proj[..., OFF_LRU_G:OFF_DQ])) @ p['w_o_lru']

def _diff_qkv(proj, p):
    b, n = proj.shape[:2]
    q = _rmsnorm(proj[..., OFF_DQ:OFF_DK].reshape(b, n, DIFF_HEADS, 2, DIFF_DH), p['diff_qn'])
    k = _rmsnorm(proj[..., OFF_DK:OFF_DV].reshape(b, n, DIFF_HEADS, 2, DIFF_DH), p['diff_kn'])
    v = proj[..., OFF_DV:IN_COLS].reshape(b, n, DIFF_HEADS, DIFF_DV)
    return q, k, v

def _diff_lambda(p, lam_init):
    lam = p['diff_lambda'].astype(jnp.float32)
    return jnp.exp(jnp.sum(lam[0] * lam[1])) - jnp.exp(jnp.sum(lam[2] * lam[3])) + lam_init

def _diff_out(o, p, lam_init):
    b, n = o.shape[:2]
    o = _rmsnorm(o, p['diff_subln']) * (1.0 - lam_init)
    return o.reshape(b, n, DIFF_HEADS * DIFF_DV) @ p['w_o_diff']

def _merge(h, o_mla, o_lru, o_diff, p):
    b, n = h.shape[:2]
    g = jax.nn.sigmoid(h @ p['w_merge'] + p['b_merge']).reshape(b, n, N_BRANCH, D_MODEL)
    merged = g[:, :, 0] * o_mla + g[:, :, 1] * o_lru + g[:, :, 2] * o_diff
    return merged @ p['w_out']

def _context_mixers(h, p, lam_init):
    proj = h @ p['w_in']
    q = _mla_query(proj, p)
    c_kv, k_rope = _mla_compress(proj, p)
    k, v = _mla_expand(c_kv, k_rope, p)
    o_mla = _mla_out(_mla_attend(q, k, v), p)
    x_r = _centred_dwconv(proj[..., OFF_LRU_X:OFF_LRU_G], p['lru_conv_w'], p['lru_conv_b'])
    h0 = jnp.zeros((h.shape[0], 2, D_RNN), h.dtype)
    y_r, lru_state = _rglru(x_r, p, h0)
    o_lru = _lru_out(y_r, proj, p)
    qd, kd, vd = _diff_qkv(proj, p)
    o_diff = _diff_out(_diff_attend(qd, kd, vd, _diff_lambda(p, lam_init)), p, lam_init)
    return _merge(h, o_mla, o_lru, o_diff, p), (c_kv, k_rope, lru_state, kd, vd)

def _latent_mixers(h, p, lam_init, c_kv_ctx, k_rope_ctx, lru_ctx, kd_ctx, vd_ctx):
    n = h.shape[1]
    proj = h @ p['w_in']
    cos_m, sin_m = _axial_rope_tables(n, MLA_ROPE)
    cos_d, sin_d = _axial_rope_tables(n, DIFF_DH)
    q = _rope_tail(_mla_query(proj, p), cos_m, sin_m, MLA_NOPE)
    c_kv, k_rope = _mla_compress(proj, p)
    k_lat, v_lat = _mla_expand(c_kv, k_rope, p)
    k_lat = _rope_tail(k_lat, cos_m, sin_m, MLA_NOPE)
    k_ctx, v_ctx = _mla_expand(c_kv_ctx, k_rope_ctx, p)
    k = jnp.concatenate([k_ctx, k_lat], axis=1)
    v = jnp.concatenate([v_ctx, v_lat], axis=1)
    o_mla = _mla_out(_mla_attend(q, k, v), p)
    x_r = _centred_dwconv(proj[..., OFF_LRU_X:OFF_LRU_G], p['lru_conv_w'], p['lru_conv_b'])
    y_r, _ = _rglru(x_r, p, lru_ctx)
    o_lru = _lru_out(y_r, proj, p)
    qd, kd, vd = _diff_qkv(proj, p)
    qd = _apply_rope(qd, cos_d, sin_d)
    kd = jnp.concatenate([kd_ctx, _apply_rope(kd, cos_d, sin_d)], axis=1)
    vd = jnp.concatenate([vd_ctx, vd], axis=1)
    o_diff = _diff_out(_diff_attend(qd, kd, vd, _diff_lambda(p, lam_init)), p, lam_init)
    return _merge(h, o_mla, o_lru, o_diff, p)

def _moe(h, p):
    b, n, d = h.shape
    t = h.reshape(b * n, d)
    logits = (t @ p['router_w'] + p['router_b']).astype(jnp.float32)
    top_v, top_i = lax.top_k(logits, TOP_K)
    w_top = jax.nn.softmax(top_v, axis=-1)
    combine = jnp.einsum('tk,tke->te', w_top, jax.nn.one_hot(top_i, N_EXPERTS, dtype=jnp.float32)).astype(t.dtype)

    def expert(acc, e):
        w1, b1, w2, b2, ce = e
        gu = t @ w1 + b1
        gate = jnp.minimum(gu[:, :D_EXPERT], SWIGLU_LIMIT)
        up = jnp.clip(gu[:, D_EXPERT:], -SWIGLU_LIMIT, SWIGLU_LIMIT)
        act = (up + 1.0) * (gate * jax.nn.sigmoid(SWIGLU_ALPHA * gate))
        return acc + ce[:, None] * (act @ w2 + b2), None

    y, _ = lax.scan(expert, jnp.zeros_like(t), (p['exp_w1'], p['exp_b1'], p['exp_w2'], p['exp_b2'], combine.T))
    return y.reshape(b, n, d)

def setup_inputs(seed: int = 0) -> dict:
    key = jax.random.key(seed)
    ks = iter(jax.random.split(key, 48))
    L, D = DEPTH, D_MODEL

    def nrm(shape, scale=1.0):
        return jax.random.normal(next(ks), shape, jnp.float32) * scale

    def gain(shape):
        return 1.0 + nrm(shape, 0.02)

    a0 = jax.random.uniform(next(ks), (L, 2, D_RNN), jnp.float32, 0.9, 0.999)
    return {
        'x_prompt': nrm((BATCH, SEQ, D)),
        'x_sample': nrm((DEC_BATCH, DEC_SEQ, D)),
        'cache_mla_ckv': nrm((DEC_BATCH, L, PAST_LEN, KV_LORA)),
        'cache_mla_krope': nrm((DEC_BATCH, L, PAST_LEN, MLA_ROPE)),
        'state_lru': nrm((DEC_BATCH, L, 2, D_RNN), 0.5),
        'cache_diff_k': nrm((DEC_BATCH, L, PAST_LEN, DIFF_HEADS, 2, DIFF_DH)),
        'cache_diff_v': nrm((DEC_BATCH, L, PAST_LEN, DIFF_HEADS, DIFF_DV)),
        'c': nrm((DEC_BATCH, D)),
        'c_ctx': nrm((D,)),
        'ada_w': nrm((L, D, 6 * D), 0.5 * D ** -0.5),
        'ada_b': nrm((L, 6 * D), 0.01),
        'norm1_g': gain((L, D)),
        'norm2_g': gain((L, D)),
        'w_in': nrm((L, D, IN_COLS), D ** -0.5),
        'mla_qa_norm': gain((L, Q_LORA)),
        'w_q_b': nrm((L, Q_LORA, MLA_HEADS * MLA_QK), Q_LORA ** -0.5),
        'mla_kva_norm': gain((L, KV_LORA)),
        'w_kv_b': nrm((L, KV_LORA, MLA_HEADS * (MLA_NOPE + MLA_V)), KV_LORA ** -0.5),
        'mla_qn': gain((L, MLA_QK)),
        'mla_kn': gain((L, MLA_QK)),
        'w_o_mla': nrm((L, MLA_HEADS * MLA_V, D), (MLA_HEADS * MLA_V) ** -0.5),
        'lru_conv_w': nrm((L, CONV_W, D_RNN), CONV_W ** -0.5),
        'lru_conv_b': nrm((L, D_RNN), 0.01),
        'lru_gate_w': nrm((L, 2, 2, LRU_BLOCKS, LRU_BW, LRU_BW), LRU_BW ** -0.5),
        'lru_gate_b': nrm((L, 2, 2, D_RNN), 0.01),
        'lru_lambda': jnp.log(a0) - jnp.log1p(-a0),
        'w_o_lru': nrm((L, D_RNN, D), D_RNN ** -0.5),
        'diff_qn': gain((L, DIFF_DH)),
        'diff_kn': gain((L, DIFF_DH)),
        'diff_lambda': nrm((L, 4, DIFF_DH), 0.1),
        'diff_subln': gain((L, DIFF_DV)),
        'w_o_diff': nrm((L, DIFF_HEADS * DIFF_DV, D), (DIFF_HEADS * DIFF_DV) ** -0.5),
        'w_merge': nrm((L, D, N_BRANCH * D), D ** -0.5),
        'b_merge': nrm((L, N_BRANCH * D), 0.01),
        'w_out': nrm((L, D, D), D ** -0.5),
        'router_w': nrm((L, D, N_EXPERTS), D ** -0.5),
        'router_b': nrm((L, N_EXPERTS), 0.01),
        'exp_w1': nrm((L, N_EXPERTS, D, 2 * D_EXPERT), D ** -0.5),
        'exp_b1': nrm((L, N_EXPERTS, 2 * D_EXPERT), 0.01),
        'exp_w2': nrm((L, N_EXPERTS, D_EXPERT, D), D_EXPERT ** -0.5),
        'exp_b2': nrm((L, N_EXPERTS, D), 0.01),
    }

def reference(x_prompt, x_sample, cache_mla_ckv, cache_mla_krope, state_lru, cache_diff_k, cache_diff_v,
              c, c_ctx, ada_w, ada_b, norm1_g, norm2_g, w_in, mla_qa_norm, w_q_b, mla_kva_norm, w_kv_b,
              mla_qn, mla_kn, w_o_mla, lru_conv_w, lru_conv_b, lru_gate_w, lru_gate_b, lru_lambda, w_o_lru,
              diff_qn, diff_kn, diff_lambda, diff_subln, w_o_diff, w_merge, b_merge, w_out,
              router_w, router_b, exp_w1, exp_b1, exp_w2, exp_b2):
    layer_params = {
        'ada_w': ada_w, 'ada_b': ada_b, 'norm1': norm1_g, 'norm2': norm2_g, 'w_in': w_in,
        'mla_qa_norm': mla_qa_norm, 'w_q_b': w_q_b, 'mla_kva_norm': mla_kva_norm, 'w_kv_b': w_kv_b,
        'mla_qn': mla_qn, 'mla_kn': mla_kn, 'w_o_mla': w_o_mla,
        'lru_conv_w': lru_conv_w, 'lru_conv_b': lru_conv_b, 'lru_gate_w': lru_gate_w,
        'lru_gate_b': lru_gate_b, 'lru_lambda': lru_lambda, 'w_o_lru': w_o_lru,
        'diff_qn': diff_qn, 'diff_kn': diff_kn, 'diff_lambda': diff_lambda, 'diff_subln': diff_subln,
        'w_o_diff': w_o_diff, 'w_merge': w_merge, 'b_merge': b_merge, 'w_out': w_out,
        'router_w': router_w, 'router_b': router_b, 'exp_w1': exp_w1, 'exp_b1': exp_b1,
        'exp_w2': exp_w2, 'exp_b2': exp_b2,
    }
    xp, xs = x_prompt, x_sample
    new_ckv, new_krope, new_lru, new_dk, new_dv = [], [], [], [], []
    for l in range(DEPTH):
        p = {name: arr[l] for name, arr in layer_params.items()}
        lam_init = 0.8 - 0.6 * math.exp(-0.3 * l)
        sh1, sc1, g1, sh2, sc2, g2 = _modulation(c_ctx[None, :], p['ada_w'], p['ada_b'])
        mix, (ckv, krope, lst, dk, dv) = _context_mixers(_modulate(xp, p['norm1'], sh1, sc1), p, lam_init)
        xp = xp + g1 * mix
        xp = xp + g2 * _moe(_modulate(xp, p['norm2'], sh2, sc2), p)
        new_ckv.append(ckv)
        new_krope.append(krope)
        new_lru.append(lst)
        new_dk.append(dk)
        new_dv.append(dv)
        sh1, sc1, g1, sh2, sc2, g2 = _modulation(c, p['ada_w'], p['ada_b'])
        mix = _latent_mixers(_modulate(xs, p['norm1'], sh1, sc1), p, lam_init,
                             cache_mla_ckv[:, l], cache_mla_krope[:, l], state_lru[:, l],
                             cache_diff_k[:, l], cache_diff_v[:, l])
        xs = xs + g1 * mix
        xs = xs + g2 * _moe(_modulate(xs, p['norm2'], sh2, sc2), p)
    return (xp, xs, jnp.stack(new_ckv, axis=1), jnp.stack(new_krope, axis=1), jnp.stack(new_lru, axis=1),
            jnp.stack(new_dk, axis=1), jnp.stack(new_dv, axis=1))


_drawn_inputs = setup_inputs


def setup_inputs(seed=0):
    import zlib

    import numpy as np

    out = dict(_drawn_inputs(seed))
    spreads = {}
    factors = {'cache_mla_krope': 3.914,
     'norm1_g': 2.865,
     'mla_qa_norm': 7.223,
     'mla_kva_norm': 2.975,
     'mla_qn': 7.755,
     'mla_kn': 6.346,
     'lru_gate_b': 7.117,
     'diff_qn': 6.788,
     'diff_kn': 2.774,
     'diff_lambda': 3.327,
     'diff_subln': 5.064,
     'b_merge': 7.95,
     'router_b': 3.309,
     'exp_b1': 6.856,
     'exp_b2': 18.93,
     'cache_diff_k': 8.0,
     'cache_diff_v': 8.0}
    for name, (base, spread) in spreads.items():
        noise = np.random.default_rng([zlib.crc32(name.encode()), seed]).standard_normal(out[name].shape)
        drawn = base * np.exp(spread * noise) if base else spread * noise
        out[name] = __import__('jax').numpy.asarray(drawn.astype(out[name].dtype))
    for name, factor in factors.items():
        out[name] = (out[name] * factor).astype(out[name].dtype)
    return out
```

```python
from contextlib import ExitStack

import concourse.bass as bass
from concourse import mybir

F32 = mybir.dt.float32
I32 = mybir.dt.int32
ALU = mybir.AluOpType
ACT = mybir.ActivationFunctionType
AX_X = mybir.AxisListType.X

P = 128
D = 1024
KC = D // P
G = 2
NT = G * P
L = 2
EPS = 1e-6

MLA_H, NOPE, ROPE, VD = 8, 64, 32, 64
QK = NOPE + ROPE
Q_LORA, KV_LORA = 384, 256
D_RNN = 512
RC = D_RNN // P
DIFF_H, DH, DV = 4, 64, 128
N_EXP, D_EXP, TOP_K = 32, 512, 4
SLOTS = 64
LIMIT, ALPHA = 7.0, 1.702
MAX_EXTRA = 16

OFF_KVA = Q_LORA
OFF_LRU = OFF_KVA + KV_LORA + ROPE
OFF_DQ = OFF_LRU + 2 * D_RNN
IN_COLS = OFF_DQ + 3 * 512
M_COLS = OFF_LRU

V_ADAB, V_N1, V_N2, V_BM, V_QA, V_SUB = 0, 48, 56, 64, 88, 91
V_CW, V_CB, V_GB, V_LAM, V_ST, V_LI, V_OML = 92, 108, 112, 128, 136, 144, 145
NV = 146
R_KVA, R_QN, R_KN, R_DQN, R_DKN, R_DL, R_RB = 0, 256, 352, 448, 512, 576, 832
NR = 864
C_ID, C_UT, C_ONE, C_IOTA = 0, 128, 256, 384
C_CM, C_SM, C_CD, C_SD = 512, 544, 576, 640
C_PIDX, C_KK, C_EIDX, C_EPS = 704, 705, 721, 753
NC = 754

RING = 6
SLOT = 4096
S_ADA, S_IN, S_QB, S_KVB = 0, 12, 19, 20
S_WM = {1: 21, 0: 24, 2: 27}
S_WO = {1: 23, 0: 26, 2: 29}
S_OUT = 30
PRE = 32
BRANCHES = (1, 0, 2)


def before_moe(s):
    return len(range(s, PRE, RING))


def build(nc, x_in, cond_in, consts, vecs, rows, ada_w, w_in, w_q_b, w_kv_b, lru_gate_w, w_o_mla, w_o_lru,
          w_o_diff, w_merge, w_out, router_w, exp_w1, exp_b1, exp_w2, exp_b2, cache_ckv, cache_krope,
          cache_dk, cache_dv, y_out, new_ckv, new_krope, new_lru, new_dk, new_dv):
    ctx = ExitStack()
    with ctx:
        def sb(name, shape, dt=F32):
            return ctx.enter_context(nc.sbuf_tensor(name, shape, dt))

        sems = []

        def sem(name):
            s = ctx.enter_context(nc.semaphore(name))
            sems.append(s)
            return s

        cst = sb("cst", [P, NC])
        vec = sb("vec", [P, NV])
        row = sb("row", [P, NR])
        cT = sb("cT", [P, KC, 32])
        modT = sb("modT", [P, 48, G])
        A1 = sb("A1", [P, KC, G])
        A2 = sb("A2", [P, KC, G])
        g1h = sb("g1h", [P, KC, G])
        gbh = sb("gbh", [P, 16])
        bmh = sb("bmh", [P, 24])
        sp = sb("sp", [P, 32])
        clh = sb("clh", [P, 8])
        lam = sb("lam", [P, 8])
        lprod = sb("lprod", [P, 128])
        subg = sb("subg", [P, 1])
        ss = sb("ss", [P, 32])
        nwt = sb("nwt", [P, 2, 32])
        krs = sb("krs", [P, 4])
        nm = sb("nm", [P, 2, 4])
        sums = sb("sums", [P, 2, 4])
        rcp = sb("rcp", [P, 2, 4])
        nl = sb("nl", [P, 2])
        rs = sb("rs", [P, NT])
        fin = sb("fin", [P, 8])
        xT = sb("xT", [P, KC, NT])
        hT = sb("hT", [P, KC, NT])
        rw = sb("rw", [P, KC, N_EXP])
        ring = sb("ring", [P, RING, SLOT])
        arena = sb("arena", [P, 21344])
        meta = sb("meta", [P, 2], I32)
        eidi = sb("eidi", [P, MAX_EXTRA], I32)
        ps = ctx.enter_context(nc.psum_tensor("ps", [P, 8, 512], F32))

        def at(off, *dims):
            n = 1
            for d in dims:
                n *= d
            v = arena[:, off:off + n]
            if len(dims) == 2:
                return v.rearrange("p (a b) -> p a b", a=dims[0])
            if len(dims) == 3:
                return v.rearrange("p (a b c) -> p a b c", a=dims[0], b=dims[1])
            if len(dims) == 4:
                return v.rearrange("p (a b c d) -> p a b c d", a=dims[0], b=dims[1], c=dims[2])
            return v

        merged = at(0, KC, NT)
        qaT = at(0, 3, NT)
        ckvT = at(768, 2, 384)
        lru_u = at(1536, 2, NT)
        tg = at(2048, KC, NT)
        lruw = at(2048, 16, P)
        projm = at(4096, G, M_COLS)
        projd = at(5440, 3, G, 512)
        E0 = 8512
        xpad = at(E0, RC, G, P + 3)
        lru_a = at(E0, RC, NT)
        lru_t = at(E0 + 1024, RC, NT)
        lru_h = [at(E0 + 2048, RC, NT), at(E0 + 3072, RC, NT)]
        xr = at(E0 + 4096, RC, NT)
        gel = at(E0 + 5120, RC, NT)
        scratch = at(E0 + 1024, 2048)
        qkT = [at(E0, 640), at(E0 + 640, 640)]
        probs = [at(E0 + 1280, 2, 384), at(E0 + 2048, 2, 384)]
        probsT = [at(E0 + 2816, 384), at(E0 + 3200, 384)]
        on = at(E0 + 3584, G, DV)
        mtmp = at(E0 + 3840, NT)
        omla = at(E0 + 4096, 4, NT)
        odif = at(E0 + 5120, 4, NT)
        Q0 = E0 + 6144
        q_tok = at(Q0, G, MLA_H, QK)
        onsq = at(Q0, G, DV)
        msb = at(Q0, 3, 512)
        v_tok = at(Q0 + 1536, 3, 512)
        k_tok = at(Q0 + 3072, 3, MLA_H, QK)
        sq = at(Q0 + 3072, KC, NT)
        assert Q0 + 3072 + 2304 == 20032
        c_ckv = at(20032, KV_LORA)
        c_kr = at(20288, ROPE)
        c_dk = at(20320, 512)
        c_dv = at(20832, 512)
        b1 = at(5440, D)
        b2 = at(6464, D)
        X2 = at(E0, G, D)
        Xg = [at(E0 + 2048, 512), at(E0 + 2560, 512)]
        xTg = [at(E0 + 3072, 4, P), at(E0 + 3584, 4, P)]
        gate_s, up_s, sig_s, act_s = (at(E0 + 4096 + 256 * i, 256) for i in range(4))
        actT = [at(E0 + 5120, 2, P), at(E0 + 5376, 2, P)]
        O_s = [at(E0 + 5632, 512), at(E0 + 6144, 512)]
        SCT = [at(E0 + 6656, NT), at(E0 + 6912, NT)]
        S_s = [at(E0 + 7168, G, SLOTS), at(E0 + 7296, G, SLOTS)]
        SC_s = [at(E0 + 7424, G, P), at(E0 + 7680, G, P)]
        oh = [at(E0 + 7936, SLOTS), at(E0 + 8000, SLOTS)]
        T0 = E0 + 8064
        lgt, rep, msk, exl, cmb = (at(T0 + 64 * i, G, N_EXP) for i in range(5))
        pm1 = at(T0 + 320, G, N_EXP)
        top8 = at(T0 + 384, G, 8)
        nv1 = at(T0 + 400, G)
        den = at(T0 + 402, G)
        cnt = at(T0 + 404, N_EXP)
        xtra = at(T0 + 436, N_EXP)
        tend = at(T0 + 468, N_EXP)
        tbeg = at(T0 + 500, N_EXP)
        npf = at(T0 + 532, 2)
        cmp8 = at(T0 + 534, 8)
        psub = at(T0 + 542, MAX_EXTRA)
        NTAB = N_EXP + MAX_EXTRA + 2
        pmT = at(T0 + 558, G, NTAB)
        cwT = at(T0 + 658, G, NTAB)
        eidf = at(T0 + 758, NTAB)
        ctT = at(T0 + 808, NT)
        K0 = Q0 + 3072
        sel, tmpx, tmpy = (at(K0 + 512 * i, MAX_EXTRA, N_EXP) for i in range(3))
        assert T0 + 808 + NT <= K0

        ident = cst[:, C_ID:C_ID + P]
        ustrict = cst[:, C_UT:C_UT + P]
        ones = cst[:, C_ONE:C_ONE + P]
        one_col = cst[:, C_ONE:C_ONE + 1]

        arr = [sem(f"slot{s}_arrived") for s in range(RING)]
        ld_vec, ld_row, ld_lruw = sem("vec_in"), sem("row_in"), sem("lruw_in")
        ld_ckv, ld_kr, ld_dk, ld_dv = sem("cckv_in"), sem("ckr_in"), sem("cdk_in"), sem("cdv_in")
        ld_rw, ld_b1, ld_b2 = sem("rw_in"), sem("b1_in"), sem("b2_in")
        out_done = sem("out_done")
        lruw_zero = sem("lruw_zero")
        v_step, a_step = sem("dve_step"), sem("act_step")
        sq_rdy, nrm_mm, nrm_sq, hraw, h_v, h_a = (
            [sem(f"{n}{i}") for i in range(2)] for n in ("sq_rdy", "nrm_mm", "nrm_sqrt", "hraw", "h_dve", "h_act"))
        ada_mm, ada_sb, ada_tr, prep, mod_rdy = (sem(n) for n in
                                                 ("ada_mm", "ada_sb", "ada_tr", "prep", "mod_rdy"))
        sp_abs, sp_ln, lam_exp = sem("sp_abs"), sem("sp_ln"), sem("lam_exp")
        win_mm, win_v, win_a = sem("win_mm"), sem("win_evac_v"), sem("win_evac_a")
        mla_n, conv_rdy = sem("mla_norm"), sem("conv_rdy")
        p3_mm, p3_ev, p4_mm, p4_ev = sem("lat_tr"), sem("lat_evac"), sem("exp_mm"), sem("exp_evac")
        lg_mm, lg_ev, lru_at, lru_w, lru_sq, lru_fr, lru_rdy = (
            sem(n) for n in ("lru_mm", "lru_evac", "lru_at", "lru_w", "lru_sqrt", "lru_free", "lru_rdy"))
        qn_rdy, kn_rdy, dn_rdy = sem("qn_rdy"), sem("kn_rdy"), sem("dn_rdy")
        f_mm, f_ac, f_dv = sem("merge_mm"), sem("merge_act"), sem("merge_dve")
        t_mm, qk_v, qk_a, s_mm, nm_v, ex_a = (sem(n) for n in ("qk_tr", "qk_evac_v", "qk_evac_a", "score_mm",
                                                              "negmax", "exp_done"))
        pn_v, pt_mm, ptc, pv_mm, om_ev, on_v, ot_mm, od_ev = (
            sem(n) for n in ("probs_rdy", "pt_tr", "pt_evac", "pv_mm", "omla_rdy", "on_rdy", "on_tr", "odif_rdy"))
        rt_mm, x2_mm, x2_ev, nv_v, exl_a, msk_v, pos_mm, cmb_v, ct_mm, ct_ev, y0_mm, routed = (
            sem(n) for n in ("router_mm", "x2_tr", "x2_evac", "negtop", "exl_rdy", "mask_rdy", "pos_mm", "cmb_rdy",
                             "ct_mm", "ct_evac", "y_init", "routed"))
        disp, ga_mm, xg_ev, xt_mm, xt_ev = (sem(n) for n in ("disp_rdy", "gather_mm", "xg_evac", "xt_tr",
                                                             "xt_evac"))
        g1_mm, gate_v, up_v, sig_a, act_v, at_mm, at_ev = (
            sem(n) for n in ("w1_mm", "gate_rdy", "up_rdy", "sig_rdy", "act_rdy", "act_tr", "act_evac"))
        g2_mm, o_ev, sct_mm, sct_ev, sc_mm = (sem(n) for n in ("w2_mm", "o_evac", "sct_tr", "sct_evac",
                                                               "scatter_mm"))
        step_m = sem("dve_moe_step")
        s_set = [ctx.enter_context(nc.semaphore(f"setup{i}")) for i in range(6)]

        def consumed(pos):
            if pos < S_IN:
                return ada_mm, pos // 4 + 1
            if pos < S_QB:
                return win_mm, 2 * (pos - S_IN + 1)
            if pos == S_QB:
                return p4_mm, 4
            if pos == S_KVB:
                return p4_mm, 10
            n = 0
            for b in BRANCHES:
                for p_, k in ((S_WM[b], 4), (S_WM[b] + 1, 4), (S_WO[b], 8)):
                    n += k
                    if pos == p_:
                        return f_mm, n
            return f_mm, n + 4 * (pos - S_OUT + 1)

        def arrived(eng, pos):
            eng.wait_ge(arr[pos % RING], 16 * (pos // RING + 1))
            return ring[:, pos % RING, :]

        MERGE = [("gate", b) if k == 0 else ("proj", b) for b in BRANCHES for k in range(2)] + [("out", 0)]

        def merge_evac(eng, f):
            g, ch = divmod(f - 2, 8)
            if MERGE[g][0] == "gate":
                eng.wait_ge(f_ac, 8 * (g // 2) + ch + 1)
            else:
                eng.wait_ge(f_dv, 8 * (g // 2) + ch + 1)

        def merge_ps(f):
            return ps[:, 6 + f % 2, 0:NT]

        with nc.Block() as block:
            @block.sync
            def _(sp_):
                sp_.dma_start(cT[:, :, 0:G], cond_in).then_inc(s_set[0], 16)
                sp_.dma_start(cst[:, :], consts).then_inc(s_set[1], 16)
                sp_.dma_start(xT[:, :, :], x_in).then_inc(s_set[2], 16)
                sp_.wait_ge(s_set[1], 16)
                sp_.wait_ge(s_set[2], 16)

            @block.scalar
            def _(act):
                act.wait_ge(s_set[0], 16)
                nc.scalar.activation(cT[:, :, G:2 * G], cT[:, :, 0:G], ACT.Tanh, scale=0.5).then_inc(s_set[3], 1)

            @block.vector
            def _(dve):
                dve.wait_ge(s_set[3], 1)
                nc.vector.tensor_scalar(cT[:, :, G:2 * G], cT[:, :, G:2 * G], 0.5, 0.5, ALU.mult,
                                        ALU.add).then_inc(s_set[4], 1)
                dve.wait_ge(s_set[4], 1)
                nc.vector.tensor_tensor(cT[:, :, 0:G], cT[:, :, 0:G], cT[:, :, G:2 * G],
                                        ALU.mult).then_inc(s_set[4], 1)
                dve.wait_ge(s_set[4], 2)
                nc.vector.memset(cT[:, :, G:32], 0.0).then_inc(s_set[4], 1)

        with nc.Fori(0, L) as l:
            with nc.Block() as block:
                @block.sync
                def _(sp_):
                    def load(pos, src, n, after=None):
                        dst = ring[:, pos % RING, 0:n]
                        if pos >= RING:
                            s, v = consumed(pos - RING)
                            sp_.wait_ge(s, v)
                        shape = src.shape
                        sp_.dma_start(dst.rearrange("p (a b) -> p a b", b=shape[2]), src).then_inc(
                            arr[pos % RING], 16)

                    def rows_of(w, r0, nk, c0, nc_):
                        v = w[bass.ds(l, 1), r0:r0 + nk * P, c0:c0 + nc_]
                        return v.rearrange("o (k p) n -> p (o k) n", p=P)

                    for n in range(12):
                        load(S_ADA + n, rows_of(ada_w, 0, KC, n * 512, 512), SLOT)
                    bounds = [(0, 512), (512, 160), (OFF_LRU, 512), (OFF_LRU + 512, 512),
                              (OFF_DQ, 512), (OFF_DQ + 512, 512), (OFF_DQ + 1024, 512)]
                    for n, (c0, w) in enumerate(bounds):
                        load(S_IN + n, rows_of(w_in, 0, KC, c0, w), KC * w)
                    load(S_QB, rows_of(w_q_b, 0, 3, 0, 768), 3 * 768)
                    load(S_KVB, rows_of(w_kv_b, 0, 2, 0, 1024), 2048)
                    wo = {0: w_o_mla, 1: w_o_lru, 2: w_o_diff}
                    for b in BRANCHES:
                        for i in range(2):
                            load(S_WM[b] + i, rows_of(w_merge, 0, KC, b * D + i * 512, 512), SLOT)
                        load(S_WO[b], rows_of(wo[b], 0, 4, 0, D), SLOT)
                    for i in range(2):
                        load(S_OUT + i, rows_of(w_out, 0, KC, i * 512, 512), SLOT)

                    def expert(e, i, waits):
                        srcs = [exp_w1[bass.ds(l * N_EXP + e, 1), 0:512, :],
                                exp_w1[bass.ds(l * N_EXP + e, 1), 512:1024, :],
                                exp_w2[bass.ds(l * N_EXP + e, 1), :, :]]
                        for j, src in enumerate(srcs):
                            s, v = waits[j]
                            sp_.wait_ge(s, v)
                            sp_.dma_start(ring[:, 3 * i + j, :].rearrange("p (k n) -> p k n", n=D),
                                          src.rearrange("o (k p) n -> p (o k) n", p=P)).then_inc(
                                              arr[3 * i + j], 16)

                    def freed(tile):
                        return [(g1_mm, tile * 2 + 1), (g1_mm, tile * 2 + 2), (g2_mm, tile + 1)]

                    last_pos = [s + RING * (before_moe(s) - 1) for s in range(RING)]
                    for i in range(2):
                        expert(i, i, [consumed(last_pos[3 * i + j]) for j in range(3)])
                    with sp_.Fori(1, N_EXP // 2) as q:
                        for i in range(2):
                            expert(q * 2 + i, i, freed(q * 2 - 2 + i))
                    sp_.wait_ge(routed, 1)
                    n_extra = sp_.value_load(meta[0:1, 0:1], min_val=0, max_val=MAX_EXTRA // 2)
                    with sp_.If(n_extra > 0):
                        with sp_.Fori(0, n_extra) as q:
                            for i in range(2):
                                e = sp_.value_load(eidi[0:1, bass.ds(q * 2 + i, 1)], min_val=0,
                                                   max_val=N_EXP - 1)
                                expert(e, i, freed(q * 2 + (N_EXP - 2) + i))
                    with sp_.Else():
                        sp_.nop()
                    sp_.nop()

                @block.gpsimd
                def _(pool):
                    nc.gpsimd.memset(lruw[:, :, :], 0.0).then_inc(lruw_zero, 1)

                @block.tensor
                def _(pe):
                    mm = nc.tensor.matmul
                    tr = nc.tensor.transpose

                    def norm(i, bank):
                        pe.wait_ge(sq_rdy[i], 1)
                        for k in range(KC):
                            last = mm(ps[:, bank, 0:NT], ones, sq[:, k, :], start=k == 0, stop=k == KC - 1)
                        last.then_inc(nrm_mm[i], 1)

                    norm(0, 7)
                    for r in range(3):
                        slots = [arrived(pe, S_ADA + 4 * r + j) for j in range(4)]
                        for k in range(KC):
                            for j in range(4):
                                last = mm(ps[32 * j:32 * j + 32, r, :], cT[:, k, :],
                                          slots[j][:, k * 512:(k + 1) * 512], start=k == 0, stop=k == KC - 1)
                        last.then_inc(ada_mm, 1)
                    for r in range(3):
                        pe.wait_ge(ada_sb, r + 1)
                        for b in range(4):
                            last = tr(ps[:, 3 + r, b * P:(b + 1) * P], msb[:, r, b * P:(b + 1) * P], ident)
                        last.then_inc(ada_tr, 1)

                    def win_bank(u):
                        if 6 <= u < 12:
                            pe.wait_ge(win_v, u - 5)
                        elif u >= 12:
                            pe.wait_ge(win_a, u - 11)
                        return u % 6

                    u = 0
                    for n, (kind, w) in enumerate((("tok", 512), ("tok", 160), ("feat", 512), ("feat", 512),
                                                   ("tok", 512), ("tok", 512), ("tok", 512))):
                        slot = arrived(pe, S_IN + n).rearrange("p (k n) -> p k n", n=512) if w == 512 else \
                            arrived(pe, S_IN + n)[:, 0:KC * w].rearrange("p (k n) -> p k n", n=w)
                        for half in range(2):
                            bank = win_bank(u)
                            if kind == "tok":
                                for k in range(KC):
                                    if u == 0:
                                        pe.wait_ge(h_v[0], k + 1)
                                    if u == 1:
                                        pe.wait_ge(h_a[0], k + 1)
                                    last = mm(ps[:, bank, 0:w], hT[:, k, half * P:(half + 1) * P],
                                              slot[:, k, :], start=k == 0, stop=k == KC - 1)
                            else:
                                for c in range(2):
                                    for k in range(KC):
                                        ch = 2 * half + c
                                        last = mm(ps[:, bank, c * NT:(c + 1) * NT],
                                                  slot[:, k, ch * P:(ch + 1) * P], hT[:, k, :],
                                                  start=k == 0, stop=k == KC - 1)
                            last.then_inc(win_mm, 1)
                            u += 1

                    pe.wait_ge(win_a, 4)
                    pe.wait_ge(win_a, 8)
                    pe.wait_ge(mla_n, 1)
                    for b in range(3):
                        for g in range(G):
                            last = tr(ps[:, b // 2, (b % 2) * NT + g * P:(b % 2) * NT + (g + 1) * P],
                                      projm[:, g, b * P:(b + 1) * P], ident)
                        last.then_inc(p3_mm, 1)
                    pe.wait_ge(ld_ckv, 16)
                    for b in range(2):
                        for s in range(3):
                            src = c_ckv[:, b * P:(b + 1) * P] if s == 1 else \
                                projm[:, s // 2, OFF_KVA + b * P:OFF_KVA + (b + 1) * P]
                            last = tr(ps[:, 6 + b, s * P:(s + 1) * P], src, ident)
                        last.then_inc(p3_mm, 1)

                    pe.wait_ge(conv_rdy, 1)
                    pe.wait_ge(ld_lruw, 32)
                    for i in range(16):
                        if i >= 8 and i % 2 == 0:
                            pe.wait_ge(lg_ev, i - 6)
                        mm(ps[:, 2 + (i % 8) // 2, (i % 2) * NT:(i % 2 + 1) * NT], lruw[:, i, :],
                           xr[:, i % 4, :], start=True, stop=True).then_inc(lg_mm, 1)

                    for v in range(10):
                        if v == 0:
                            pe.wait_ge(p3_ev, 5)
                            slot = arrived(pe, S_QB)[:, 0:3 * 768].rearrange("p (k n) -> p k n", n=768)
                        if v == 4:
                            slot = arrived(pe, S_KVB)[:, 0:2048].rearrange("p (k n) -> p k n", n=1024)
                        if v >= 2:
                            pe.wait_ge(p4_ev, v - 1)
                        half = v % 2
                        if v < 4:
                            for k in range(3):
                                last = mm(ps[:, half, 0:384], qaT[:, k, (v // 2) * P:(v // 2 + 1) * P],
                                          slot[:, k, half * 384:(half + 1) * 384], start=k == 0, stop=k == 2)
                        else:
                            s = v // 2 - 2
                            for k in range(2):
                                last = mm(ps[:, half, :], ckvT[:, k, s * P:(s + 1) * P],
                                          slot[:, k, half * 512:(half + 1) * 512], start=k == 0, stop=k == 1)
                        last.then_inc(p4_mm, 1)

                    done = [0]

                    def merge(n):
                        for _ in range(n):
                            f = done[0]
                            done[0] += 1
                            grp, ch = divmod(f, 8)
                            kind, b = MERGE[grp]
                            if f >= 2:
                                merge_evac(pe, f)
                            out = merge_ps(f)
                            if kind == "proj":
                                slot = arrived(pe, S_WO[b]).rearrange("p (k n) -> p k n", n=D)
                                cols = slice(ch * P, (ch + 1) * P)
                                if ch == 0:
                                    if b == 1:
                                        pe.wait_ge(lru_rdy, 1)
                                    elif b == 0:
                                        pe.wait_ge(om_ev, 4)
                                    else:
                                        pe.wait_ge(od_ev, 4)
                                src, nk = {1: gel, 0: omla, 2: odif}[b], 4
                            else:
                                pos = (S_OUT if kind == "out" else S_WM[b]) + ch // 4
                                slot = arrived(pe, pos).rearrange("p (k n) -> p k n", n=512)
                                cols = slice((ch % 4) * P, (ch % 4 + 1) * P)
                                src, nk = (merged if kind == "out" else hT), KC
                                if kind == "out" and ch == 0:
                                    pe.wait_ge(f_dv, 24)
                            for k in range(nk):
                                last = mm(out, slot[:, k, cols], src[:, k, :], start=k == 0, stop=k == nk - 1)
                            last.then_inc(f_mm, 1)

                    merge(16)

                    def qk_transposes(u):
                        if u == 0:
                            pe.wait_ge(qn_rdy, 2)
                            pe.wait_ge(kn_rdy, 3)
                        if u == 8:
                            pe.wait_ge(dn_rdy, 4)
                            pe.wait_ge(ld_dk, 16)
                        if u < 8:
                            rows_, srcs = QK, [q_tok[:, 0, u, :], q_tok[:, 1, u, :]] + \
                                [k_tok[:, s, u, :] for s in range(3)]
                        else:
                            c = slice((u - 8) * P, (u - 7) * P)
                            rows_, srcs = P, [projd[:, 0, 0, c], projd[:, 0, 1, c], projd[:, 1, 0, c],
                                              c_dk[:, c], projd[:, 1, 1, c]]
                        for n in range(3):
                            last = tr(ps[0:rows_, 0, n * P:(n + 1) * P], srcs[n], ident)
                        last.then_inc(t_mm, 1)
                        for n in range(2):
                            last = tr(ps[0:rows_, 1, n * P:(n + 1) * P], srcs[3 + n], ident)
                        last.then_inc(t_mm, 1)

                    qk_transposes(0)
                    for u in range(12):
                        b = qkT[u % 2]
                        pe.wait_ge(qk_v, u + 1)
                        pe.wait_ge(qk_a, u + 1)
                        if u == 0:
                            pe.wait_ge(lg_ev, 16)
                        if u >= 2:
                            pe.wait_ge(ex_a, u if u >= 8 else u - 1)
                        if u < 8:
                            bank = 2 + u % 2
                            mm(ps[:, bank, 0:128], b[0:QK, 0:128], b[0:QK, 256:384], start=True, stop=True)
                            mm(ps[:, bank, 128:384], b[0:QK, 128:256], b[0:QK, 384:640], start=True,
                               stop=True).then_inc(s_mm, 1)
                        else:
                            for c in range(2):
                                r = slice(64 * c, 64 * c + 64)
                                mm(ps[:, 2 + c, 0:128], b[r, 0:128], b[r, 256:384], start=True, stop=True)
                            for c in range(2):
                                r = slice(64 * c, 64 * c + 64)
                                last = mm(ps[:, 2 + c, 128:384], b[r, 128:256], b[r, 384:640], start=True,
                                          stop=True)
                            last.then_inc(s_mm, 1)
                        if u < 11:
                            qk_transposes(u + 1)
                        merge(1)
                        if u == 7:
                            pass
                        pe.wait_ge(pn_v, u + 1)
                        if u >= 1:
                            pe.wait_ge(ptc, u)
                        for n in range(3):
                            last = tr(ps[:, 4, n * P:(n + 1) * P], probs[u % 2][:, 0, n * P:(n + 1) * P], ident)
                        last.then_inc(pt_mm, 1)
                        if u >= 8:
                            merge(1)
                        pe.wait_ge(ptc, u + 1)
                        t = probsT[u % 2]
                        if u < 8:
                            if u % 2 == 0 and u:
                                pe.wait_ge(om_ev, u // 2)
                            r = slice(64 * (u % 2), 64 * (u % 2) + 64)
                            c = slice(u * VD, (u + 1) * VD)
                            mm(ps[r, 5, 0:P], v_tok[:, 0, c], t[:, 0:P], start=True, stop=True)
                            mm(ps[r, 5, P:NT], v_tok[:, 1, c], t[:, P:2 * P], start=True, stop=False)
                            mm(ps[r, 5, P:NT], v_tok[:, 2, c], t[:, 2 * P:3 * P], start=False,
                               stop=True).then_inc(pv_mm, 1)
                        else:
                            if u == 8:
                                pe.wait_ge(om_ev, 4)
                                pe.wait_ge(ld_dv, 16)
                            else:
                                pe.wait_ge(od_ev, u - 8)
                            c = slice((u - 8) * P, (u - 7) * P)
                            mm(ps[:, 5, 0:P], t[:, 0:P], projd[:, 2, 0, c], start=True, stop=True)
                            mm(ps[:, 5, P:NT], t[:, P:2 * P], c_dv[:, c], start=True, stop=False)
                            mm(ps[:, 5, P:NT], t[:, 2 * P:3 * P], projd[:, 2, 1, c], start=False,
                               stop=True).then_inc(pv_mm, 1)
                            pe.wait_ge(on_v, u - 7)
                            for g in range(G):
                                last = tr(ps[:, 5, NT + g * P:NT + (g + 1) * P], on[:, g, :], ident)
                            last.then_inc(ot_mm, 1)
                        if u == 7:
                            merge(8)
                    merge(16)

                    norm(1, 0)
                    pe.wait_ge(h_v[1], 8)
                    pe.wait_ge(h_a[1], 8)
                    pe.wait_ge(ld_rw, 16)
                    for g in range(G):
                        for k in range(KC):
                            last = mm(ps[:, 1, g * N_EXP:(g + 1) * N_EXP], hT[:, k, g * P:(g + 1) * P],
                                      rw[:, k, :], start=k == 0, stop=k == KC - 1)
                    last.then_inc(rt_mm, 1)
                    for n in range(4):
                        for j in range(4):
                            k = (n % 2) * 4 + j
                            last = tr(ps[:, 2 + n, j * P:(j + 1) * P], hT[:, k, (n // 2) * P:(n // 2 + 1) * P],
                                      ident)
                        last.then_inc(x2_mm, 1)
                    pe.wait_ge(msk_v, 1)
                    mm(ps[:, 1, 64:96], ustrict, msk[:, 0, :], start=True, stop=True)
                    mm(ps[:, 1, 96:128], ones, msk[:, 0, :], start=True, stop=False)
                    mm(ps[:, 1, 96:128], ustrict, msk[:, 1, :], start=False, stop=True)
                    mm(ps[:, 1, 128:160], ones, msk[:, 0, :], start=True, stop=False)
                    mm(ps[:, 1, 128:160], ones, msk[:, 1, :], start=False, stop=True).then_inc(pos_mm, 1)
                    pe.wait_ge(cmb_v, 1)
                    for g in range(G):
                        last = mm(ps[0:N_EXP, 0, g * P:(g + 1) * P], cmb[:, g, :], ident, start=True, stop=True)
                    last.then_inc(ct_mm, 1)
                    pe.wait_ge(ct_ev, 1)
                    pe.wait_ge(ld_b2, 16)
                    pe.wait_ge(x2_ev, 4)
                    for k in range(KC):
                        mm(ps[:, 4 + k // 2, (k % 2) * NT:(k % 2 + 1) * NT], b2[0:N_EXP, k * P:(k + 1) * P],
                           ctT[0:N_EXP, :], start=k % 2 == 0, stop=True, skip_group_check=True)

                    def gather(p):
                        for g in range(G):
                            for h in range(2):
                                last = mm(ps[64 * h:64 * h + 64, 0, :], S_s[p][:, g, :],
                                          X2[:, g, h * 512:(h + 1) * 512], start=g == 0, stop=g == 1)
                        last.then_inc(ga_mm, 1)

                    def token_transposes(p):
                        for b in range(4):
                            last = tr(ps[:, 1, b * P:(b + 1) * P], Xg[p][:, b * P:(b + 1) * P], ident)
                        last.then_inc(xt_mm, 1)

                    def combine_transposes(p):
                        for g in range(G):
                            last = tr(ps[:, 3, NT + g * P:NT + (g + 1) * P], SC_s[p][:, g, :], ident)
                        last.then_inc(sct_mm, 1)

                    pe.wait_ge(disp, 1)
                    gather(0)
                    pe.wait_ge(xg_ev, 1)
                    token_transposes(0)
                    combine_transposes(0)
                    pe.wait_ge(ld_b1, 16)
                    pe.wait_ge(routed, 1)
                    pairs = pe.value_load(meta[0:1, 1:2], min_val=N_EXP // 2, max_val=(N_EXP + MAX_EXTRA) // 2)
                    with pe.Fori(0, pairs) as q:
                        for i in range(2):
                            t1 = q * 2 + (i + 1)
                            pe.wait_ge(xt_ev, t1)
                            pe.wait_ge(up_v, t1)
                            for h in range(2):
                                rhs = b1[0:N_EXP, :].rearrange("e (c n) -> e c n", c=2)[:, :, h * 256:(h + 1) * 256]
                                mm(ps[64 * h:64 * h + 64, 2, :], oh[i][0:N_EXP, :], rhs, start=True, stop=False)
                            for part in range(2):
                                s = 3 * i + part
                                pe.wait_ge(arr[s], q * 16 + 16 * (before_moe(s) + 1))
                                w = ring[:, s, :].rearrange("p (k c n) -> p k c n", k=4, c=2)
                                for k in range(4):
                                    for h in range(2):
                                        last = mm(ps[64 * h:64 * h + 64, 2, :],
                                                  xTg[i][:, k, part * 64:(part + 1) * 64],
                                                  w[:, k, :, h * 256:(h + 1) * 256], start=False,
                                                  stop=part == 1 and k == 3)
                                last.then_inc(g1_mm, 1)
                            pe.wait_ge(disp, t1 + 1)
                            pe.wait_ge(o_ev, t1)
                            gather(1 - i)
                            pe.wait_ge(act_v, t1)
                            pe.wait_ge(at_ev, t1)
                            pe.wait_ge(sct_ev, t1)
                            for b in range(2):
                                last = tr(ps[:, 3, b * P:(b + 1) * P], act_s[:, b * P:(b + 1) * P], ident)
                            last.then_inc(at_mm, 1)
                            pe.wait_ge(xg_ev, t1 + 1)
                            token_transposes(1 - i)
                            pe.wait_ge(at_ev, t1 + 1)
                            s = 3 * i + 2
                            pe.wait_ge(arr[s], q * 16 + 16 * (before_moe(s) + 1))
                            w = ring[:, s, :].rearrange("p (f n) -> p f n", f=4)
                            for f in range(4):
                                for h in range(2):
                                    last = mm(ps[64 * h:64 * h + 64, 0, :],
                                              actT[i][:, f % 2, (f // 2) * 64:(f // 2 + 1) * 64],
                                              w[:, f, h * 512:(h + 1) * 512], start=f == 0, stop=f == 3)
                            last.then_inc(g2_mm, 1)
                            combine_transposes(1 - i)
                            pe.wait_ge(o_ev, t1 + 1)
                            for c in range(4):
                                for h in range(2):
                                    k = 4 * h + c
                                    r = slice(64 * h, 64 * h + 64)
                                    last = mm(ps[:, 4 + k // 2, (k % 2) * NT:(k % 2 + 1) * NT],
                                              O_s[i][r, c * P:(c + 1) * P], SCT[i][r, :], start=False, stop=True,
                                              skip_group_check=True)
                            last.then_inc(sc_mm, 1)

                @block.scalar
                def _(act):
                    A = nc.scalar.activation
                    a_n = [0]

                    def link(ins):
                        a_n[0] += 1
                        ins.then_inc(a_step, 1)
                        act.wait_ge(a_step, a_n[0])

                    def root_mean_square(i, bank):
                        A(sq[:, :, :], xT[:, :, :], ACT.Square).then_inc(sq_rdy[i], 1)
                        act.wait_ge(nrm_mm[i], 1)
                        A(rs[:, :], ps[:, bank, 0:NT], ACT.Sqrt, bias=cst[:, C_EPS:C_EPS + 1],
                          scale=1.0 / D).then_inc(nrm_sq[i], 1)

                    act.dma_start(vec[:, :], vecs[bass.ds(l, 1), :, :].rearrange("o p n -> (o p) n")).then_inc(
                        ld_vec, 16)
                    act.dma_start(row[:, :], rows[bass.ds(l, 1), :].broadcast_to((P, NR))).then_inc(ld_row, 16)

                    def cache(dst, src, s):
                        act.dma_start(dst, src[bass.ds(l, 1), :, :].rearrange("o p n -> (o p) n")).then_inc(s, 16)

                    def store(dst, src):
                        act.dma_start(dst[bass.ds(l, 1), :, :].rearrange("o p n -> (o p) n"), src).then_inc(
                            out_done, 16)

                    root_mean_square(0, 7)
                    act.wait_ge(lruw_zero, 1)
                    for j in range(2):
                        src = lru_gate_w[bass.ds(l, 1), bass.ds(j, 16, step=2), :, :]
                        act.dma_start(lruw[64 * j:64 * j + 64, :, 64 * j:64 * j + 64],
                                      src.rearrange("o b c e -> c (o b) e")).then_inc(ld_lruw, 16)
                    cache(c_ckv[:, :], cache_ckv, ld_ckv)
                    cache(c_kr[:, :], cache_krope, ld_kr)
                    cache(c_dk[:, :], cache_dk, ld_dk)
                    cache(c_dv[:, :], cache_dv, ld_dv)
                    act.dma_start(rw[:, :, :], router_w[bass.ds(l, 1), :, :].rearrange(
                        "o (k p) n -> p (o k) n", p=P)).then_inc(ld_rw, 16)
                    act.sem_inc(o_ev, 1)
                    act.wait_ge(sp_abs, 1)
                    link(A(sp[:, 8:16], sp[:, 0:8], ACT.Exp, scale=-1.0))
                    A(sp[:, 16:24], sp[:, 8:16], ACT.Ln, bias=one_col).then_inc(sp_ln, 1)

                    def modulate(i, scale, shift):
                        act.wait_ge(hraw[i], 1)
                        act.wait_ge(mod_rdy, 1)
                        for k in range(KC):
                            A(hT[:, k, P:NT], hT[:, k, P:NT], ACT.Identity, bias=modT[:, shift + k, 1:2],
                              scale=scale[:, k, 1:2]).then_inc(h_a[i], 1)

                    modulate(0, A1, 0)
                    for u in range(6, 14):
                        act.wait_ge(win_mm, u + 1)
                        bank = u % 6
                        if u < 8:
                            A(gel[:, 2 * (u - 6):2 * (u - 6) + 2, :],
                              ps[:, bank, :].rearrange("p (c n) -> p c n", c=2),
                              ACT.Gelu_apprx_tanh).then_inc(win_a, 1)
                        else:
                            A(projd[:, (u - 8) // 2, u % 2, :], ps[:, bank, :], ACT.Copy).then_inc(win_a, 1)

                    def lru_gates(d):
                        for t in range(2):
                            for c in range(RC):
                                i = 8 * d + 4 * t + c
                                act.wait_ge(lg_mm, i // 2 * 2 + 2)
                                dst = lru_t if t == 0 else lru_h[d]
                                A(dst[:, c, :], ps[:, 2 + (i % 8) // 2, (i % 2) * NT:(i % 2 + 1) * NT], ACT.Tanh,
                                  bias=gbh[:, i:i + 1], scale=0.5).then_inc(lg_ev, 1)
                        act.wait_ge(lg_ev, 8 * d + 4)
                        for c in range(RC):
                            z = clh[:, 4 * d + c:4 * d + c + 1]
                            last = A(lru_a[:, c, :], lru_t[:, c, :], ACT.Exp, bias=z, scale=z)
                        link(last)
                        for c in range(RC):
                            z = clh[:, 4 * d + c:4 * d + c + 1]
                            A(lru_t[:, c, :], lru_t[:, c, :], ACT.Tanh, bias=z, scale=z).then_inc(lru_at, 1)

                    def lru_roots(d):
                        for half in range(2):
                            c = slice(2 * half, 2 * half + 2)
                            act.wait_ge(lru_w, 2 * d + half + 1)
                            A(lru_t[:, c, :], lru_t[:, c, :], ACT.Sqrt).then_inc(lru_sq, 1)

                    act.wait_ge(prep, 2)
                    A(lam[:, 4:6], lam[:, 0:2], ACT.Exp).then_inc(lam_exp, 1)
                    lru_gates(0)
                    act.wait_ge(mla_n, 1)
                    store(new_ckv, projm[:, 0, OFF_KVA:OFF_KVA + KV_LORA])
                    store(new_krope, projm[:, 0, OFF_KVA + KV_LORA:M_COLS])
                    act.wait_ge(win_a, 8)
                    store(new_dv, projd[:, 2, 0, :])
                    for v in range(10):
                        act.wait_ge(p4_mm, v + 1)
                        half = v % 2
                        if v < 4:
                            A(q_tok[:, v // 2, 4 * half:4 * half + 4, :],
                              ps[:, half, 0:384].rearrange("p (h n) -> p h n", h=4), ACT.Copy).then_inc(p4_ev, 1)
                        else:
                            s = v // 2 - 2
                            src = ps[:, half, :].rearrange("p (h n) -> p h n", h=4)
                            A(k_tok[:, s, 4 * half:4 * half + 4, 0:NOPE], src[:, :, 0:NOPE], ACT.Copy)
                            A(v_tok[:, s, 256 * half:256 * half + 256].rearrange("p (h n) -> p h n", h=4),
                              src[:, :, NOPE:128], ACT.Copy).then_inc(p4_ev, 1)
                    lru_roots(0)
                    act.wait_ge(lru_fr, 1)
                    lru_gates(1)
                    lru_roots(1)

                    done = [0]

                    def merge_gates(n):
                        for _ in range(n):
                            j = done[0]
                            done[0] += 1
                            grp, ch = 2 * (j // 8), j % 8
                            b = BRANCHES[j // 8]
                            f = 8 * grp + ch
                            act.wait_ge(f_mm, f + 1)
                            if j >= 8:
                                act.wait_ge(f_dv, j - 8 + 1)
                            A(tg[:, ch, :], merge_ps(f), ACT.Tanh, bias=bmh[:, 8 * b + ch:8 * b + ch + 1],
                              scale=0.5).then_inc(f_ac, 1)

                    merge_gates(8)
                    act.wait_ge(lru_rdy, 1)
                    store(new_lru, fin[:, :])
                    act.wait_ge(dn_rdy, 3)
                    store(new_dk, projd[:, 1, 0, :])

                    def qk_copy(u):
                        n = QK if u < 8 else P
                        act.wait_ge(t_mm, 2 * u + 2)
                        A(qkT[u % 2][0:n, 384:640], ps[0:n, 1, 0:256], ACT.Copy).then_inc(qk_a, 1)

                    qk_copy(0)
                    for u in range(12):
                        act.wait_ge(nm_v, u + 1)
                        j = u % 2
                        if u < 8:
                            for n, c in enumerate((slice(0, 128), slice(128, 384))):
                                last = A(probs[j][:, 0, c], ps[:, 2 + j, c], ACT.Exp, bias=nm[:, j, n:n + 1],
                                         accum_out=sums[:, j, n:n + 1])
                        else:
                            for n, c in enumerate((slice(0, 128), slice(128, 384))):
                                for m in range(2):
                                    e = 2 * n + m
                                    last = A(probs[j][:, m, c], ps[:, 2 + m, c], ACT.Exp, bias=nm[:, j, e:e + 1],
                                             accum_out=sums[:, j, e:e + 1])
                        last.then_inc(ex_a, 1)
                        if u < 11:
                            qk_copy(u + 1)
                        merge_gates(1)
                        act.wait_ge(pt_mm, u + 1)
                        A(probsT[j], ps[:, 4, 0:384], ACT.Copy).then_inc(ptc, 1)
                        if u >= 8:
                            merge_gates(1)
                            act.wait_ge(ot_mm, u - 7)
                            A(odif[:, u - 8, :], ps[:, 5, NT:2 * NT], ACT.Copy,
                              scale=subg[:, 0:1]).then_inc(od_ev, 1)

                    act.wait_ge(pv_mm, 12)
                    act.wait_ge(out_done, 16 * 5)
                    cache(b1[0:N_EXP, :], exp_b1, ld_b1)
                    cache(b2[0:N_EXP, :], exp_b2, ld_b2)
                    act.wait_ge(f_dv, 32)
                    root_mean_square(1, 0)
                    modulate(1, A2, 24)
                    for n in range(4):
                        act.wait_ge(x2_mm, n + 1)
                        A(X2[:, n // 2, (n % 2) * 512:(n % 2 + 1) * 512], ps[:, 2 + n, :],
                          ACT.Copy).then_inc(x2_ev, 1)
                    act.wait_ge(nv_v, 1)
                    for g in range(G):
                        last = A(exl[:, g, :], lgt[:, g, :], ACT.Exp, bias=nv1[:, g:g + 1])
                    last.then_inc(exl_a, 1)
                    act.wait_ge(ct_mm, 1)
                    A(ctT[0:N_EXP, :], ps[0:N_EXP, 0, 0:NT], ACT.Copy).then_inc(ct_ev, 1)

                    act.wait_ge(ga_mm, 1)
                    A(Xg[0][:, :], ps[:, 0, :], ACT.Copy).then_inc(xg_ev, 1)
                    act.wait_ge(sct_mm, 1)
                    A(SCT[0][:, :], ps[:, 3, NT:2 * NT], ACT.Copy).then_inc(sct_ev, 1)
                    act.wait_ge(routed, 1)
                    pairs = act.value_load(meta[0:1, 1:2], min_val=N_EXP // 2, max_val=(N_EXP + MAX_EXTRA) // 2)
                    with act.Fori(0, pairs) as q:
                        for i in range(2):
                            t1 = q * 2 + (i + 1)
                            act.wait_ge(gate_v, t1)
                            A(sig_s, gate_s, ACT.Sigmoid, scale=ALPHA).then_inc(sig_a, 1)
                            act.wait_ge(ga_mm, t1 + 1)
                            A(Xg[1 - i][:, :], ps[:, 0, :], ACT.Copy).then_inc(xg_ev, 1)
                            act.wait_ge(g2_mm, t1)
                            A(O_s[i][:, :], ps[:, 0, :], ACT.Copy).then_inc(o_ev, 1)
                            act.wait_ge(sct_mm, t1 + 1)
                            A(SCT[1 - i][:, :], ps[:, 3, NT:2 * NT], ACT.Copy).then_inc(sct_ev, 1)

                @block.vector
                def _(dve):
                    V = nc.vector
                    v_n = [0]

                    def link(ins):
                        v_n[0] += 1
                        ins.then_inc(v_step, 1)
                        dve.wait_ge(v_step, v_n[0])

                    dve.sem_inc(up_v, 1)
                    dve.sem_inc(at_ev, 1)
                    dve.wait_ge(ld_vec, 16)
                    lmb = vec[:, V_LAM:V_LAM + 8]
                    V.scalar_tensor_tensor(out=sp[:, 0:8], in0=lmb, scalar=-1.0, in1=lmb, op0=ALU.mult,
                                           op1=ALU.max).then_inc(sp_abs, 1)

                    def normalise(i):
                        dve.wait_ge(nrm_sq[i], 1)
                        link(V.reciprocal(rs[:, :], rs[:, :]))
                        V.tensor_tensor(hT[:, :, :], xT[:, :, :], rs[:, None, :].broadcast_to((P, KC, NT)),
                                        ALU.mult).then_inc(hraw[i], 1)

                    normalise(0)

                    def rsqrt(x):
                        n = x.shape[1]
                        y, t = nwt[:, 0, 0:n], nwt[:, 1, 0:n]
                        link(V.tensor_scalar(y.bitcast(I32), x.bitcast(I32), 1, None, ALU.logical_shift_right))
                        link(V.tensor_scalar(y.bitcast(I32), y.bitcast(I32), -1.0, float(0x5f3759df), ALU.mult,
                                             ALU.add))
                        for it in range(4):
                            link(V.tensor_tensor(t, y, y, ALU.mult))
                            link(V.scalar_tensor_tensor(out=t, in0=t, scalar=-0.5, in1=x, op0=ALU.mult,
                                                        op1=ALU.mult))
                            link(V.scalar_tensor_tensor(out=y if it < 3 else x, in0=t, scalar=1.5, in1=y,
                                                        op0=ALU.add, op1=ALU.mult))

                    V.tensor_scalar(gbh[:, :], vec[:, V_GB:V_GB + 16], 0.5, None, ALU.mult)
                    V.tensor_scalar(bmh[:, :], vec[:, V_BM:V_BM + 24], 0.5, None, ALU.mult)
                    V.tensor_tensor(subg[:, :], vec[:, V_SUB:V_SUB + 1], vec[:, V_OML:V_OML + 1], ALU.mult)
                    link(V.tensor_scalar(sp[:, 24:32], vec[:, V_LAM:V_LAM + 8], -1.0, 0.0, ALU.mult, ALU.max))
                    dve.wait_ge(sp_ln, 1)
                    link(V.tensor_tensor(clh[:, :], sp[:, 24:32], sp[:, 16:24], ALU.add))
                    V.tensor_scalar(clh[:, :], clh[:, :], -4.0, None, ALU.mult).then_inc(prep, 1)
                    dve.wait_ge(ld_row, 16)
                    dl = row[:, R_DL:R_DL + 256].rearrange("p (a b n) -> p a b n", a=2, b=2)
                    link(V.tensor_tensor(lprod[:, :].rearrange("p (a n) -> p a n", a=2), dl[:, :, 0, :], dl[:, :, 1, :],
                                         ALU.mult))
                    V.tensor_reduce(lam[:, 0:2], lprod[:, :].rearrange("p (a n) -> p a n", a=2), AX_X,
                                    ALU.add).then_inc(prep, 1)

                    for r in range(3):
                        dve.wait_ge(ada_mm, r + 1)
                        V.tensor_copy(msb[:, r, :], ps[:, r, :]).then_inc(ada_sb, 1)
                    for r in range(3):
                        dve.wait_ge(ada_tr, r + 1)
                        src = ps[:, 3 + r, :].rearrange("p (b j z) -> p j b z", b=4, j=4)[:, :, :, 0:G]
                        dst = modT[:, 16 * r:16 * r + 16, :].rearrange("p (j b) z -> p j b z", j=4)
                        bias = vec[:, V_ADAB + 16 * r:V_ADAB + 16 * r + 16].rearrange("p (j b) -> p j b", j=4)
                        last = V.tensor_tensor(dst, src, bias[:, :, :, None].broadcast_to((P, 4, 4, G)), ALU.add)
                    link(last)
                    for out, sc, nrm in ((A1, 8, V_N1), (A2, 32, V_N2)):
                        V.scalar_tensor_tensor(out=out[:, :, :], in0=modT[:, sc:sc + 8, :], scalar=1.0,
                                               in1=vec[:, nrm:nrm + 8][:, :, None].broadcast_to((P, KC, G)),
                                               op0=ALU.add, op1=ALU.mult)
                    V.tensor_scalar(g1h[:, :, :], modT[:, 16:24, :], 0.5, None, ALU.mult).then_inc(mod_rdy, 1)

                    def modulate(i, scale, shift):
                        dve.wait_ge(mod_rdy, 1)
                        dve.wait_ge(hraw[i], 1)
                        for k in range(KC):
                            V.tensor_scalar(hT[:, k, 0:P], hT[:, k, 0:P], scale[:, k, 0:1],
                                            modT[:, shift + k, 0:1], ALU.mult, ALU.add).then_inc(h_v[i], 1)

                    modulate(0, A1, 0)

                    for u in range(4):
                        dve.wait_ge(win_mm, u + 1)
                        c0, w = (0, 512) if u < 2 else (512, 160)
                        V.tensor_copy(projm[:, u % 2, c0:c0 + w], ps[:, u, 0:w]).then_inc(win_v, 1)
                    dve.wait_ge(win_v, 4)
                    spare = at(E0 + 2048, G, 640)
                    for g in range(G):
                        V.tensor_tensor_reduce(out=spare[:, g, 0:Q_LORA], in0=projm[:, g, 0:Q_LORA],
                                               in1=projm[:, g, 0:Q_LORA], scale=1.0, scalar=0.0, op0=ALU.mult,
                                               op1=ALU.add, accum_out=ss[:, g:g + 1])
                        kv = projm[:, g, OFF_KVA:OFF_KVA + KV_LORA]
                        last = V.tensor_tensor_reduce(out=spare[:, g, 384:640], in0=kv, in1=kv, scale=1.0, scalar=0.0,
                                                      op0=ALU.mult, op1=ALU.add, accum_out=ss[:, 2 + g:3 + g])
                    link(last)
                    V.tensor_scalar(ss[:, 0:2], ss[:, 0:2], 1.0 / Q_LORA, EPS, ALU.mult, ALU.add)
                    link(V.tensor_scalar(ss[:, 2:4], ss[:, 2:4], 1.0 / KV_LORA, EPS, ALU.mult, ALU.add))
                    rsqrt(ss[:, 0:4])
                    for g in range(G):
                        V.tensor_scalar(projm[:, g, 0:Q_LORA], projm[:, g, 0:Q_LORA], ss[:, g:g + 1], None,
                                        ALU.mult)
                        kv = projm[:, g, OFF_KVA:OFF_KVA + KV_LORA]
                        last = V.scalar_tensor_tensor(out=kv, in0=kv, scalar=ss[:, 2 + g:3 + g],
                                                      in1=row[:, R_KVA:R_KVA + KV_LORA], op0=ALU.mult, op1=ALU.mult)
                    last.then_inc(mla_n, 1)

                    V.memset(xpad[:, :, :, 0:2], 0.0)
                    V.memset(xpad[:, :, :, P + 2:P + 3], 0.0)
                    for u in (4, 5):
                        dve.wait_ge(win_mm, u + 1)
                        V.tensor_copy(xpad[:, 2 * (u - 4):2 * (u - 4) + 2, :, 2:P + 2],
                                      ps[:, u, :].rearrange("p (c g n) -> p c g n", c=2, g=G)).then_inc(win_v, 1)
                    dve.wait_ge(win_v, 6)
                    for j in range(4):
                        for c in range(RC):
                            w = vec[:, V_CW + 4 * j + c:V_CW + 4 * j + c + 1]
                            o = xr[:, c, :].rearrange("p (g n) -> p g n", g=G)
                            if j == 0:
                                last = V.tensor_scalar(o, xpad[:, c, :, 0:P], w, vec[:, V_CB + c:V_CB + c + 1],
                                                       ALU.mult, ALU.add)
                            else:
                                last = V.scalar_tensor_tensor(out=o, in0=xpad[:, c, :, j:j + P], scalar=w, in1=o,
                                                              op0=ALU.mult, op1=ALU.add)
                        if j < 3:
                            link(last)
                    last.then_inc(conv_rdy, 1)

                    for b in range(3):
                        dve.wait_ge(p3_mm, 2 if b < 2 else 3)
                        V.tensor_scalar(qaT[:, b, :], ps[:, b // 2, (b % 2) * NT:(b % 2 + 1) * NT],
                                        vec[:, V_QA + b:V_QA + b + 1], None, ALU.mult).then_inc(p3_ev, 1)
                    for b in range(2):
                        dve.wait_ge(p3_mm, 4 + b)
                        V.tensor_copy(ckvT[:, b, :], ps[:, 6 + b, 0:384]).then_inc(p3_ev, 1)

                    dve.wait_ge(conv_rdy, 1)
                    for d in range(2):
                        h = lru_h[d]
                        for half in range(2):
                            c = slice(2 * half, 2 * half + 2)
                            dve.wait_ge(lru_at, 4 * d + 2 * half + 2)
                            V.scalar_tensor_tensor(out=h[:, c, :], in0=h[:, c, :], scalar=1.0, in1=xr[:, c, :],
                                                   op0=ALU.add, op1=ALU.mult)
                            link(V.tensor_tensor(lru_u[:, :, :], lru_a[:, c, :], lru_a[:, c, :], ALU.mult))
                            link(V.scalar_tensor_tensor(out=lru_u[:, :, :], in0=lru_u[:, :, :], scalar=1.0,
                                                        in1=lru_t[:, c, :], op0=ALU.add, op1=ALU.mult))
                            V.tensor_scalar(lru_t[:, c, :], lru_u[:, :, :], -0.25, 2.0 ** -116, ALU.mult,
                                            ALU.max).then_inc(lru_w, 1)
                            dve.wait_ge(lru_w, 2 * d + half + 1)
                        for half in range(2):
                            c = slice(2 * half, 2 * half + 2)
                            dve.wait_ge(lru_sq, 2 * d + half + 1)
                            link(V.tensor_tensor(h[:, c, :], h[:, c, :], lru_t[:, c, :], ALU.mult))
                            for ch in (2 * half, 2 * half + 1):
                                for g in range(G):
                                    init = 0.0 if g == 0 else vec[:, V_ST + 4 * d + ch:V_ST + 4 * d + ch + 1]
                                    lo, hi = g * P, (g + 1) * P
                                    if d == 0:
                                        aa, bb = lru_a[:, ch, lo:hi], h[:, ch, lo:hi]
                                    else:
                                        aa, bb = lru_a[:, ch, lo:hi][:, ::-1], h[:, ch, lo:hi][:, ::-1]
                                    last = V.tensor_tensor_scan(bb, aa, bb, init, ALU.mult, ALU.add)
                        last.then_inc(lru_fr, 1)
                    dve.wait_ge(lru_fr, 2)
                    V.tensor_copy(fin[:, 0:4], lru_h[0][:, :, P - 1])
                    V.tensor_copy(fin[:, 4:8], lru_h[1][:, :, 0])
                    link(V.tensor_tensor(xr[:, :, :], lru_h[0][:, :, :], lru_h[1][:, :, :], ALU.add))
                    V.tensor_tensor(gel[:, :, :], xr[:, :, :], gel[:, :, :], ALU.mult).then_inc(lru_rdy, 1)

                    def rotate(x, n, w, cos, sin):
                        swapped = scratch[:, 0:n * 4 * w].rearrange("p (h a b c) -> p h a b c", h=n, a=2, b=2)
                        for b in range(2):
                            s = sin.rearrange("p (a b c) -> p a b c", a=2, b=2)[:, :, b, :]
                            last_ = V.tensor_tensor(swapped[:, :, :, b, :], x[:, :, :, 1 - b, :],
                                                    s[:, None, :, :].broadcast_to((P, n, 2, w)), ALU.mult)
                        link(last_)
                        flat = x.rearrange("p h a b c -> p h (a b c)")
                        link(V.tensor_tensor(flat, flat, cos[:, None, :].broadcast_to((P, n, 4 * w)), ALU.mult))
                        return V.tensor_tensor(flat, flat, swapped.rearrange("p h a b c -> p h (a b c)"), ALU.add)

                    def axes(x, w):
                        return x.rearrange("p h (a b c) -> p h a b c", a=2, b=2)

                    def squares(x, n, w, dst):
                        s2 = scratch[:, 0:n * w].rearrange("p (h n) -> p h n", h=n)
                        link(V.tensor_tensor(s2, x, x, ALU.mult))
                        link(V.tensor_reduce(dst, s2, AX_X, ALU.add))

                    def scaled(x, n, w, r, gain, factor):
                        link(V.tensor_tensor(x, x, r[:, :, None].broadcast_to((P, n, w)), ALU.mult))
                        return V.scalar_tensor_tensor(out=x, in0=x, scalar=factor,
                                                      in1=gain[:, None, :].broadcast_to((P, n, w)), op0=ALU.mult,
                                                      op1=ALU.mult)

                    cosm, sinm = cst[:, C_CM:C_CM + ROPE], cst[:, C_SM:C_SM + ROPE]
                    cosd, sind = cst[:, C_CD:C_CD + DH], cst[:, C_SD:C_SD + DH]
                    for g in range(G):
                        dve.wait_ge(p4_ev, 2 * g + 2)
                        squares(q_tok[:, g, :, :], MLA_H, QK, ss[:, 8 * g:8 * g + 8])
                    link(V.tensor_scalar(ss[:, 0:16], ss[:, 0:16], 1.0 / QK, EPS, ALU.mult, ALU.add))
                    rsqrt(ss[:, 0:16])
                    for g in range(G):
                        last = scaled(q_tok[:, g, :, :], MLA_H, QK, ss[:, 8 * g:8 * g + 8], row[:, R_QN:R_QN + QK],
                                      float(QK) ** -0.5)
                        if g == 1:
                            link(last)
                            last = rotate(axes(q_tok[:, 1, :, NOPE:QK], 8), MLA_H, 8, cosm, sinm)
                        last.then_inc(qn_rdy, 1)
                        dve.wait_ge(qn_rdy, g + 1)
                    dve.wait_ge(ld_kr, 16)
                    kr = (projm[:, 0, 640:M_COLS], c_kr[:, :], projm[:, 1, 640:M_COLS])
                    for s in range(3):
                        dve.wait_ge(p4_ev, 2 * s + 6)
                        V.tensor_tensor_reduce(out=scratch[:, 1024:1056], in0=kr[s], in1=kr[s], scale=1.0,
                                               scalar=0.0, op0=ALU.mult, op1=ALU.add, accum_out=krs[:, s:s + 1])
                        r8 = ss[:, 8 * s:8 * s + 8]
                        squares(k_tok[:, s, :, 0:NOPE], MLA_H, NOPE, r8)
                        link(V.tensor_scalar(r8, r8, krs[:, s:s + 1], 1.0 / QK, ALU.add, ALU.mult))
                        link(V.tensor_scalar(r8, r8, EPS, None, ALU.add))
                    rsqrt(ss[:, 0:24])
                    for s in range(3):
                        r8 = ss[:, 8 * s:8 * s + 8]
                        link(V.tensor_copy(k_tok[:, s, :, NOPE:QK],
                                      kr[s][:, None, :].broadcast_to((P, MLA_H, ROPE))))
                        last = scaled(k_tok[:, s, :, :], MLA_H, QK, r8, row[:, R_KN:R_KN + QK], 1.0)
                        if s == 2:
                            link(last)
                            last = rotate(axes(k_tok[:, 2, :, NOPE:QK], 8), MLA_H, 8, cosm, sinm)
                        last.then_inc(kn_rdy, 1)
                        dve.wait_ge(kn_rdy, s + 1)
                    dve.wait_ge(win_a, 8)
                    for n in range(4):
                        squares(projd[:, n // 2, n % 2, :].rearrange("p (h n) -> p h n", n=DH), 8, DH,
                                ss[:, 8 * n:8 * n + 8])
                    link(V.tensor_scalar(ss[:, :], ss[:, :], 1.0 / DH, EPS, ALU.mult, ALU.add))
                    rsqrt(ss[:, :])
                    for n in range(4):
                        x = projd[:, n // 2, n % 2, :].rearrange("p (h n) -> p h n", n=DH)
                        gain = row[:, R_DQN:R_DQN + DH] if n < 2 else row[:, R_DKN:R_DKN + DH]
                        last = scaled(x, 8, DH, ss[:, 8 * n:8 * n + 8], gain, float(DH) ** -0.5 if n < 2 else 1.0)
                        if n % 2:
                            link(last)
                            last = rotate(axes(x, 16), 8, 16, cosd, sind)
                        last.then_inc(dn_rdy, 1)
                        dve.wait_ge(dn_rdy, n + 1)
                    dve.wait_ge(lam_exp, 1)
                    link(V.tensor_tensor(lam[:, 6:7], lam[:, 5:6], lam[:, 4:5], ALU.subtract))
                    link(V.tensor_tensor(lam[:, 7:8], lam[:, 6:7], vec[:, V_LI:V_LI + 1], ALU.subtract))
                    nlam = lam[:, 7:8]

                    done = [0]

                    def merge(n):
                        for _ in range(n):
                            j = done[0]
                            done[0] += 1
                            grp, ch = 2 * (j // 8) + 1, j % 8
                            if j < 24:
                                f = 8 * grp + ch
                                dve.wait_ge(f_mm, f + 1)
                                dve.wait_ge(f_ac, j + 1)
                                if j < 8:
                                    V.scalar_tensor_tensor(out=merged[:, ch, :], in0=tg[:, ch, :], scalar=1.0,
                                                           in1=merge_ps(f), op0=ALU.add,
                                                           op1=ALU.mult).then_inc(f_dv, 1)
                                else:
                                    dve.wait_ge(f_dv, j)
                                    link(V.scalar_tensor_tensor(out=mtmp, in0=tg[:, ch, :], scalar=1.0,
                                                                in1=merge_ps(f), op0=ALU.add, op1=ALU.mult))
                                    V.tensor_tensor(merged[:, ch, :], merged[:, ch, :], mtmp,
                                                    ALU.add).then_inc(f_dv, 1)
                            else:
                                f = 48 + ch
                                dve.wait_ge(f_mm, f + 1)
                                for g in range(G):
                                    c = slice(g * P, (g + 1) * P)
                                    last = V.scalar_tensor_tensor(out=xT[:, ch, c], in0=merge_ps(f)[:, c],
                                                                  scalar=g1h[:, ch, g:g + 1], in1=xT[:, ch, c],
                                                                  op0=ALU.mult, op1=ALU.add)
                                last.then_inc(f_dv, 1)

                    merge(8)

                    def qk_copy(u):
                        n = QK if u < 8 else P
                        dve.wait_ge(t_mm, 2 * u + 1)
                        V.tensor_copy(qkT[u % 2][0:n, 0:384], ps[0:n, 0, 0:384]).then_inc(qk_v, 1)

                    qk_copy(0)
                    for u in range(12):
                        j = u % 2
                        dve.wait_ge(s_mm, u + 1)
                        if u < 8:
                            V.tensor_reduce(nm[:, j, 0:1], ps[:, 2 + j, 0:128], AX_X, ALU.max, negate=True)
                            V.tensor_reduce(nm[:, j, 1:2], ps[:, 2 + j, 128:384], AX_X, ALU.max,
                                            negate=True).then_inc(nm_v, 1)
                        else:
                            V.tensor_reduce(nm[:, j, 0:2], ps[:, 2:4, 0:128], AX_X, ALU.max, negate=True)
                            V.tensor_reduce(nm[:, j, 2:4], ps[:, 2:4, 128:384], AX_X, ALU.max,
                                            negate=True).then_inc(nm_v, 1)
                        if u < 11:
                            qk_copy(u + 1)
                        dve.wait_ge(ex_a, u + 1)
                        if u < 8:
                            link(V.reciprocal(rcp[:, j, 0:2], sums[:, j, 0:2]))
                            for n, c in enumerate((slice(0, 128), slice(128, 384))):
                                last = V.tensor_scalar(probs[j][:, 0, c], probs[j][:, 0, c], rcp[:, j, n:n + 1],
                                                       None, ALU.mult)
                        else:
                            link(V.reciprocal(rcp[:, j, :], sums[:, j, :]))
                            V.tensor_scalar(nl[:, :], rcp[:, j, :].rearrange("p (n m) -> p n m", m=2)[:, :, 1], nlam,
                                            None, ALU.mult)
                            for n, c in enumerate((slice(0, 128), slice(128, 384))):
                                last = V.tensor_scalar(probs[j][:, 0, c], probs[j][:, 0, c],
                                                       rcp[:, j, 2 * n:2 * n + 1], None, ALU.mult)
                            link(last)
                            for n, c in enumerate((slice(0, 128), slice(128, 384))):
                                last = V.scalar_tensor_tensor(out=probs[j][:, 0, c], in0=probs[j][:, 1, c],
                                                              scalar=nl[:, n:n + 1], in1=probs[j][:, 0, c],
                                                              op0=ALU.mult, op1=ALU.add)
                        last.then_inc(pn_v, 1)
                        if u < 8 and u % 2:
                            dve.wait_ge(pv_mm, u + 1)
                            V.tensor_copy(omla[:, u // 2, :], ps[:, 5, 0:NT]).then_inc(om_ev, 1)
                        if u == 7:
                            merge(8)
                        if u >= 8:
                            dve.wait_ge(pv_mm, u + 1)
                            if u > 8:
                                dve.wait_ge(ot_mm, u - 8)
                            link(V.tensor_copy(on[:, :, :], ps[:, 5, 0:NT].rearrange("p (g n) -> p g n", g=G)))
                            for g in range(G):
                                last = V.tensor_tensor_reduce(out=onsq[:, g, :], in0=on[:, g, :],
                                                              in1=on[:, g, :], scale=1.0, scalar=0.0, op0=ALU.mult,
                                                              op1=ALU.add, accum_out=ss[:, g:g + 1])
                            link(last)
                            link(V.tensor_scalar(ss[:, 0:2], ss[:, 0:2], 1.0 / DV, EPS, ALU.mult, ALU.add))
                            rsqrt(ss[:, 0:2])
                            for g in range(G):
                                last = V.tensor_scalar(on[:, g, :], on[:, g, :], ss[:, g:g + 1], None, ALU.mult)
                            last.then_inc(on_v, 1)
                    merge(16)

                    dve.wait_ge(f_dv, 32)
                    normalise(1)
                    modulate(1, A2, 24)

                    dve.wait_ge(rt_mm, 1)
                    rb = row[:, R_RB:R_RB + N_EXP]
                    link(V.tensor_tensor(lgt[:, :, :], ps[:, 1, 0:64].rearrange("p (g e) -> p g e", g=G),
                                         rb[:, None, :].broadcast_to((P, G, N_EXP)), ALU.add))
                    for g in range(G):
                        last = V.max(top8[:, g, :], lgt[:, g, :])
                    link(last)
                    V.tensor_scalar(nv1[:, :], top8[:, :, 0], -1.0, None, ALU.mult).then_inc(nv_v, 1)
                    link(V.memset(top8[:, :, TOP_K:8], -3e38))
                    for g in range(G):
                        last = V.match_replace(rep[:, g, :], top8[:, g, :], lgt[:, g, :], 3e38)
                    link(last)
                    V.tensor_tensor(msk[:, :, :], rep[:, :, :], lgt[:, :, :], ALU.not_equal).then_inc(msk_v, 1)
                    dve.wait_ge(msk_v, 1)
                    dve.wait_ge(exl_a, 1)
                    for g in range(G):
                        last = V.tensor_tensor_reduce(out=cmb[:, g, :], in0=exl[:, g, :], in1=msk[:, g, :], scale=1.0,
                                                      scalar=0.0, op0=ALU.mult, op1=ALU.add,
                                                      accum_out=den[:, g:g + 1])
                    link(last)
                    link(V.reciprocal(den[:, :], den[:, :]))
                    V.tensor_tensor(cmb[:, :, :], cmb[:, :, :], den[:, :, None].broadcast_to((P, G, N_EXP)),
                                    ALU.mult).then_inc(cmb_v, 1)

                    V.memset(pmT[:, :, :], -1.0)
                    V.memset(cwT[:, :, :], 0.0)
                    link(V.memset(eidf[:, :], 0.0))
                    dve.wait_ge(pos_mm, 1)
                    dve.wait_ge(cmb_v, 1)
                    V.tensor_copy(eidf[:, 0:N_EXP], cst[:, C_EIDX:C_EIDX + N_EXP])
                    V.tensor_copy(cwT[:, :, 0:N_EXP], cmb[:, :, :])
                    V.tensor_copy(cnt[:, :], ps[:, 1, 128:160])
                    link(V.scalar_tensor_tensor(out=pm1[:, :, :], in0=ps[:, 1, 64:128].rearrange(
                        "p (g e) -> p g e", g=G), scalar=1.0, in1=msk[:, :, :], op0=ALU.add, op1=ALU.mult))
                    link(V.tensor_scalar(pmT[:, :, 0:N_EXP], pm1[:, :, :], -1.0, None, ALU.add))

                    def dispatch(p, t, last_sem):
                        def col(tab, g):
                            return tab[:, g, bass.ds(t, 1)]
                        for g in range(G):
                            V.tensor_scalar(S_s[p][:, g, :], cst[:, C_IOTA:C_IOTA + SLOTS], col(pmT, g), None,
                                            ALU.is_equal)
                        for g in range(G):
                            V.tensor_scalar(SC_s[p][:, g, :], cst[:, C_IOTA:C_IOTA + P], col(pmT, g), col(cwT, g),
                                            ALU.is_equal, ALU.mult)
                        V.tensor_scalar(oh[p][0:N_EXP, :],
                                        cst[0:N_EXP, C_PIDX:C_PIDX + 1].broadcast_to((N_EXP, SLOTS)),
                                        eidf[0:N_EXP, bass.ds(t, 1)], None, ALU.is_equal).then_inc(last_sem, 1)

                    dispatch(0, 0, disp)
                    link(V.tensor_scalar(xtra[:, :], cnt[:, :], 64.5, None, ALU.is_gt))
                    for m in (128.5, 192.5):
                        link(V.scalar_tensor_tensor(out=xtra[:, :], in0=cnt[:, :], scalar=m, in1=xtra[:, :],
                                                    op0=ALU.is_gt, op1=ALU.add))
                    link(V.tensor_tensor_scan(tend[:, :], ones[:, 0:N_EXP], xtra[:, :], 0.0, ALU.mult, ALU.add))
                    link(V.tensor_tensor(tbeg[:, :], tend[:, :], xtra[:, :], ALU.subtract))
                    kk = cst[:, C_KK:C_KK + MAX_EXTRA][:, :, None].broadcast_to((P, MAX_EXTRA, N_EXP))

                    def over_e(v):
                        return v[:, None, :].broadcast_to((P, MAX_EXTRA, N_EXP))

                    V.tensor_tensor(sel[:, :, :], kk, over_e(tbeg), ALU.is_ge)
                    link(V.tensor_tensor(tmpx[:, :, :], kk, over_e(tend), ALU.is_lt))
                    link(V.tensor_tensor(sel[:, :, :], sel[:, :, :], tmpx[:, :, :], ALU.mult))
                    V.tensor_tensor(tmpx[:, :, :], sel[:, :, :], over_e(cst[:, C_EIDX:C_EIDX + N_EXP]), ALU.mult)
                    link(V.tensor_tensor(tmpy[:, :, :], kk, over_e(tbeg), ALU.subtract))
                    V.tensor_reduce(eidf[:, N_EXP:N_EXP + MAX_EXTRA], tmpx[:, :, :], AX_X, ALU.add)
                    link(V.scalar_tensor_tensor(out=tmpy[:, :, :], in0=tmpy[:, :, :], scalar=1.0, in1=sel[:, :, :],
                                                op0=ALU.add, op1=ALU.mult))
                    link(V.tensor_reduce(psub[:, :], tmpy[:, :, :], AX_X, ALU.add))
                    for g in range(G):
                        link(V.tensor_tensor(tmpx[:, :, :], sel[:, :, :], over_e(pm1[:, g, :]), ALU.mult))
                        link(V.tensor_tensor(tmpy[:, :, :], sel[:, :, :], over_e(cmb[:, g, :]), ALU.mult))
                        dst = pmT[:, g, N_EXP:N_EXP + MAX_EXTRA]
                        V.tensor_reduce(cwT[:, g, N_EXP:N_EXP + MAX_EXTRA], tmpy[:, :, :], AX_X, ALU.add)
                        link(V.tensor_reduce(dst, tmpx[:, :, :], AX_X, ALU.add))
                        link(V.scalar_tensor_tensor(out=dst, in0=psub[:, :], scalar=-float(SLOTS), in1=dst,
                                                    op0=ALU.mult, op1=ALU.add))
                        link(V.tensor_scalar(dst, dst, -1.0, None, ALU.add))
                    link(V.tensor_scalar(cmp8[:, :], cst[:, C_KK:C_KK + 8], 2.0, tend[:, N_EXP - 1:N_EXP], ALU.mult,
                                         ALU.is_lt))
                    link(V.tensor_reduce(npf[:, 0:1], cmp8[:, :], AX_X, ALU.add))
                    link(V.tensor_scalar(npf[:, 1:2], npf[:, 0:1], float(N_EXP // 2), None, ALU.add))
                    V.tensor_copy(eidi[:, :], eidf[:, N_EXP:N_EXP + MAX_EXTRA])
                    V.tensor_copy(meta[:, :], npf[:, :]).then_inc(routed, 1)

                    dve.wait_ge(xt_mm, 1)
                    V.tensor_copy(xTg[0].rearrange("p a b -> p (a b)"), ps[:, 1, :]).then_inc(xt_ev, 1)
                    dve.wait_ge(routed, 1)
                    pairs = dve.value_load(meta[0:1, 1:2], min_val=N_EXP // 2, max_val=(N_EXP + MAX_EXTRA) // 2)
                    with dve.Fori(0, pairs) as q:
                        for i in range(2):
                            t1 = q * 2 + (i + 1)
                            dispatch(1 - i, t1, disp)
                            dve.wait_ge(g1_mm, q * 4 + 2 * (i + 1))
                            V.tensor_scalar(gate_s, ps[:, 2, 0:256], LIMIT, None, ALU.min).then_inc(gate_v, 1)
                            V.tensor_scalar(up_s, ps[:, 2, 256:512], LIMIT, -LIMIT, ALU.min,
                                            ALU.max).then_inc(up_v, 1)
                            dve.wait_ge(up_v, t1 + 1)
                            V.scalar_tensor_tensor(out=up_s, in0=up_s, scalar=1.0, in1=gate_s, op0=ALU.add,
                                                   op1=ALU.mult).then_inc(step_m, 1)
                            dve.wait_ge(step_m, t1)
                            dve.wait_ge(sig_a, t1)
                            V.tensor_tensor(act_s, up_s, sig_s, ALU.mult).then_inc(act_v, 1)
                            dve.wait_ge(at_mm, t1)
                            V.tensor_copy(actT[i].rearrange("p a b -> p (a b)"), ps[:, 3, 0:256]).then_inc(at_ev, 1)
                            dve.wait_ge(xt_mm, t1 + 1)
                            V.tensor_copy(xTg[1 - i].rearrange("p a b -> p (a b)"), ps[:, 1, :]).then_inc(xt_ev, 1)
                    dve.wait_ge(sc_mm, pairs * 2)
                    for k in range(KC):
                        for g in range(G):
                            c = slice(g * P, (g + 1) * P)
                            V.scalar_tensor_tensor(out=xT[:, k, c],
                                                   in0=ps[:, 4 + k // 2, (k % 2) * NT + g * P:(k % 2) * NT + (g + 1) * P],
                                                   scalar=modT[:, 40 + k, g:g + 1], in1=xT[:, k, c], op0=ALU.mult,
                                                   op1=ALU.add)
            for s in sems:
                nc.gpsimd.sem_clear(s)
            nc.all_engine_barrier()

        with nc.Block() as block:
            @block.sync
            def _(sp_):
                sp_.dma_start(y_out, xT[:, :, :]).then_inc(s_set[5], 16)
                sp_.wait_ge(s_set[5], 16)


def constants(np):
    c = np.zeros((P, NC), np.float32)
    c[:, C_ID:C_ID + P] = np.eye(P)
    c[:, C_UT:C_UT + P] = np.triu(np.ones((P, P)), 1)
    c[:, C_ONE:C_ONE + P] = 1.0
    c[:, C_IOTA:C_IOTA + P] = np.tile(np.arange(SLOTS), 2)
    for dim, cc, cs in ((ROPE, C_CM, C_SM), (DH, C_CD, C_SD)):
        half = dim // 2
        inv = (1.0 / (np.float32(10000.0) ** (np.arange(0, half, 2, dtype=np.float32) / np.float32(half))))
        inv = inv.astype(np.float32)
        t = np.arange(P)
        ang = [((pos.astype(np.float32))[:, None] * inv[None, :]).astype(np.float32) for pos in (t // 64, t % 64)]
        ang = np.concatenate([ang[0], ang[0], ang[1], ang[1]], axis=1)
        sign = np.tile(np.repeat([-1.0, 1.0], half // 2), 2)
        c[:, cc:cc + dim] = np.cos(ang)
        c[:, cs:cs + dim] = np.sin(ang) * sign
    c[:, C_PIDX] = np.arange(P)
    c[:, C_EPS] = EPS
    c[:, C_KK:C_KK + MAX_EXTRA] = np.arange(MAX_EXTRA)
    c[:, C_EIDX:C_EIDX + N_EXP] = np.arange(N_EXP)
    return c


def kernel(**inputs):
    import math

    import numpy as np
    import concourse.bacc as _bacc
    from concourse import mybir as _mybir
    from concourse.bass_utils import run_bass_kernel_spmd as _run

    a = {k: np.asarray(v) for k, v in inputs.items()}

    def columns(x):
        return x.reshape(L, -1, P).transpose(0, 2, 1)

    x = np.concatenate([a["x_prompt"][0], a["x_sample"][0]], axis=0)
    cond = np.stack([a["c_ctx"], a["c"][0]], axis=0)
    lam_init = np.array([0.8 - 0.6 * math.exp(-0.3 * i) for i in range(L)])
    li = np.zeros((L, P, 2), np.float32)
    li[:, :, 0] = lam_init[:, None]
    li[:, :, 1] = 1.0 - lam_init[:, None]
    vecs = np.concatenate([columns(v) for v in (
        a["ada_b"], a["norm1_g"], a["norm2_g"], a["b_merge"], a["mla_qa_norm"], a["diff_subln"],
        a["lru_conv_w"].reshape(L, -1), a["lru_conv_b"], a["lru_gate_b"].reshape(L, -1),
        a["lru_lambda"].reshape(L, -1), a["state_lru"][0].reshape(L, -1))] + [li], axis=2)
    rows = np.concatenate([a["mla_kva_norm"], a["mla_qn"], a["mla_kn"], a["diff_qn"], a["diff_kn"],
                           a["diff_lambda"].reshape(L, -1), a["router_b"]], axis=1)
    arrays = {
        "x_in": x.T.reshape(KC, P, NT).transpose(1, 0, 2),
        "cond_in": cond.T.reshape(KC, P, G).transpose(1, 0, 2),
        "consts": constants(np), "vecs": vecs, "rows": rows,
        "ada_w": a["ada_w"], "w_in": a["w_in"], "w_q_b": a["w_q_b"], "w_kv_b": a["w_kv_b"],
        "lru_gate_w": a["lru_gate_w"].reshape(L, 32, 64, 64),
        "w_o_mla": a["w_o_mla"], "w_o_lru": a["w_o_lru"], "w_o_diff": a["w_o_diff"],
        "w_merge": a["w_merge"], "w_out": a["w_out"], "router_w": a["router_w"],
        "exp_w1": a["exp_w1"].reshape(L * N_EXP, D, 2 * D_EXP), "exp_b1": a["exp_b1"],
        "exp_w2": a["exp_w2"].reshape(L * N_EXP, D_EXP, D), "exp_b2": a["exp_b2"],
        "cache_ckv": a["cache_mla_ckv"][0], "cache_krope": a["cache_mla_krope"][0],
        "cache_dk": a["cache_diff_k"][0].reshape(L, P, 512), "cache_dv": a["cache_diff_v"][0].reshape(L, P, 512),
    }
    outs = {"y_out": (P, KC, NT), "new_ckv": (L, P, KV_LORA), "new_krope": (L, P, ROPE), "new_lru": (L, P, 8),
            "new_dk": (L, P, 512), "new_dv": (L, P, 512)}
    nc = _bacc.Bacc("TRN2", target_bir_lowering=False, num_devices=1)
    given, args = {}, []
    for name, v in arrays.items():
        given[f"{name}_dram"] = np.ascontiguousarray(v)
        args.append(nc.dram_tensor(f"{name}_dram", v.shape, _mybir.dt.float32, kind="ExternalInput").ap())
    for name, shape in outs.items():
        args.append(nc.dram_tensor(f"{name}_dram", shape, _mybir.dt.float32, kind="ExternalOutput").ap())
    build(nc, *args)
    r = _run(nc, [given], core_ids=[0]).results[0]
    y = r["y_out_dram"].transpose(1, 0, 2).reshape(D, NT).T
    return (np.ascontiguousarray(y[:P])[None], np.ascontiguousarray(y[P:])[None],
            r["new_ckv_dram"][None], r["new_krope_dram"][None],
            np.ascontiguousarray(r["new_lru_dram"].transpose(0, 2, 1)).reshape(1, L, 2, D_RNN),
            r["new_dk_dram"].reshape(1, L, P, DIFF_H, 2, DH), r["new_dv_dram"].reshape(1, L, P, DIFF_H, DV))
```

```python
from contextlib import ExitStack

import concourse.bass as bass
from concourse import mybir

F32 = mybir.dt.float32
I32 = mybir.dt.int32
ALU = mybir.AluOpType
ACT = mybir.ActivationFunctionType
AX_X = mybir.AxisListType.X

P = 128
D = 1024
KC = D // P
G = 2
NT = G * P
L = 2
EPS = 1e-6

MLA_H, NOPE, ROPE, VD = 8, 64, 32, 64
QK = NOPE + ROPE
Q_LORA, KV_LORA = 384, 256
D_RNN = 512
RC = D_RNN // P
DIFF_H, DH, DV = 4, 64, 128
N_EXP, D_EXP, TOP_K = 32, 512, 4
SLOTS = 64
LIMIT, ALPHA = 7.0, 1.702
MAX_EXTRA = 16

OFF_KVA = Q_LORA
OFF_LRU = OFF_KVA + KV_LORA + ROPE
OFF_DQ = OFF_LRU + 2 * D_RNN
IN_COLS = OFF_DQ + 3 * 512
M_COLS = OFF_LRU

V_ADAB, V_N1, V_N2, V_BM, V_QA, V_SUB = 0, 48, 56, 64, 88, 91
V_CW, V_CB, V_GB, V_LAM, V_ST, V_LI, V_OML = 92, 108, 112, 128, 136, 144, 145
NV = 146
R_KVA, R_QN, R_KN, R_DQN, R_DKN, R_DL, R_RB = 0, 256, 352, 448, 512, 576, 832
NR = 864
C_ID, C_UT, C_ONE, C_IOTA = 0, 128, 256, 384
C_CM, C_SM, C_CD, C_SD = 512, 544, 576, 640
C_PIDX, C_KK, C_EIDX, C_EPS = 704, 705, 721, 753
NC = 754

RING = 6
SLOT = 4096
S_ADA = (0, 15, 25)
S_IN = (4, 5, 6, 7, 10, 11, 12)
S_QB, S_KVB = 8, 9
S_WM = {1: 13, 0: 20, 2: 23}
S_WO = {1: 19, 0: 22, 2: 29}
S_OUT = 30
PRE = 32
IN_SLICES = ((0, 512), (512, 160), (OFF_LRU, 512), (OFF_LRU + 512, 512), (OFF_DQ, 512), (OFF_DQ + 512, 512),
             (OFF_DQ + 1024, 512))
BRANCHES = (1, 0, 2)
MERGE = [("gate", 1, ch) for ch in range(KC)]
for _b, _next in ((1, 0), (0, 2)):
    for _ch in range(KC):
        MERGE += [("proj", _b, _ch), ("gate", _next, _ch)]
MERGE += [("proj", 2, ch) for ch in range(KC)] + [("out", 0, ch) for ch in range(KC)]


def merge_slot(kind, b, ch):
    return {"gate": S_WM[b] + ch // 4, "proj": S_WO[b], "out": S_OUT + ch // 4}[kind]


MOE_SLOT = [(PRE + j) % RING for j in range(RING)]


def later_uses(s):
    return len(range(s, PRE, RING)) - 1


def build(nc, x_in, cond_in, consts, vecs, rows, ada_w, w_in, w_q_b, w_kv_b, lru_gate_w, w_o_mla, w_o_lru,
          w_o_diff, w_merge, w_out, router_w, exp_w1, exp_b1, exp_w2, exp_b2, cache_ckv, cache_krope,
          cache_dk, cache_dv, y_out, new_ckv, new_krope, new_lru, new_dk, new_dv):
    ctx = ExitStack()
    with ctx:
        def sb(name, shape, dt=F32):
            return ctx.enter_context(nc.sbuf_tensor(name, shape, dt))

        sems = []

        def sem(name):
            s = ctx.enter_context(nc.semaphore(name))
            sems.append(s)
            return s

        cst = sb("cst", [P, NC])
        vec = sb("vec", [P, NV])
        row = sb("row", [P, NR])
        cT = sb("cT", [P, KC, 32])
        modT = sb("modT", [P, 48, G])
        A1 = sb("A1", [P, KC, G])
        A2 = sb("A2", [P, KC, G])
        g1h = sb("g1h", [P, KC, G])
        gbh = sb("gbh", [P, 16])
        bmh = sb("bmh", [P, 24])
        sp = sb("sp", [P, 32])
        clh = sb("clh", [P, 8])
        lam = sb("lam", [P, 8])
        lprod = sb("lprod", [P, 128])
        subg = sb("subg", [P, 1])
        ss = sb("ss", [P, 32])
        nwt = sb("nwt", [P, 2, 32])
        krs = sb("krs", [P, 4])
        nm = sb("nm", [P, 2, 4])
        sums = sb("sums", [P, 2, 4])
        rcp = sb("rcp", [P, 2, 4])
        nl = sb("nl", [P, 2])
        rs = sb("rs", [P, NT])
        fin = sb("fin", [P, 8])
        xT = sb("xT", [P, KC, NT])
        hT = sb("hT", [P, KC, NT])
        rw = sb("rw", [P, KC, N_EXP])
        ring = sb("ring", [P, RING, SLOT])
        arena = sb("arena", [P, 21344])
        meta = sb("meta", [P, 2], I32)
        eidi = sb("eidi", [P, MAX_EXTRA], I32)
        ps = ctx.enter_context(nc.psum_tensor("ps", [P, 8, 512], F32))

        def at(off, *dims):
            n = 1
            for d in dims:
                n *= d
            v = arena[:, off:off + n]
            if len(dims) == 2:
                return v.rearrange("p (a b) -> p a b", a=dims[0])
            if len(dims) == 3:
                return v.rearrange("p (a b c) -> p a b c", a=dims[0], b=dims[1])
            if len(dims) == 4:
                return v.rearrange("p (a b c d) -> p a b c d", a=dims[0], b=dims[1], c=dims[2])
            return v

        merged = at(0, KC, NT)
        qaT = at(0, 3, NT)
        ckvT = at(768, 2, 384)
        lru_u = at(1536, 2, NT)
        tg = at(2048, KC, NT)
        lruw = at(2048, 16, P)
        projm = at(4096, G, M_COLS)
        projd = at(5440, 3, G, 512)
        E0 = 8512
        xpad = at(E0, RC, G, P + 3)
        lru_a = at(E0, RC, NT)
        lru_t = at(E0 + 1024, RC, NT)
        lru_h = [at(E0 + 2048, RC, NT), at(E0 + 3072, RC, NT)]
        xr = at(E0 + 4096, RC, NT)
        gel = at(E0 + 5120, RC, NT)
        scratch = at(0, 768)
        qkT = [at(E0, 640), at(E0 + 640, 640)]
        probs = [at(E0 + 1280, 2, 384), at(E0 + 2048, 2, 384)]
        probsT = [at(E0 + 2816, 384), at(E0 + 3200, 384)]
        on = at(E0 + 3584, G, DV)
        mtmp = at(E0 + 3840, NT)
        omla = at(E0 + 4096, 4, NT)
        odif = at(E0 + 5120, 4, NT)
        Q0 = E0 + 6144
        q_tok = at(Q0, G, MLA_H, QK)
        onsq = at(Q0, G, DV)
        msb = (at(Q0, 512), at(768, 512), at(Q0 + 512, 512))
        v_tok = at(Q0 + 1536, 3, 512)
        k_tok = at(Q0 + 3072, 3, MLA_H, QK)
        sq = at(Q0 + 3072, KC, NT)
        assert Q0 + 3072 + 2304 == 20032
        c_ckv = at(20032, KV_LORA)
        c_kr = at(20288, ROPE)
        c_dk = at(20320, 512)
        c_dv = at(20832, 512)
        b1 = at(5440, D)
        b2 = at(6464, D)
        X2 = at(E0, G, D)
        Xg = at(E0 + 2048, D)
        xTg = at(E0 + 3072, KC, P)
        gate_s, up_s, sig_s, act_s = (at(E0 + 4096 + 512 * i, 512) for i in range(4))
        actT = at(E0 + 6144, 4, P)
        O_s = at(E0 + 6656, D)
        SCT = at(E0 + 7680, NT)
        S_s = at(E0 + 7936, G, P)
        SC_s = at(E0 + 8192, G, P)
        oh = at(E0 + 8448, P)
        T0 = E0 + 8576
        lgt, rep, msk, exl, cmb = (at(T0 + 64 * i, G, N_EXP) for i in range(5))
        pm1 = at(T0 + 320, G, N_EXP)
        top8 = at(T0 + 384, G, 8)
        nv1 = at(T0 + 400, G)
        den = at(T0 + 402, G)
        cnt = at(T0 + 404, N_EXP)
        xtra = at(T0 + 436, N_EXP)
        tend = at(T0 + 468, N_EXP)
        tbeg = at(T0 + 500, N_EXP)
        npf = at(T0 + 532, 2)
        cmp8 = at(T0 + 534, 8)
        psub = at(T0 + 542, MAX_EXTRA)
        NTAB = N_EXP + MAX_EXTRA + 2
        pmT = at(T0 + 558, G, NTAB)
        cwT = at(T0 + 658, G, NTAB)
        eidf = at(T0 + 758, NTAB)
        ctT = at(T0 + 808, NT)
        K0 = T0 + 1064
        sel, tmpx, tmpy = (at(K0 + 512 * i, MAX_EXTRA, N_EXP) for i in range(3))
        assert K0 + 3 * 512 <= 21344

        ident = cst[:, C_ID:C_ID + P]
        ustrict = cst[:, C_UT:C_UT + P]
        ones = cst[:, C_ONE:C_ONE + P]
        one_col = cst[:, C_ONE:C_ONE + 1]

        arr = [sem(f"slot{s}_arrived") for s in range(RING)]
        ld_vec, ld_row, ld_lruw = sem("vec_in"), sem("row_in"), sem("lruw_in")
        ld_ckv, ld_kr, ld_dk, ld_dv = sem("cckv_in"), sem("ckr_in"), sem("cdk_in"), sem("cdv_in")
        ld_rw, ld_b1, ld_b2 = sem("rw_in"), sem("b1_in"), sem("b2_in")
        out_done = sem("out_done")
        lruw_zero = sem("lruw_zero")
        v_step, a_step = sem("dve_step"), sem("act_step")
        sq_rdy, nrm_mm, nrm_sq, hraw, h_v, h_a = (
            [sem(f"{n}{i}") for i in range(2)] for n in ("sq_rdy", "nrm_mm", "nrm_sqrt", "hraw", "h_dve", "h_act"))
        ada_mm, ada_sb, ada_tr, prep, mod_rdy = (sem(n) for n in
                                                 ("ada_mm", "ada_sb", "ada_tr", "prep", "mod_rdy"))
        sp_abs, sp_ln, lam_exp = sem("sp_abs"), sem("sp_ln"), sem("lam_exp")
        win_mm, win_v, win_a = sem("win_mm"), sem("win_evac_v"), sem("win_evac_a")
        mla_n, conv_rdy = sem("mla_norm"), sem("conv_rdy")
        p3_mm, p3_ev, p4_mm, p4_ev = sem("lat_tr"), sem("lat_evac"), sem("exp_mm"), sem("exp_evac")
        lg_mm, lg_ev, lru_at, lru_w, lru_sq, lru_fr, lru_rdy = (
            sem(n) for n in ("lru_mm", "lru_evac", "lru_at", "lru_w", "lru_sqrt", "lru_free", "lru_rdy"))
        qn_rdy, kn_rdy, dn_rdy = sem("qn_rdy"), sem("kn_rdy"), sem("dn_rdy")
        f_mm, f_ac, f_dv = sem("merge_mm"), sem("merge_act"), sem("merge_dve")
        t_mm, qk_v, qk_a, s_mm, nm_v, ex_a = (sem(n) for n in ("qk_tr", "qk_evac_v", "qk_evac_a", "score_mm",
                                                              "negmax", "exp_done"))
        pn_v, pt_mm, ptc, pv_mm, om_ev, on_v, ot_mm, od_ev = (
            sem(n) for n in ("probs_rdy", "pt_tr", "pt_evac", "pv_mm", "omla_rdy", "on_rdy", "on_tr", "odif_rdy"))
        rt_mm, x2_mm, x2_ev, nv_v, exl_a, msk_v, pos_mm, cmb_v, ct_mm, ct_ev, y0_mm, routed = (
            sem(n) for n in ("router_mm", "x2_tr", "x2_evac", "negtop", "exl_rdy", "mask_rdy", "pos_mm", "cmb_rdy",
                             "ct_mm", "ct_evac", "y_init", "routed"))
        disp, ga_mm, xg_ev, xt_mm, xt_a, xt_v = (sem(n) for n in ("disp_rdy", "gather_mm", "xg_evac", "xt_tr",
                                                                  "xt_evac_a", "xt_evac_v"))
        g1_mm, gate_v, up_v, prod_v, sig_a, act_v, at_mm, at_ev = (
            sem(n) for n in ("w1_mm", "gate_rdy", "up_rdy", "prod_rdy", "sig_rdy", "act_rdy", "act_tr",
                             "act_evac"))
        g2_mm, o_a, o_v, sct_mm, sct_ev, sc_mm = (sem(n) for n in ("w2_mm", "o_evac_a", "o_evac_v", "sct_tr",
                                                                   "sct_evac", "scatter_mm"))
        early = [ctx.enter_context(nc.semaphore(f"slot{s}_early")) for s in range(RING)]
        s_set = [ctx.enter_context(nc.semaphore(f"setup{i}")) for i in range(6)]

        def consumed(pos):
            for r in range(3):
                if S_ADA[r] <= pos < S_ADA[r] + 4:
                    return ada_mm, r + 1
            if pos in S_IN:
                return win_mm, 2 * (S_IN.index(pos) + 1)
            if pos in (S_QB, S_KVB):
                return p4_mm, {S_QB: 4, S_KVB: 10}[pos]
            return f_mm, max(f for f, m in enumerate(MERGE) if merge_slot(*m) == pos) + 1

        def arrived(eng, pos):
            if pos < RING:
                eng.wait_ge(early[pos], l * 16 + 16)
            else:
                eng.wait_ge(arr[pos % RING], 16 * (pos // RING))
            return ring[:, pos % RING, :]

        def merge_evac(eng, f):
            gates = sum(m[0] == "gate" for m in MERGE[:f - 1])
            if MERGE[f - 2][0] == "gate":
                eng.wait_ge(f_ac, gates)
            else:
                eng.wait_ge(f_dv, f - 1 - gates)

        def merge_ps(f):
            return ps[:, 6 + f % 2, 0:NT]

        def rows_of(w, layer, nk, c0, nc_):
            return w[bass.ds(layer, 1), 0:nk * P, c0:c0 + nc_].rearrange("o (k p) n -> p (o k) n", p=P)

        def ada_or_in(layer, pos):
            for r in range(3):
                if S_ADA[r] <= pos < S_ADA[r] + 4:
                    return rows_of(ada_w, layer, KC, (4 * r + pos - S_ADA[r]) * 512, 512), 512
            c0, w = IN_SLICES[S_IN.index(pos)]
            return rows_of(w_in, layer, KC, c0, w), w

        def load_early(eng, layer, pos):
            src, w = ada_or_in(layer, pos)
            eng.dma_start(ring[:, pos, 0:KC * w].rearrange("p (k n) -> p k n", n=w), src).then_inc(early[pos], 16)

        with nc.Block() as block:
            @block.sync
            def _(sp_):
                sp_.dma_start(xT[:, :, :], x_in).then_inc(s_set[2], 16)
                sp_.dma_start(cT[:, :, 0:G], cond_in).then_inc(s_set[0], 16)
                sp_.dma_start(cst[:, :], consts).then_inc(s_set[1], 16)
                for pos in range(RING):
                    load_early(sp_, 0, pos)
                sp_.wait_ge(s_set[1], 16)
                sp_.wait_ge(s_set[2], 16)

            @block.scalar
            def _(act):
                act.wait_ge(s_set[0], 16)
                nc.scalar.activation(cT[:, :, G:2 * G], cT[:, :, 0:G], ACT.Tanh, scale=0.5).then_inc(s_set[3], 1)

            @block.vector
            def _(dve):
                dve.wait_ge(s_set[3], 1)
                nc.vector.tensor_scalar(cT[:, :, G:2 * G], cT[:, :, G:2 * G], 0.5, 0.5, ALU.mult,
                                        ALU.add).then_inc(s_set[4], 1)
                dve.wait_ge(s_set[4], 1)
                nc.vector.tensor_tensor(cT[:, :, 0:G], cT[:, :, 0:G], cT[:, :, G:2 * G],
                                        ALU.mult).then_inc(s_set[4], 1)
                dve.wait_ge(s_set[4], 2)
                nc.vector.memset(cT[:, :, G:32], 0.0).then_inc(s_set[4], 1)

        with nc.Fori(0, L) as l:
            with nc.Block() as block:
                @block.sync
                def _(sp_):
                    def load(pos, src, n):
                        dst = ring[:, pos % RING, 0:n]
                        s, v = consumed(pos - RING)
                        sp_.wait_ge(s, v)
                        shape = src.shape
                        sp_.dma_start(dst.rearrange("p (a b) -> p a b", b=shape[2]), src).then_inc(
                            arr[pos % RING], 16)

                    wo = {0: w_o_mla, 1: w_o_lru, 2: w_o_diff}
                    for pos in range(RING, PRE):
                        for b in BRANCHES:
                            if pos in (S_WM[b], S_WM[b] + 1):
                                load(pos, rows_of(w_merge, l, KC, b * D + (pos - S_WM[b]) * 512, 512), SLOT)
                            if pos == S_WO[b]:
                                load(pos, rows_of(wo[b], l, 4, 0, D), SLOT)
                        if pos == S_QB:
                            load(pos, rows_of(w_q_b, l, 3, 0, 768), 3 * 768)
                        elif pos == S_KVB:
                            load(pos, rows_of(w_kv_b, l, 2, 0, 1024), 2048)
                        elif pos >= S_OUT:
                            load(pos, rows_of(w_out, l, KC, (pos - S_OUT) * 512, 512), SLOT)
                        elif pos in S_IN or any(r <= pos < r + 4 for r in S_ADA):
                            src, w = ada_or_in(l, pos)
                            load(pos, src, KC * w)

                    def pair(experts, waits):
                        base = [l * N_EXP + e for e in experts]
                        srcs = [exp_w1[bass.ds(b, 1), 0:512, :] for b in base] + \
                            [exp_w1[bass.ds(b, 1), 512:1024, :] for b in base] + \
                            [exp_w2[bass.ds(b, 1), :, :] for b in base]
                        for slot, src, (s, v) in zip(MOE_SLOT, srcs, waits):
                            sp_.wait_ge(s, v)
                            sp_.dma_start(ring[:, slot, :].rearrange("p (k n) -> p k n", n=D),
                                          src.rearrange("o (k p) n -> p (o k) n", p=P)).then_inc(arr[slot], 16)

                    def freed(pairs_before):
                        return [(g1_mm, pairs_before * 2 - 1)] * 2 + [(g1_mm, pairs_before * 2)] * 2 + \
                            [(g2_mm, pairs_before * 2)] * 2

                    pair((0, 1), [consumed(PRE - RING + j) for j in range(RING)])
                    with sp_.Fori(1, N_EXP // 2) as q:
                        pair((q * 2, q * 2 + 1), freed(q))
                    sp_.wait_ge(routed, 1)
                    n_extra = sp_.value_load(meta[0:1, 0:1], min_val=0, max_val=MAX_EXTRA // 2)
                    with sp_.If(n_extra > 0):
                        with sp_.Fori(0, n_extra) as q:
                            e = [sp_.value_load(eidi[0:1, bass.ds(q * 2 + i, 1)], min_val=0, max_val=N_EXP - 1)
                                 for i in range(2)]
                            pair(e, freed(q + N_EXP // 2))
                    with sp_.Else():
                        sp_.nop()
                    with sp_.If(l < L - 1):
                        following = nc.s_assert_within(
                            l + 1, 1, L - 1, skip_runtime_bounds_check_because="this is the branch l < L - 1")
                        for slot, (s, v) in zip(MOE_SLOT, freed(n_extra + N_EXP // 2)):
                            sp_.wait_ge(s, v)
                            load_early(sp_, following, slot)
                    with sp_.Else():
                        sp_.nop()
                    sp_.nop()

                @block.gpsimd
                def _(pool):
                    nc.gpsimd.memset(lruw[:, :, :], 0.0).then_inc(lruw_zero, 1)

                @block.tensor
                def _(pe):
                    mm = nc.tensor.matmul
                    tr = nc.tensor.transpose

                    def norm(i, bank):
                        pe.wait_ge(sq_rdy[i], 1)
                        for k in range(KC):
                            last = mm(ps[:, bank, 0:NT], ones, sq[:, k, :], start=k == 0, stop=k == KC - 1)
                        last.then_inc(nrm_mm[i], 1)

                    norm(0, 7)
                    def ada_products(r, bank):
                        slots = [arrived(pe, S_ADA[r] + j) for j in range(4)]
                        for k in range(KC):
                            for j in range(4):
                                last = mm(ps[32 * j:32 * j + 32, bank, :], cT[:, k, :],
                                          slots[j][:, k * 512:(k + 1) * 512], start=k == 0, stop=k == KC - 1)
                        last.then_inc(ada_mm, 1)

                    def ada_transposes(r, bank):
                        pe.wait_ge(ada_sb, r + 1)
                        for b in range(4):
                            last = tr(ps[:, bank, b * P:(b + 1) * P], msb[r][:, b * P:(b + 1) * P], ident)
                        last.then_inc(ada_tr, 1)

                    ada_products(0, 0)
                    ada_transposes(0, 3)

                    def lru_products(d):
                        for i in range(8 * d, 8 * d + 8):
                            if d and i % 2 == 0:
                                pe.wait_ge(lg_ev, i - 6)
                            mm(ps[:, 2 + (i % 8) // 2, (i % 2) * NT:(i % 2 + 1) * NT], lruw[:, i, :],
                               xr[:, i % 4, :], start=True, stop=True).then_inc(lg_mm, 1)

                    def latent_products():
                        pe.wait_ge(win_a, 2)
                        pe.wait_ge(mla_n, 1)
                        for b in range(3):
                            for g in range(G):
                                last = tr(ps[:, b // 2, (b % 2) * NT + g * P:(b % 2) * NT + (g + 1) * P],
                                          projm[:, g, b * P:(b + 1) * P], ident)
                            last.then_inc(p3_mm, 1)
                        pe.wait_ge(ld_ckv, 16)
                        for b in range(2):
                            for s in range(3):
                                src = c_ckv[:, b * P:(b + 1) * P] if s == 1 else \
                                    projm[:, s // 2, OFF_KVA + b * P:OFF_KVA + (b + 1) * P]
                                last = tr(ps[:, 6 + b, s * P:(s + 1) * P], src, ident)
                            last.then_inc(p3_mm, 1)
                        pe.wait_ge(conv_rdy, 1)
                        pe.wait_ge(ld_lruw, 32)
                        lru_products(0)
                        for v in range(10):
                            if v == 0:
                                pe.wait_ge(p3_ev, 5)
                                slot = arrived(pe, S_QB)[:, 0:3 * 768].rearrange("p (k n) -> p k n", n=768)
                            if v == 4:
                                slot = arrived(pe, S_KVB)[:, 0:2048].rearrange("p (k n) -> p k n", n=1024)
                            if v >= 2:
                                pe.wait_ge(p4_ev, v - 1)
                            half = v % 2
                            if v < 4:
                                for k in range(3):
                                    last = mm(ps[:, half, 0:384], qaT[:, k, (v // 2) * P:(v // 2 + 1) * P],
                                              slot[:, k, half * 384:(half + 1) * 384], start=k == 0, stop=k == 2)
                            else:
                                s = v // 2 - 2
                                for k in range(2):
                                    last = mm(ps[:, half, :], ckvT[:, k, s * P:(s + 1) * P],
                                              slot[:, k, half * 512:(half + 1) * 512], start=k == 0, stop=k == 1)
                            last.then_inc(p4_mm, 1)

                    u = 0
                    for n, (kind, w) in enumerate((("tok", 512), ("tok", 160), ("feat", 512), ("feat", 512),
                                                   ("tok", 512), ("tok", 512), ("tok", 512))):
                        if n == 4:
                            latent_products()
                        slot = arrived(pe, S_IN[n])[:, 0:KC * w].rearrange("p (k n) -> p k n", n=w)
                        for half in range(2):
                            bank = u if u < 6 else u % 2
                            if 6 <= u < 8:
                                pe.wait_ge(win_v, u - 5)
                            elif u >= 8:
                                pe.wait_ge(p4_ev, min(u + 1, 10))
                                if u >= 10:
                                    pe.wait_ge(win_a, u - 7)
                            if kind == "tok":
                                for k in range(KC):
                                    if u == 0:
                                        pe.wait_ge(h_v[0], k + 1)
                                    if u == 1:
                                        pe.wait_ge(h_a[0], k + 1)
                                    last = mm(ps[:, bank, 0:w], hT[:, k, half * P:(half + 1) * P],
                                              slot[:, k, :], start=k == 0, stop=k == KC - 1)
                            else:
                                for c in range(2):
                                    for k in range(KC):
                                        ch = 2 * half + c
                                        last = mm(ps[:, bank, c * NT:(c + 1) * NT],
                                                  slot[:, k, ch * P:(ch + 1) * P], hT[:, k, :],
                                                  start=k == 0, stop=k == KC - 1)
                            last.then_inc(win_mm, 1)
                            u += 1
                            if u == 10:
                                lru_products(1)

                    done = [0]

                    def merge(n):
                        for _ in range(n):
                            f = done[0]
                            done[0] += 1
                            kind, b, ch = MERGE[f]
                            if f >= 2:
                                merge_evac(pe, f)
                            out = merge_ps(f)
                            slot = arrived(pe, merge_slot(kind, b, ch))
                            if kind == "proj":
                                slot = slot.rearrange("p (k n) -> p k n", n=D)
                                cols = slice(ch * P, (ch + 1) * P)
                                if ch == 0:
                                    pe.wait_ge(*{1: (lru_rdy, 1), 0: (om_ev, 4), 2: (od_ev, 4)}[b])
                                src, nk = {1: gel, 0: omla, 2: odif}[b], 4
                            else:
                                slot = slot.rearrange("p (k n) -> p k n", n=512)
                                cols = slice((ch % 4) * P, (ch % 4 + 1) * P)
                                src, nk = (merged if kind == "out" else hT), KC
                                if kind == "out" and ch == 0:
                                    pe.wait_ge(f_dv, 24)
                            for k in range(nk):
                                last = mm(out, slot[:, k, cols], src[:, k, :], start=k == 0, stop=k == nk - 1)
                            last.then_inc(f_mm, 1)

                    pe.wait_ge(p3_ev, 5)
                    merge(8)
                    pe.wait_ge(win_a, 8)
                    ada_products(1, 0)
                    ada_transposes(1, 1)
                    merge(1)

                    def qk_transposes(u):
                        if u == 0:
                            pe.wait_ge(mod_rdy, 2)
                            pe.wait_ge(qn_rdy, 2)
                            pe.wait_ge(kn_rdy, 3)
                        if u == 8:
                            pe.wait_ge(dn_rdy, 4)
                            pe.wait_ge(ld_dk, 16)
                        if u < 8:
                            rows_, srcs = QK, [q_tok[:, 0, u, :], q_tok[:, 1, u, :]] + \
                                [k_tok[:, s, u, :] for s in range(3)]
                        else:
                            c = slice((u - 8) * P, (u - 7) * P)
                            rows_, srcs = P, [projd[:, 0, 0, c], projd[:, 0, 1, c], projd[:, 1, 0, c],
                                              c_dk[:, c], projd[:, 1, 1, c]]
                        for n in range(3):
                            last = tr(ps[0:rows_, 0, n * P:(n + 1) * P], srcs[n], ident)
                        last.then_inc(t_mm, 1)
                        for n in range(2):
                            last = tr(ps[0:rows_, 1, n * P:(n + 1) * P], srcs[3 + n], ident)
                        last.then_inc(t_mm, 1)

                    def odif_transposes(u):
                        pe.wait_ge(on_v, u - 7)
                        for g in range(G):
                            last = tr(ps[:, 5, NT + g * P:NT + (g + 1) * P], on[:, g, :], ident)
                        last.then_inc(ot_mm, 1)

                    qk_transposes(0)
                    for u in range(12):
                        b = qkT[u % 2]
                        pe.wait_ge(qk_v, u + 1)
                        pe.wait_ge(qk_a, u + 1)
                        if u == 0:
                            pe.wait_ge(lg_ev, 16)
                        if u >= 2:
                            pe.wait_ge(ex_a, u if u >= 8 else u - 1)
                        if u < 8:
                            bank = 2 + u % 2
                            mm(ps[:, bank, 0:128], b[0:QK, 0:128], b[0:QK, 256:384], start=True, stop=True)
                            mm(ps[:, bank, 128:384], b[0:QK, 128:256], b[0:QK, 384:640], start=True,
                               stop=True).then_inc(s_mm, 1)
                        else:
                            for c in range(2):
                                r = slice(64 * c, 64 * c + 64)
                                mm(ps[:, 2 + c, 0:128], b[r, 0:128], b[r, 256:384], start=True, stop=True)
                            for c in range(2):
                                r = slice(64 * c, 64 * c + 64)
                                last = mm(ps[:, 2 + c, 128:384], b[r, 128:256], b[r, 384:640], start=True,
                                          stop=True)
                            last.then_inc(s_mm, 1)
                        if u < 11:
                            qk_transposes(u + 1)
                        merge(1 if u < 8 else 2)
                        pe.wait_ge(pn_v, u + 1)
                        if u >= 1:
                            pe.wait_ge(ptc, u)
                        for n in range(3):
                            last = tr(ps[:, 4, n * P:(n + 1) * P], probs[u % 2][:, 0, n * P:(n + 1) * P], ident)
                        last.then_inc(pt_mm, 1)
                        if u > 8:
                            odif_transposes(u - 1)
                        if u != 7:
                            merge(1)
                        pe.wait_ge(ptc, u + 1)
                        t = probsT[u % 2]
                        if u < 8:
                            if u % 2 == 0 and u:
                                pe.wait_ge(om_ev, u // 2)
                            r = slice(64 * (u % 2), 64 * (u % 2) + 64)
                            c = slice(u * VD, (u + 1) * VD)
                            mm(ps[r, 5, 0:P], v_tok[:, 0, c], t[:, 0:P], start=True, stop=True)
                            mm(ps[r, 5, P:NT], v_tok[:, 1, c], t[:, P:2 * P], start=True, stop=False)
                            mm(ps[r, 5, P:NT], v_tok[:, 2, c], t[:, 2 * P:3 * P], start=False,
                               stop=True).then_inc(pv_mm, 1)
                        else:
                            if u == 8:
                                pe.wait_ge(om_ev, 4)
                                pe.wait_ge(ld_dv, 16)
                            else:
                                pe.wait_ge(od_ev, u - 8)
                            c = slice((u - 8) * P, (u - 7) * P)
                            mm(ps[:, 5, 0:P], t[:, 0:P], projd[:, 2, 0, c], start=True, stop=True)
                            mm(ps[:, 5, P:NT], t[:, P:2 * P], c_dv[:, c], start=True, stop=False)
                            mm(ps[:, 5, P:NT], t[:, 2 * P:3 * P], projd[:, 2, 1, c], start=False,
                               stop=True).then_inc(pv_mm, 1)
                            merge(1)
                    ada_products(2, 0)
                    odif_transposes(11)
                    merge(8)
                    ada_transposes(2, 1)
                    merge(8)

                    norm(1, 0)
                    pe.wait_ge(h_v[1], 8)
                    pe.wait_ge(h_a[1], 8)
                    pe.wait_ge(ld_rw, 16)
                    for g in range(G):
                        for k in range(KC):
                            last = mm(ps[:, 1, g * N_EXP:(g + 1) * N_EXP], hT[:, k, g * P:(g + 1) * P],
                                      rw[:, k, :], start=k == 0, stop=k == KC - 1)
                    last.then_inc(rt_mm, 1)
                    for n in range(4):
                        for j in range(4):
                            k = (n % 2) * 4 + j
                            last = tr(ps[:, 2 + n, j * P:(j + 1) * P], hT[:, k, (n // 2) * P:(n // 2 + 1) * P],
                                      ident)
                        last.then_inc(x2_mm, 1)
                    pe.wait_ge(msk_v, 1)
                    mm(ps[:, 1, 64:96], ustrict, msk[:, 0, :], start=True, stop=True)
                    mm(ps[:, 1, 96:128], ones, msk[:, 0, :], start=True, stop=False)
                    mm(ps[:, 1, 96:128], ustrict, msk[:, 1, :], start=False, stop=True)
                    mm(ps[:, 1, 128:160], ones, msk[:, 0, :], start=True, stop=False)
                    mm(ps[:, 1, 128:160], ones, msk[:, 1, :], start=False, stop=True).then_inc(pos_mm, 1)
                    pe.wait_ge(cmb_v, 1)
                    for g in range(G):
                        last = mm(ps[0:N_EXP, 0, g * P:(g + 1) * P], cmb[:, g, :], ident, start=True, stop=True)
                    last.then_inc(ct_mm, 1)
                    pe.wait_ge(ct_ev, 1)
                    pe.wait_ge(ld_b2, 16)
                    pe.wait_ge(x2_ev, 4)
                    for k in range(KC):
                        mm(ps[:, 4 + k // 2, (k % 2) * NT:(k % 2 + 1) * NT], b2[0:N_EXP, k * P:(k + 1) * P],
                           ctT[0:N_EXP, :], start=k % 2 == 0, stop=True, skip_group_check=True)

                    def gather():
                        for h in range(2):
                            for g in range(G):
                                last = mm(ps[:, 2 + h, :], S_s[:, g, :], X2[:, g, h * 512:(h + 1) * 512],
                                          start=g == 0, stop=g == 1)
                            last.then_inc(ga_mm, 1)

                    def token_transposes(h):
                        for b in range(4 * h, 4 * h + 4):
                            last = tr(ps[:, 2 + h, (b % 4) * P:(b % 4 + 1) * P], Xg[:, b * P:(b + 1) * P], ident)
                        last.then_inc(xt_mm, 1)

                    def biases():
                        for h in range(2):
                            mm(ps[:, h, :], oh[0:N_EXP, :], b1[0:N_EXP, h * 512:(h + 1) * 512], start=True,
                               stop=True, skip_group_check=True)

                    pe.wait_ge(disp, 1)
                    gather()
                    pe.wait_ge(ld_b1, 16)
                    biases()
                    for h in range(2):
                        pe.wait_ge(xg_ev, h + 1)
                        token_transposes(h)
                    pe.wait_ge(xt_a, 1)
                    pe.wait_ge(xt_v, 1)
                    pe.wait_ge(routed, 1)
                    pairs = pe.value_load(meta[0:1, 1:2], min_val=N_EXP // 2, max_val=(N_EXP + MAX_EXTRA) // 2)
                    with pe.Fori(0, pairs) as q:
                        for part in range(2):
                            w = []
                            for i in range(2):
                                s = MOE_SLOT[2 * part + i]
                                pe.wait_ge(arr[s], q * 16 + 16 * (later_uses(s) + 1))
                                w.append(ring[:, s, :].rearrange("p (k n) -> p k n", k=4))
                            for k in range(4):
                                for h in range(2):
                                    for i in range(2):
                                        c = slice(64 * i, 64 * i + 64)
                                        last = mm(ps[c, h, :], xTg[:, 4 * part + k, c],
                                                  w[i][:, k, h * 512:(h + 1) * 512], start=False,
                                                  stop=True, skip_group_check=True)
                            last.then_inc(g1_mm, 1)
                        pe.wait_ge(disp, q + 2)
                        gather()
                        pe.wait_ge(act_v, q + 1)
                        for b in range(4):
                            last = tr(ps[:, 0, b * P:(b + 1) * P], act_s[:, b * P:(b + 1) * P], ident)
                        last.then_inc(at_mm, 1)
                        for g in range(G):
                            last = tr(ps[:, 1, g * P:(g + 1) * P], SC_s[:, g, :], ident)
                        last.then_inc(sct_mm, 1)
                        for h in range(2):
                            pe.wait_ge(xg_ev, q * 2 + (3 + h))
                            token_transposes(h)
                        w = []
                        for i in range(2):
                            s = MOE_SLOT[4 + i]
                            pe.wait_ge(arr[s], q * 16 + 16 * (later_uses(s) + 1))
                            w.append(ring[:, s, :].rearrange("p (f n) -> p f n", f=4))
                        pe.wait_ge(at_ev, q + 1)
                        for h in range(2):
                            pe.wait_ge((xt_a, xt_v)[h], q + 2)
                            for f in range(4):
                                for i in range(2):
                                    c = slice(64 * i, 64 * i + 64)
                                    last = mm(ps[c, 2 + h, :], actT[:, f, c], w[i][:, f, h * 512:(h + 1) * 512],
                                              start=f == 0, stop=f == 3)
                            last.then_inc(g2_mm, 1)
                        pe.wait_ge(sct_ev, q + 1)
                        biases()
                        for k in range(KC):
                            if k % 4 == 0:
                                pe.wait_ge((o_a, o_v)[k // 4], q + 1)
                            last = mm(ps[:, 4 + k // 2, (k % 2) * NT:(k % 2 + 1) * NT],
                                      O_s[:, k * P:(k + 1) * P], SCT[:, :], start=False, stop=True,
                                      skip_group_check=True)
                        last.then_inc(sc_mm, 1)

                @block.scalar
                def _(act):
                    A = nc.scalar.activation
                    a_n = [0]

                    def link(ins):
                        a_n[0] += 1
                        ins.then_inc(a_step, 1)
                        act.wait_ge(a_step, a_n[0])

                    def root_mean_square(i, bank):
                        A(sq[:, :, :], xT[:, :, :], ACT.Square).then_inc(sq_rdy[i], 1)
                        act.wait_ge(nrm_mm[i], 1)
                        A(rs[:, :], ps[:, bank, 0:NT], ACT.Sqrt, bias=cst[:, C_EPS:C_EPS + 1],
                          scale=1.0 / D).then_inc(nrm_sq[i], 1)

                    act.dma_start(vec[:, :], vecs[bass.ds(l, 1), :, :].rearrange("o p n -> (o p) n")).then_inc(
                        ld_vec, 16)
                    act.dma_start(row[:, :], rows[bass.ds(l, 1), :].broadcast_to((P, NR))).then_inc(ld_row, 16)

                    def cache(dst, src, s):
                        act.dma_start(dst, src[bass.ds(l, 1), :, :].rearrange("o p n -> (o p) n")).then_inc(s, 16)

                    def store(dst, src):
                        act.dma_start(dst[bass.ds(l, 1), :, :].rearrange("o p n -> (o p) n"), src).then_inc(
                            out_done, 16)

                    root_mean_square(0, 7)
                    act.wait_ge(lruw_zero, 1)
                    for j in range(2):
                        src = lru_gate_w[bass.ds(l, 1), bass.ds(j, 16, step=2), :, :]
                        act.dma_start(lruw[64 * j:64 * j + 64, :, 64 * j:64 * j + 64],
                                      src.rearrange("o b c e -> c (o b) e")).then_inc(ld_lruw, 16)
                    cache(c_ckv[:, :], cache_ckv, ld_ckv)
                    cache(c_kr[:, :], cache_krope, ld_kr)
                    cache(c_dk[:, :], cache_dk, ld_dk)
                    cache(c_dv[:, :], cache_dv, ld_dv)
                    act.dma_start(rw[:, :, :], router_w[bass.ds(l, 1), :, :].rearrange(
                        "o (k p) n -> p (o k) n", p=P)).then_inc(ld_rw, 16)
                    act.wait_ge(sp_abs, 1)
                    link(A(sp[:, 8:16], sp[:, 0:8], ACT.Exp, scale=-1.0))
                    A(sp[:, 16:24], sp[:, 8:16], ACT.Ln, bias=one_col).then_inc(sp_ln, 1)

                    def modulate(i, scale, shift):
                        act.wait_ge(hraw[i], 1)
                        act.wait_ge(mod_rdy, 1 + 2 * i)
                        for k in range(KC):
                            A(hT[:, k, P:NT], hT[:, k, P:NT], ACT.Identity, bias=modT[:, shift + k, 1:2],
                              scale=scale[:, k, 1:2]).then_inc(h_a[i], 1)

                    modulate(0, A1, 0)

                    def win_evac(u):
                        act.wait_ge(win_mm, u + 1)
                        if u < 8:
                            A(gel[:, 2 * (u - 6):2 * (u - 6) + 2, :],
                              ps[:, u % 2, :].rearrange("p (c n) -> p c n", c=2),
                              ACT.Gelu_apprx_tanh).then_inc(win_a, 1)
                        else:
                            A(projd[:, (u - 8) // 2, u % 2, :], ps[:, u % 2, :], ACT.Copy).then_inc(win_a, 1)

                    def lru_tanh(i):
                        act.wait_ge(lg_mm, i // 2 * 2 + 2)
                        dst = lru_t if i % 8 < 4 else lru_h[i // 8]
                        A(dst[:, i % 4, :], ps[:, 2 + (i % 8) // 2, (i % 2) * NT:(i % 2 + 1) * NT], ACT.Tanh,
                          bias=gbh[:, i:i + 1], scale=0.5).then_inc(lg_ev, 1)

                    def lru_decay(d):
                        act.wait_ge(lg_ev, 8 * d + 4)
                        for c in range(RC):
                            z = clh[:, 4 * d + c:4 * d + c + 1]
                            last = A(lru_a[:, c, :], lru_t[:, c, :], ACT.Exp, bias=z, scale=z)
                        link(last)
                        for c in range(RC):
                            z = clh[:, 4 * d + c:4 * d + c + 1]
                            A(lru_t[:, c, :], lru_t[:, c, :], ACT.Tanh, bias=z, scale=z).then_inc(lru_at, 1)

                    def lru_roots(d):
                        for half in range(2):
                            c = slice(2 * half, 2 * half + 2)
                            act.wait_ge(lru_w, 2 * d + half + 1)
                            A(lru_t[:, c, :], lru_t[:, c, :], ACT.Sqrt).then_inc(lru_sq, 1)

                    act.wait_ge(prep, 2)
                    A(lam[:, 4:6], lam[:, 0:2], ACT.Exp).then_inc(lam_exp, 1)
                    for u in (6, 7):
                        win_evac(u)
                    for v in range(10):
                        act.wait_ge(p4_mm, v + 1)
                        half = v % 2
                        if v < 4:
                            A(q_tok[:, v // 2, 4 * half:4 * half + 4, :],
                              ps[:, half, 0:384].rearrange("p (h n) -> p h n", h=4), ACT.Copy).then_inc(p4_ev, 1)
                        else:
                            s = v // 2 - 2
                            src = ps[:, half, :].rearrange("p (h n) -> p h n", h=4)
                            A(k_tok[:, s, 4 * half:4 * half + 4, 0:NOPE], src[:, :, 0:NOPE], ACT.Copy)
                            A(v_tok[:, s, 256 * half:256 * half + 256].rearrange("p (h n) -> p h n", h=4),
                              src[:, :, NOPE:128], ACT.Copy).then_inc(p4_ev, 1)
                        if v < 8:
                            lru_tanh(v)
                    lru_decay(0)
                    act.wait_ge(mla_n, 1)
                    store(new_ckv, projm[:, 0, OFF_KVA:OFF_KVA + KV_LORA])
                    store(new_krope, projm[:, 0, OFF_KVA + KV_LORA:M_COLS])
                    win_evac(8)
                    win_evac(9)
                    lru_roots(0)
                    win_evac(10)
                    act.wait_ge(lru_fr, 1)
                    for i in range(8, 16):
                        lru_tanh(i)
                    lru_decay(1)
                    win_evac(11)
                    lru_roots(1)
                    win_evac(12)
                    win_evac(13)
                    act.wait_ge(win_a, 7)
                    store(new_dv, projd[:, 2, 0, :])

                    done = [0]

                    def merge_gates(n):
                        for _ in range(n):
                            j = done[0]
                            done[0] += 1
                            b, ch = BRANCHES[j // 8], j % 8
                            f = MERGE.index(("gate", b, ch))
                            act.wait_ge(f_mm, f + 1)
                            if j >= 8:
                                act.wait_ge(f_dv, j - 8 + 1)
                            A(tg[:, ch, :], merge_ps(f), ACT.Tanh, bias=bmh[:, 8 * b + ch:8 * b + ch + 1],
                              scale=0.5).then_inc(f_ac, 1)

                    def modulation(r, bank):
                        act.wait_ge(ada_mm, r + 1)
                        A(msb[r], ps[:, bank, :], ACT.Copy).then_inc(ada_sb, 1)

                    merge_gates(8)
                    modulation(1, 0)
                    act.wait_ge(lru_rdy, 1)
                    store(new_lru, fin[:, :])
                    act.wait_ge(dn_rdy, 3)
                    store(new_dk, projd[:, 1, 0, :])

                    def qk_copy(u):
                        n = QK if u < 8 else P
                        act.wait_ge(t_mm, 2 * u + 2)
                        A(qkT[u % 2][0:n, 384:640], ps[0:n, 1, 0:256], ACT.Copy).then_inc(qk_a, 1)

                    def odif_evac(u):
                        act.wait_ge(ot_mm, u - 7)
                        A(odif[:, u - 8, :], ps[:, 5, NT:2 * NT], ACT.Copy, scale=subg[:, 0:1]).then_inc(od_ev, 1)

                    qk_copy(0)
                    for u in range(12):
                        act.wait_ge(nm_v, u + 1)
                        j = u % 2
                        if u < 8:
                            for n, c in enumerate((slice(0, 128), slice(128, 384))):
                                last = A(probs[j][:, 0, c], ps[:, 2 + j, c], ACT.Exp, bias=nm[:, j, n:n + 1],
                                         accum_out=sums[:, j, n:n + 1])
                        else:
                            for n, c in enumerate((slice(0, 128), slice(128, 384))):
                                for m in range(2):
                                    e = 2 * n + m
                                    last = A(probs[j][:, m, c], ps[:, 2 + m, c], ACT.Exp, bias=nm[:, j, e:e + 1],
                                             accum_out=sums[:, j, e:e + 1])
                        last.then_inc(ex_a, 1)
                        if u < 11:
                            qk_copy(u + 1)
                        merge_gates(1)
                        act.wait_ge(pt_mm, u + 1)
                        A(probsT[j], ps[:, 4, 0:384], ACT.Copy).then_inc(ptc, 1)
                        if u > 8:
                            odif_evac(u - 1)
                        if u >= 8:
                            merge_gates(1)
                    modulation(2, 0)
                    odif_evac(11)

                    act.wait_ge(pv_mm, 12)
                    act.wait_ge(out_done, 16 * 5)
                    cache(b1[0:N_EXP, :], exp_b1, ld_b1)
                    cache(b2[0:N_EXP, :], exp_b2, ld_b2)
                    act.wait_ge(f_dv, 32)
                    root_mean_square(1, 0)
                    modulate(1, A2, 24)
                    for n in range(4):
                        act.wait_ge(x2_mm, n + 1)
                        A(X2[:, n // 2, (n % 2) * 512:(n % 2 + 1) * 512], ps[:, 2 + n, :],
                          ACT.Copy).then_inc(x2_ev, 1)
                    act.wait_ge(nv_v, 1)
                    for g in range(G):
                        last = A(exl[:, g, :], lgt[:, g, :], ACT.Exp, bias=nv1[:, g:g + 1])
                    last.then_inc(exl_a, 1)
                    act.wait_ge(ct_mm, 1)
                    A(ctT[0:N_EXP, :], ps[0:N_EXP, 0, 0:NT], ACT.Copy).then_inc(ct_ev, 1)

                    def gathered(n):
                        for h in range(2):
                            act.wait_ge(ga_mm, n + (h + 1))
                            A(Xg[:, h * 512:(h + 1) * 512], ps[:, 2 + h, :], ACT.Copy).then_inc(xg_ev, 1)

                    def transposed(n):
                        act.wait_ge(xt_mm, n + 1)
                        A(xTg[:, 0:4, :], ps[:, 2, :].rearrange("p (a b) -> p a b", a=4), ACT.Copy).then_inc(xt_a, 1)

                    gathered(0)
                    transposed(0)
                    act.wait_ge(routed, 1)
                    pairs = act.value_load(meta[0:1, 1:2], min_val=N_EXP // 2, max_val=(N_EXP + MAX_EXTRA) // 2)
                    with act.Fori(0, pairs) as q:
                        act.wait_ge(gate_v, q + 1)
                        A(sig_s, gate_s, ACT.Sigmoid, scale=ALPHA).then_inc(sig_a, 1)
                        gathered(q * 2 + 2)
                        act.wait_ge(sct_mm, q + 1)
                        A(SCT[:, :], ps[:, 1, 0:NT], ACT.Copy).then_inc(sct_ev, 1)
                        transposed(q * 2 + 2)
                        act.wait_ge(g2_mm, q * 2 + 1)
                        A(O_s[:, 0:512], ps[:, 2, :], ACT.Copy).then_inc(o_a, 1)

                @block.vector
                def _(dve):
                    V = nc.vector
                    v_n = [0]

                    def link(ins):
                        v_n[0] += 1
                        ins.then_inc(v_step, 1)
                        dve.wait_ge(v_step, v_n[0])

                    dve.wait_ge(ld_vec, 16)
                    lmb = vec[:, V_LAM:V_LAM + 8]
                    V.scalar_tensor_tensor(out=sp[:, 0:8], in0=lmb, scalar=-1.0, in1=lmb, op0=ALU.mult,
                                           op1=ALU.max).then_inc(sp_abs, 1)

                    def normalise(i):
                        dve.wait_ge(nrm_sq[i], 1)
                        link(V.reciprocal(rs[:, :], rs[:, :]))
                        V.tensor_tensor(hT[:, :, :], xT[:, :, :], rs[:, None, :].broadcast_to((P, KC, NT)),
                                        ALU.mult).then_inc(hraw[i], 1)

                    normalise(0)

                    def rsqrt(x):
                        n = x.shape[1]
                        y, t = nwt[:, 0, 0:n], nwt[:, 1, 0:n]
                        link(V.tensor_scalar(y.bitcast(I32), x.bitcast(I32), 1, None, ALU.logical_shift_right))
                        link(V.tensor_scalar(y.bitcast(I32), y.bitcast(I32), -1.0, float(0x5f3759df), ALU.mult,
                                             ALU.add))
                        for it in range(4):
                            link(V.tensor_tensor(t, y, y, ALU.mult))
                            link(V.scalar_tensor_tensor(out=t, in0=t, scalar=-0.5, in1=x, op0=ALU.mult,
                                                        op1=ALU.mult))
                            link(V.scalar_tensor_tensor(out=y if it < 3 else x, in0=t, scalar=1.5, in1=y,
                                                        op0=ALU.add, op1=ALU.mult))

                    V.tensor_scalar(gbh[:, :], vec[:, V_GB:V_GB + 16], 0.5, None, ALU.mult)
                    V.tensor_scalar(bmh[:, :], vec[:, V_BM:V_BM + 24], 0.5, None, ALU.mult)
                    V.tensor_tensor(subg[:, :], vec[:, V_SUB:V_SUB + 1], vec[:, V_OML:V_OML + 1], ALU.mult)
                    link(V.tensor_scalar(sp[:, 24:32], vec[:, V_LAM:V_LAM + 8], -1.0, 0.0, ALU.mult, ALU.max))
                    dve.wait_ge(sp_ln, 1)
                    link(V.tensor_tensor(clh[:, :], sp[:, 24:32], sp[:, 16:24], ALU.add))
                    V.tensor_scalar(clh[:, :], clh[:, :], -4.0, None, ALU.mult).then_inc(prep, 1)
                    dve.wait_ge(ld_row, 16)
                    dl = row[:, R_DL:R_DL + 256].rearrange("p (a b n) -> p a b n", a=2, b=2)
                    link(V.tensor_tensor(lprod[:, :].rearrange("p (a n) -> p a n", a=2), dl[:, :, 0, :], dl[:, :, 1, :],
                                         ALU.mult))
                    V.tensor_reduce(lam[:, 0:2], lprod[:, :].rearrange("p (a n) -> p a n", a=2), AX_X,
                                    ALU.add).then_inc(prep, 1)

                    def modulation(r, bank):
                        dve.wait_ge(ada_tr, r + 1)
                        src = ps[:, bank, :].rearrange("p (b j z) -> p j b z", b=4, j=4)[:, :, :, 0:G]
                        dst = modT[:, 16 * r:16 * r + 16, :].rearrange("p (j b) z -> p j b z", j=4)
                        bias = vec[:, V_ADAB + 16 * r:V_ADAB + 16 * r + 16].rearrange("p (j b) -> p j b", j=4)
                        link(V.tensor_tensor(dst, src, bias[:, :, :, None].broadcast_to((P, 4, 4, G)), ALU.add))
                        if r == 1:
                            V.tensor_scalar(g1h[:, :, :], modT[:, 16:24, :], 0.5, None, ALU.mult).then_inc(mod_rdy, 1)
                        else:
                            out, sc, nrm = ((A1, 8, V_N1), None, (A2, 32, V_N2))[r]
                            V.scalar_tensor_tensor(out=out[:, :, :], in0=modT[:, sc:sc + 8, :], scalar=1.0,
                                                   in1=vec[:, nrm:nrm + 8][:, :, None].broadcast_to((P, KC, G)),
                                                   op0=ALU.add, op1=ALU.mult).then_inc(mod_rdy, 1)

                    dve.wait_ge(ada_mm, 1)
                    V.tensor_copy(msb[0], ps[:, 0, :]).then_inc(ada_sb, 1)
                    modulation(0, 3)

                    def modulate(i, scale, shift):
                        dve.wait_ge(mod_rdy, 1 + 2 * i)
                        dve.wait_ge(hraw[i], 1)
                        for k in range(KC):
                            V.tensor_scalar(hT[:, k, 0:P], hT[:, k, 0:P], scale[:, k, 0:1],
                                            modT[:, shift + k, 0:1], ALU.mult, ALU.add).then_inc(h_v[i], 1)

                    modulate(0, A1, 0)

                    for u in range(4):
                        dve.wait_ge(win_mm, u + 1)
                        c0, w = (0, 512) if u < 2 else (512, 160)
                        V.tensor_copy(projm[:, u % 2, c0:c0 + w], ps[:, u, 0:w]).then_inc(win_v, 1)
                    dve.wait_ge(win_v, 4)
                    spare = at(E0 + 2048, G, 640)
                    for g in range(G):
                        V.tensor_tensor_reduce(out=spare[:, g, 0:Q_LORA], in0=projm[:, g, 0:Q_LORA],
                                               in1=projm[:, g, 0:Q_LORA], scale=1.0, scalar=0.0, op0=ALU.mult,
                                               op1=ALU.add, accum_out=ss[:, g:g + 1])
                        kv = projm[:, g, OFF_KVA:OFF_KVA + KV_LORA]
                        last = V.tensor_tensor_reduce(out=spare[:, g, 384:640], in0=kv, in1=kv, scale=1.0, scalar=0.0,
                                                      op0=ALU.mult, op1=ALU.add, accum_out=ss[:, 2 + g:3 + g])
                    link(last)
                    V.tensor_scalar(ss[:, 0:2], ss[:, 0:2], 1.0 / Q_LORA, EPS, ALU.mult, ALU.add)
                    link(V.tensor_scalar(ss[:, 2:4], ss[:, 2:4], 1.0 / KV_LORA, EPS, ALU.mult, ALU.add))
                    rsqrt(ss[:, 0:4])
                    for g in range(G):
                        V.tensor_scalar(projm[:, g, 0:Q_LORA], projm[:, g, 0:Q_LORA], ss[:, g:g + 1], None,
                                        ALU.mult)
                        kv = projm[:, g, OFF_KVA:OFF_KVA + KV_LORA]
                        last = V.scalar_tensor_tensor(out=kv, in0=kv, scalar=ss[:, 2 + g:3 + g],
                                                      in1=row[:, R_KVA:R_KVA + KV_LORA], op0=ALU.mult, op1=ALU.mult)
                    last.then_inc(mla_n, 1)

                    V.memset(xpad[:, :, :, 0:2], 0.0)
                    V.memset(xpad[:, :, :, P + 2:P + 3], 0.0)
                    for u in (4, 5):
                        dve.wait_ge(win_mm, u + 1)
                        V.tensor_copy(xpad[:, 2 * (u - 4):2 * (u - 4) + 2, :, 2:P + 2],
                                      ps[:, u, :].rearrange("p (c g n) -> p c g n", c=2, g=G)).then_inc(win_v, 1)
                    dve.wait_ge(win_v, 6)
                    for j in range(4):
                        for c in range(RC):
                            w = vec[:, V_CW + 4 * j + c:V_CW + 4 * j + c + 1]
                            o = xr[:, c, :].rearrange("p (g n) -> p g n", g=G)
                            if j == 0:
                                last = V.tensor_scalar(o, xpad[:, c, :, 0:P], w, vec[:, V_CB + c:V_CB + c + 1],
                                                       ALU.mult, ALU.add)
                            else:
                                last = V.scalar_tensor_tensor(out=o, in0=xpad[:, c, :, j:j + P], scalar=w, in1=o,
                                                              op0=ALU.mult, op1=ALU.add)
                        if j < 3:
                            link(last)
                    last.then_inc(conv_rdy, 1)

                    for b in range(3):
                        dve.wait_ge(p3_mm, 2 if b < 2 else 3)
                        V.tensor_scalar(qaT[:, b, :], ps[:, b // 2, (b % 2) * NT:(b % 2 + 1) * NT],
                                        vec[:, V_QA + b:V_QA + b + 1], None, ALU.mult).then_inc(p3_ev, 1)
                    for b in range(2):
                        dve.wait_ge(p3_mm, 4 + b)
                        V.tensor_copy(ckvT[:, b, :], ps[:, 6 + b, 0:384]).then_inc(p3_ev, 1)

                    def rotate(x, n, w, cos, sin):
                        swapped = scratch[:, 0:n * 4 * w].rearrange("p (h a b c) -> p h a b c", h=n, a=2, b=2)
                        for b in range(2):
                            s = sin.rearrange("p (a b c) -> p a b c", a=2, b=2)[:, :, b, :]
                            last_ = V.tensor_tensor(swapped[:, :, :, b, :], x[:, :, :, 1 - b, :],
                                                    s[:, None, :, :].broadcast_to((P, n, 2, w)), ALU.mult)
                        link(last_)
                        flat = x.rearrange("p h a b c -> p h (a b c)")
                        link(V.tensor_tensor(flat, flat, cos[:, None, :].broadcast_to((P, n, 4 * w)), ALU.mult))
                        return V.tensor_tensor(flat, flat, swapped.rearrange("p h a b c -> p h (a b c)"), ALU.add)

                    def axes(x, w):
                        return x.rearrange("p h (a b c) -> p h a b c", a=2, b=2)

                    def squares(x, n, w, dst):
                        s2 = scratch[:, 0:n * w].rearrange("p (h n) -> p h n", h=n)
                        link(V.tensor_tensor(s2, x, x, ALU.mult))
                        link(V.tensor_reduce(dst, s2, AX_X, ALU.add))

                    def scaled(x, n, w, r, gain, factor):
                        link(V.tensor_tensor(x, x, r[:, :, None].broadcast_to((P, n, w)), ALU.mult))
                        return V.scalar_tensor_tensor(out=x, in0=x, scalar=factor,
                                                      in1=gain[:, None, :].broadcast_to((P, n, w)), op0=ALU.mult,
                                                      op1=ALU.mult)

                    cosm, sinm = cst[:, C_CM:C_CM + ROPE], cst[:, C_SM:C_SM + ROPE]
                    cosd, sind = cst[:, C_CD:C_CD + DH], cst[:, C_SD:C_SD + DH]
                    dve.wait_ge(p4_ev, 4)
                    for g in range(G):
                        squares(q_tok[:, g, :, :], MLA_H, QK, ss[:, 8 * g:8 * g + 8])
                    link(V.tensor_scalar(ss[:, 0:16], ss[:, 0:16], 1.0 / QK, EPS, ALU.mult, ALU.add))
                    rsqrt(ss[:, 0:16])
                    for g in range(G):
                        last = scaled(q_tok[:, g, :, :], MLA_H, QK, ss[:, 8 * g:8 * g + 8], row[:, R_QN:R_QN + QK],
                                      float(QK) ** -0.5)
                        if g == 1:
                            link(last)
                            last = rotate(axes(q_tok[:, 1, :, NOPE:QK], 8), MLA_H, 8, cosm, sinm)
                        last.then_inc(qn_rdy, 1)
                        dve.wait_ge(qn_rdy, g + 1)
                    dve.wait_ge(ld_kr, 16)
                    kr = (projm[:, 0, 640:M_COLS], c_kr[:, :], projm[:, 1, 640:M_COLS])
                    for s in range(3):
                        dve.wait_ge(p4_ev, 2 * s + 6)
                        V.tensor_tensor_reduce(out=scratch[:, 512:544], in0=kr[s], in1=kr[s], scale=1.0,
                                               scalar=0.0, op0=ALU.mult, op1=ALU.add, accum_out=krs[:, s:s + 1])
                        r8 = ss[:, 8 * s:8 * s + 8]
                        squares(k_tok[:, s, :, 0:NOPE], MLA_H, NOPE, r8)
                        link(V.tensor_scalar(r8, r8, krs[:, s:s + 1], 1.0 / QK, ALU.add, ALU.mult))
                        link(V.tensor_scalar(r8, r8, EPS, None, ALU.add))
                    rsqrt(ss[:, 0:24])
                    for s in range(3):
                        r8 = ss[:, 8 * s:8 * s + 8]
                        link(V.tensor_copy(k_tok[:, s, :, NOPE:QK],
                                      kr[s][:, None, :].broadcast_to((P, MLA_H, ROPE))))
                        last = scaled(k_tok[:, s, :, :], MLA_H, QK, r8, row[:, R_KN:R_KN + QK], 1.0)
                        if s == 2:
                            link(last)
                            last = rotate(axes(k_tok[:, 2, :, NOPE:QK], 8), MLA_H, 8, cosm, sinm)
                        last.then_inc(kn_rdy, 1)
                        dve.wait_ge(kn_rdy, s + 1)
                    dve.wait_ge(conv_rdy, 1)
                    for d in range(2):
                        h = lru_h[d]
                        for half in range(2):
                            c = slice(2 * half, 2 * half + 2)
                            dve.wait_ge(lru_at, 4 * d + 2 * half + 2)
                            V.scalar_tensor_tensor(out=h[:, c, :], in0=h[:, c, :], scalar=1.0, in1=xr[:, c, :],
                                                   op0=ALU.add, op1=ALU.mult)
                            link(V.tensor_tensor(lru_u[:, :, :], lru_a[:, c, :], lru_a[:, c, :], ALU.mult))
                            link(V.scalar_tensor_tensor(out=lru_u[:, :, :], in0=lru_u[:, :, :], scalar=1.0,
                                                        in1=lru_t[:, c, :], op0=ALU.add, op1=ALU.mult))
                            V.tensor_scalar(lru_t[:, c, :], lru_u[:, :, :], -0.25, 2.0 ** -116, ALU.mult,
                                            ALU.max).then_inc(lru_w, 1)
                            dve.wait_ge(lru_w, 2 * d + half + 1)
                        for half in range(2):
                            c = slice(2 * half, 2 * half + 2)
                            dve.wait_ge(lru_sq, 2 * d + half + 1)
                            link(V.tensor_tensor(h[:, c, :], h[:, c, :], lru_t[:, c, :], ALU.mult))
                            for ch in (2 * half, 2 * half + 1):
                                for g in range(G):
                                    init = 0.0 if g == 0 else vec[:, V_ST + 4 * d + ch:V_ST + 4 * d + ch + 1]
                                    lo, hi = g * P, (g + 1) * P
                                    if d == 0:
                                        aa, bb = lru_a[:, ch, lo:hi], h[:, ch, lo:hi]
                                    else:
                                        aa, bb = lru_a[:, ch, lo:hi][:, ::-1], h[:, ch, lo:hi][:, ::-1]
                                    last = V.tensor_tensor_scan(bb, aa, bb, init, ALU.mult, ALU.add)
                        last.then_inc(lru_fr, 1)
                    dve.wait_ge(lru_fr, 2)
                    V.tensor_copy(fin[:, 0:4], lru_h[0][:, :, P - 1])
                    V.tensor_copy(fin[:, 4:8], lru_h[1][:, :, 0])
                    link(V.tensor_tensor(xr[:, :, :], lru_h[0][:, :, :], lru_h[1][:, :, :], ALU.add))
                    V.tensor_tensor(gel[:, :, :], xr[:, :, :], gel[:, :, :], ALU.mult).then_inc(lru_rdy, 1)

                    dve.wait_ge(win_a, 8)
                    for n in range(4):
                        squares(projd[:, n // 2, n % 2, :].rearrange("p (h n) -> p h n", n=DH), 8, DH,
                                ss[:, 8 * n:8 * n + 8])
                    link(V.tensor_scalar(ss[:, :], ss[:, :], 1.0 / DH, EPS, ALU.mult, ALU.add))
                    rsqrt(ss[:, :])
                    for n in range(4):
                        x = projd[:, n // 2, n % 2, :].rearrange("p (h n) -> p h n", n=DH)
                        gain = row[:, R_DQN:R_DQN + DH] if n < 2 else row[:, R_DKN:R_DKN + DH]
                        last = scaled(x, 8, DH, ss[:, 8 * n:8 * n + 8], gain, float(DH) ** -0.5 if n < 2 else 1.0)
                        if n % 2:
                            link(last)
                            last = rotate(axes(x, 16), 8, 16, cosd, sind)
                        last.then_inc(dn_rdy, 1)
                        dve.wait_ge(dn_rdy, n + 1)
                    dve.wait_ge(lam_exp, 1)
                    link(V.tensor_tensor(lam[:, 6:7], lam[:, 5:6], lam[:, 4:5], ALU.subtract))
                    link(V.tensor_tensor(lam[:, 7:8], lam[:, 6:7], vec[:, V_LI:V_LI + 1], ALU.subtract))
                    nlam = lam[:, 7:8]

                    done = [0]

                    def merge(n):
                        for _ in range(n):
                            j = done[0]
                            done[0] += 1
                            ch = j % 8
                            if j < 24:
                                f = MERGE.index(("proj", BRANCHES[j // 8], ch))
                                dve.wait_ge(f_mm, f + 1)
                                dve.wait_ge(f_ac, j + 1)
                                if j < 8:
                                    V.scalar_tensor_tensor(out=merged[:, ch, :], in0=tg[:, ch, :], scalar=1.0,
                                                           in1=merge_ps(f), op0=ALU.add,
                                                           op1=ALU.mult).then_inc(f_dv, 1)
                                else:
                                    dve.wait_ge(f_dv, j)
                                    link(V.scalar_tensor_tensor(out=mtmp, in0=tg[:, ch, :], scalar=1.0,
                                                                in1=merge_ps(f), op0=ALU.add, op1=ALU.mult))
                                    V.tensor_tensor(merged[:, ch, :], merged[:, ch, :], mtmp,
                                                    ALU.add).then_inc(f_dv, 1)
                            else:
                                f = MERGE.index(("out", 0, ch))
                                dve.wait_ge(f_mm, f + 1)
                                for g in range(G):
                                    c = slice(g * P, (g + 1) * P)
                                    last = V.scalar_tensor_tensor(out=xT[:, ch, c], in0=merge_ps(f)[:, c],
                                                                  scalar=g1h[:, ch, g:g + 1], in1=xT[:, ch, c],
                                                                  op0=ALU.mult, op1=ALU.add)
                                last.then_inc(f_dv, 1)

                    modulation(1, 1)
                    dve.wait_ge(mod_rdy, 2)
                    merge(1)

                    def qk_copy(u):
                        n = QK if u < 8 else P
                        dve.wait_ge(t_mm, 2 * u + 1)
                        V.tensor_copy(qkT[u % 2][0:n, 0:384], ps[0:n, 0, 0:384]).then_inc(qk_v, 1)

                    qk_copy(0)
                    for u in range(12):
                        j = u % 2
                        dve.wait_ge(s_mm, u + 1)
                        if u < 8:
                            V.tensor_reduce(nm[:, j, 0:1], ps[:, 2 + j, 0:128], AX_X, ALU.max, negate=True)
                            V.tensor_reduce(nm[:, j, 1:2], ps[:, 2 + j, 128:384], AX_X, ALU.max,
                                            negate=True).then_inc(nm_v, 1)
                        else:
                            V.tensor_reduce(nm[:, j, 0:2], ps[:, 2:4, 0:128], AX_X, ALU.max, negate=True)
                            V.tensor_reduce(nm[:, j, 2:4], ps[:, 2:4, 128:384], AX_X, ALU.max,
                                            negate=True).then_inc(nm_v, 1)
                        if u < 11:
                            qk_copy(u + 1)
                        dve.wait_ge(ex_a, u + 1)
                        if u < 8:
                            link(V.reciprocal(rcp[:, j, 0:2], sums[:, j, 0:2]))
                            for n, c in enumerate((slice(0, 128), slice(128, 384))):
                                last = V.tensor_scalar(probs[j][:, 0, c], probs[j][:, 0, c], rcp[:, j, n:n + 1],
                                                       None, ALU.mult)
                        else:
                            link(V.reciprocal(rcp[:, j, :], sums[:, j, :]))
                            V.tensor_scalar(nl[:, :], rcp[:, j, :].rearrange("p (n m) -> p n m", m=2)[:, :, 1], nlam,
                                            None, ALU.mult)
                            for n, c in enumerate((slice(0, 128), slice(128, 384))):
                                last = V.tensor_scalar(probs[j][:, 0, c], probs[j][:, 0, c],
                                                       rcp[:, j, 2 * n:2 * n + 1], None, ALU.mult)
                            link(last)
                            for n, c in enumerate((slice(0, 128), slice(128, 384))):
                                last = V.scalar_tensor_tensor(out=probs[j][:, 0, c], in0=probs[j][:, 1, c],
                                                              scalar=nl[:, n:n + 1], in1=probs[j][:, 0, c],
                                                              op0=ALU.mult, op1=ALU.add)
                        last.then_inc(pn_v, 1)
                        if u != 7:
                            merge(1 if u < 7 else 2)
                        if u < 8 and u % 2:
                            dve.wait_ge(pv_mm, u + 1)
                            V.tensor_copy(omla[:, u // 2, :], ps[:, 5, 0:NT]).then_inc(om_ev, 1)
                        if u >= 8:
                            dve.wait_ge(pv_mm, u + 1)
                            if u > 8:
                                dve.wait_ge(ot_mm, u - 8)
                            link(V.tensor_copy(on[:, :, :], ps[:, 5, 0:NT].rearrange("p (g n) -> p g n", g=G)))
                            for g in range(G):
                                last = V.tensor_tensor_reduce(out=onsq[:, g, :], in0=on[:, g, :],
                                                              in1=on[:, g, :], scale=1.0, scalar=0.0, op0=ALU.mult,
                                                              op1=ALU.add, accum_out=ss[:, g:g + 1])
                            link(last)
                            link(V.tensor_scalar(ss[:, 0:2], ss[:, 0:2], 1.0 / DV, EPS, ALU.mult, ALU.add))
                            rsqrt(ss[:, 0:2])
                            for g in range(G):
                                last = V.tensor_scalar(on[:, g, :], on[:, g, :], ss[:, g:g + 1], None, ALU.mult)
                            last.then_inc(on_v, 1)
                    merge(8)
                    modulation(2, 1)
                    merge(8)

                    dve.wait_ge(f_dv, 32)
                    normalise(1)
                    modulate(1, A2, 24)

                    dve.wait_ge(rt_mm, 1)
                    rb = row[:, R_RB:R_RB + N_EXP]
                    link(V.tensor_tensor(lgt[:, :, :], ps[:, 1, 0:64].rearrange("p (g e) -> p g e", g=G),
                                         rb[:, None, :].broadcast_to((P, G, N_EXP)), ALU.add))
                    for g in range(G):
                        last = V.max(top8[:, g, :], lgt[:, g, :])
                    link(last)
                    V.tensor_scalar(nv1[:, :], top8[:, :, 0], -1.0, None, ALU.mult).then_inc(nv_v, 1)
                    link(V.memset(top8[:, :, TOP_K:8], -3e38))
                    for g in range(G):
                        last = V.match_replace(rep[:, g, :], top8[:, g, :], lgt[:, g, :], 3e38)
                    link(last)
                    V.tensor_tensor(msk[:, :, :], rep[:, :, :], lgt[:, :, :], ALU.not_equal).then_inc(msk_v, 1)
                    dve.wait_ge(msk_v, 1)
                    dve.wait_ge(exl_a, 1)
                    for g in range(G):
                        last = V.tensor_tensor_reduce(out=cmb[:, g, :], in0=exl[:, g, :], in1=msk[:, g, :], scale=1.0,
                                                      scalar=0.0, op0=ALU.mult, op1=ALU.add,
                                                      accum_out=den[:, g:g + 1])
                    link(last)
                    link(V.reciprocal(den[:, :], den[:, :]))
                    V.tensor_tensor(cmb[:, :, :], cmb[:, :, :], den[:, :, None].broadcast_to((P, G, N_EXP)),
                                    ALU.mult).then_inc(cmb_v, 1)

                    V.memset(pmT[:, :, :], -1.0)
                    V.memset(cwT[:, :, :], 0.0)
                    link(V.memset(eidf[:, :], 0.0))
                    dve.wait_ge(pos_mm, 1)
                    dve.wait_ge(cmb_v, 1)
                    V.tensor_copy(eidf[:, 0:N_EXP], cst[:, C_EIDX:C_EIDX + N_EXP])
                    V.tensor_copy(cwT[:, :, 0:N_EXP], cmb[:, :, :])
                    V.tensor_copy(cnt[:, :], ps[:, 1, 128:160])
                    link(V.scalar_tensor_tensor(out=pm1[:, :, :], in0=ps[:, 1, 64:128].rearrange(
                        "p (g e) -> p g e", g=G), scalar=1.0, in1=msk[:, :, :], op0=ALU.add, op1=ALU.mult))
                    link(V.tensor_scalar(pmT[:, :, 0:N_EXP], pm1[:, :, :], -1.0, None, ALU.add))

                    def tokens_onehot(t):
                        for i in range(2):
                            c = slice(SLOTS * i, SLOTS * (i + 1))
                            for g in range(G):
                                V.tensor_scalar(S_s[:, g, c], cst[:, C_IOTA:C_IOTA + SLOTS],
                                                pmT[:, g, bass.ds(t + i, 1)], None, ALU.is_equal)
                            last = V.tensor_scalar(oh[0:N_EXP, c],
                                                   cst[0:N_EXP, C_PIDX:C_PIDX + 1].broadcast_to((N_EXP, SLOTS)),
                                                   eidf[0:N_EXP, bass.ds(t + i, 1)], None, ALU.is_equal)
                        return last

                    def combine_onehot(t):
                        for i in range(2):
                            for g in range(G):
                                V.tensor_scalar(SC_s[:, g, SLOTS * i:SLOTS * (i + 1)],
                                                cst[:, C_IOTA:C_IOTA + SLOTS], pmT[:, g, bass.ds(t + i, 1)],
                                                cwT[:, g, bass.ds(t + i, 1)], ALU.is_equal, ALU.mult)

                    def transposed(n):
                        dve.wait_ge(xt_mm, n + 2)
                        V.tensor_copy(xTg[:, 4:8, :], ps[:, 3, :].rearrange("p (a b) -> p a b", a=4)).then_inc(xt_v, 1)

                    tokens_onehot(0).then_inc(disp, 1)
                    link(V.tensor_scalar(xtra[:, :], cnt[:, :], 64.5, None, ALU.is_gt))
                    for m in (128.5, 192.5):
                        link(V.scalar_tensor_tensor(out=xtra[:, :], in0=cnt[:, :], scalar=m, in1=xtra[:, :],
                                                    op0=ALU.is_gt, op1=ALU.add))
                    link(V.tensor_tensor_scan(tend[:, :], ones[:, 0:N_EXP], xtra[:, :], 0.0, ALU.mult, ALU.add))
                    link(V.tensor_tensor(tbeg[:, :], tend[:, :], xtra[:, :], ALU.subtract))
                    kk = cst[:, C_KK:C_KK + MAX_EXTRA][:, :, None].broadcast_to((P, MAX_EXTRA, N_EXP))

                    def over_e(v):
                        return v[:, None, :].broadcast_to((P, MAX_EXTRA, N_EXP))

                    V.tensor_tensor(sel[:, :, :], kk, over_e(tbeg), ALU.is_ge)
                    link(V.tensor_tensor(tmpx[:, :, :], kk, over_e(tend), ALU.is_lt))
                    link(V.tensor_tensor(sel[:, :, :], sel[:, :, :], tmpx[:, :, :], ALU.mult))
                    V.tensor_tensor(tmpx[:, :, :], sel[:, :, :], over_e(cst[:, C_EIDX:C_EIDX + N_EXP]), ALU.mult)
                    link(V.tensor_tensor(tmpy[:, :, :], kk, over_e(tbeg), ALU.subtract))
                    V.tensor_reduce(eidf[:, N_EXP:N_EXP + MAX_EXTRA], tmpx[:, :, :], AX_X, ALU.add)
                    link(V.scalar_tensor_tensor(out=tmpy[:, :, :], in0=tmpy[:, :, :], scalar=1.0, in1=sel[:, :, :],
                                                op0=ALU.add, op1=ALU.mult))
                    link(V.tensor_reduce(psub[:, :], tmpy[:, :, :], AX_X, ALU.add))
                    for g in range(G):
                        link(V.tensor_tensor(tmpx[:, :, :], sel[:, :, :], over_e(pm1[:, g, :]), ALU.mult))
                        link(V.tensor_tensor(tmpy[:, :, :], sel[:, :, :], over_e(cmb[:, g, :]), ALU.mult))
                        dst = pmT[:, g, N_EXP:N_EXP + MAX_EXTRA]
                        V.tensor_reduce(cwT[:, g, N_EXP:N_EXP + MAX_EXTRA], tmpy[:, :, :], AX_X, ALU.add)
                        link(V.tensor_reduce(dst, tmpx[:, :, :], AX_X, ALU.add))
                        link(V.scalar_tensor_tensor(out=dst, in0=psub[:, :], scalar=-float(SLOTS), in1=dst,
                                                    op0=ALU.mult, op1=ALU.add))
                        link(V.tensor_scalar(dst, dst, -1.0, None, ALU.add))
                    link(V.tensor_scalar(cmp8[:, :], cst[:, C_KK:C_KK + 8], 2.0, tend[:, N_EXP - 1:N_EXP], ALU.mult,
                                         ALU.is_lt))
                    link(V.tensor_reduce(npf[:, 0:1], cmp8[:, :], AX_X, ALU.add))
                    link(V.tensor_scalar(npf[:, 1:2], npf[:, 0:1], float(N_EXP // 2), None, ALU.add))
                    V.tensor_copy(eidi[:, :], eidf[:, N_EXP:N_EXP + MAX_EXTRA])
                    V.tensor_copy(meta[:, :], npf[:, :]).then_inc(routed, 1)

                    transposed(0)
                    dve.wait_ge(routed, 1)
                    pairs = dve.value_load(meta[0:1, 1:2], min_val=N_EXP // 2, max_val=(N_EXP + MAX_EXTRA) // 2)
                    with dve.Fori(0, pairs) as q:
                        dve.wait_ge(g1_mm, q * 2 + 1)
                        combine_onehot(q * 2)
                        tokens_onehot(q * 2 + 2).then_inc(disp, 1)
                        dve.wait_ge(g1_mm, q * 2 + 2)
                        V.tensor_scalar(gate_s, ps[:, 0, :], LIMIT, None, ALU.min).then_inc(gate_v, 1)
                        V.tensor_scalar(up_s, ps[:, 1, :], LIMIT, -LIMIT, ALU.min, ALU.max).then_inc(up_v, 1)
                        dve.wait_ge(up_v, q + 1)
                        V.scalar_tensor_tensor(out=up_s, in0=up_s, scalar=1.0, in1=gate_s, op0=ALU.add,
                                               op1=ALU.mult).then_inc(prod_v, 1)
                        dve.wait_ge(prod_v, q + 1)
                        dve.wait_ge(sig_a, q + 1)
                        V.tensor_tensor(act_s, up_s, sig_s, ALU.mult).then_inc(act_v, 1)
                        dve.wait_ge(at_mm, q + 1)
                        V.tensor_copy(actT.rearrange("p a b -> p (a b)"), ps[:, 0, :]).then_inc(at_ev, 1)
                        transposed(q * 2 + 2)
                        dve.wait_ge(g2_mm, q * 2 + 2)
                        V.tensor_copy(O_s[:, 512:1024], ps[:, 3, :]).then_inc(o_v, 1)
                    dve.wait_ge(sc_mm, pairs)
                    for k in range(KC):
                        for g in range(G):
                            c = slice(g * P, (g + 1) * P)
                            V.scalar_tensor_tensor(out=xT[:, k, c],
                                                   in0=ps[:, 4 + k // 2, (k % 2) * NT + g * P:(k % 2) * NT + (g + 1) * P],
                                                   scalar=modT[:, 40 + k, g:g + 1], in1=xT[:, k, c], op0=ALU.mult,
                                                   op1=ALU.add)
            for s in sems:
                nc.gpsimd.sem_clear(s)
            nc.all_engine_barrier()

        with nc.Block() as block:
            @block.sync
            def _(sp_):
                sp_.dma_start(y_out, xT[:, :, :]).then_inc(s_set[5], 16)
                sp_.wait_ge(s_set[5], 16)


def constants(np):
    c = np.zeros((P, NC), np.float32)
    c[:, C_ID:C_ID + P] = np.eye(P)
    c[:, C_UT:C_UT + P] = np.triu(np.ones((P, P)), 1)
    c[:, C_ONE:C_ONE + P] = 1.0
    c[:, C_IOTA:C_IOTA + P] = np.tile(np.arange(SLOTS), 2)
    for dim, cc, cs in ((ROPE, C_CM, C_SM), (DH, C_CD, C_SD)):
        half = dim // 2
        inv = (1.0 / (np.float32(10000.0) ** (np.arange(0, half, 2, dtype=np.float32) / np.float32(half))))
        inv = inv.astype(np.float32)
        t = np.arange(P)
        ang = [((pos.astype(np.float32))[:, None] * inv[None, :]).astype(np.float32) for pos in (t // 64, t % 64)]
        ang = np.concatenate([ang[0], ang[0], ang[1], ang[1]], axis=1)
        sign = np.tile(np.repeat([-1.0, 1.0], half // 2), 2)
        c[:, cc:cc + dim] = np.cos(ang)
        c[:, cs:cs + dim] = np.sin(ang) * sign
    c[:, C_PIDX] = np.arange(P)
    c[:, C_EPS] = EPS
    c[:, C_KK:C_KK + MAX_EXTRA] = np.arange(MAX_EXTRA)
    c[:, C_EIDX:C_EIDX + N_EXP] = np.arange(N_EXP)
    return c


def kernel(**inputs):
    import math

    import numpy as np
    import concourse.bacc as _bacc
    from concourse import mybir as _mybir
    from concourse.bass_utils import run_bass_kernel_spmd as _run

    a = {k: np.asarray(v) for k, v in inputs.items()}

    def columns(x):
        return x.reshape(L, -1, P).transpose(0, 2, 1)

    x = np.concatenate([a["x_prompt"][0], a["x_sample"][0]], axis=0)
    cond = np.stack([a["c_ctx"], a["c"][0]], axis=0)
    lam_init = np.array([0.8 - 0.6 * math.exp(-0.3 * i) for i in range(L)])
    li = np.zeros((L, P, 2), np.float32)
    li[:, :, 0] = lam_init[:, None]
    li[:, :, 1] = 1.0 - lam_init[:, None]
    vecs = np.concatenate([columns(v) for v in (
        a["ada_b"], a["norm1_g"], a["norm2_g"], a["b_merge"], a["mla_qa_norm"], a["diff_subln"],
        a["lru_conv_w"].reshape(L, -1), a["lru_conv_b"], a["lru_gate_b"].reshape(L, -1),
        a["lru_lambda"].reshape(L, -1), a["state_lru"][0].reshape(L, -1))] + [li], axis=2)
    rows = np.concatenate([a["mla_kva_norm"], a["mla_qn"], a["mla_kn"], a["diff_qn"], a["diff_kn"],
                           a["diff_lambda"].reshape(L, -1), a["router_b"]], axis=1)
    arrays = {
        "x_in": x.T.reshape(KC, P, NT).transpose(1, 0, 2),
        "cond_in": cond.T.reshape(KC, P, G).transpose(1, 0, 2),
        "consts": constants(np), "vecs": vecs, "rows": rows,
        "ada_w": a["ada_w"], "w_in": a["w_in"], "w_q_b": a["w_q_b"], "w_kv_b": a["w_kv_b"],
        "lru_gate_w": a["lru_gate_w"].reshape(L, 32, 64, 64),
        "w_o_mla": a["w_o_mla"], "w_o_lru": a["w_o_lru"], "w_o_diff": a["w_o_diff"],
        "w_merge": a["w_merge"], "w_out": a["w_out"], "router_w": a["router_w"],
        "exp_w1": a["exp_w1"].reshape(L * N_EXP, D, 2 * D_EXP), "exp_b1": a["exp_b1"],
        "exp_w2": a["exp_w2"].reshape(L * N_EXP, D_EXP, D), "exp_b2": a["exp_b2"],
        "cache_ckv": a["cache_mla_ckv"][0], "cache_krope": a["cache_mla_krope"][0],
        "cache_dk": a["cache_diff_k"][0].reshape(L, P, 512), "cache_dv": a["cache_diff_v"][0].reshape(L, P, 512),
    }
    outs = {"y_out": (P, KC, NT), "new_ckv": (L, P, KV_LORA), "new_krope": (L, P, ROPE), "new_lru": (L, P, 8),
            "new_dk": (L, P, 512), "new_dv": (L, P, 512)}
    nc = _bacc.Bacc("TRN2", target_bir_lowering=False, num_devices=1)
    given, args = {}, []
    for name, v in arrays.items():
        given[f"{name}_dram"] = np.ascontiguousarray(v)
        args.append(nc.dram_tensor(f"{name}_dram", v.shape, _mybir.dt.float32, kind="ExternalInput").ap())
    for name, shape in outs.items():
        args.append(nc.dram_tensor(f"{name}_dram", shape, _mybir.dt.float32, kind="ExternalOutput").ap())
    build(nc, *args)
    r = _run(nc, [given], core_ids=[0]).results[0]
    y = r["y_out_dram"].transpose(1, 0, 2).reshape(D, NT).T
    return (np.ascontiguousarray(y[:P])[None], np.ascontiguousarray(y[P:])[None],
            r["new_ckv_dram"][None], r["new_krope_dram"][None],
            np.ascontiguousarray(r["new_lru_dram"].transpose(0, 2, 1)).reshape(1, L, 2, D_RNN),
            r["new_dk_dram"].reshape(1, L, P, DIFF_H, 2, DH), r["new_dv_dram"].reshape(1, L, P, DIFF_H, DV))
```

```python
from contextlib import ExitStack

import concourse.bass as bass
from concourse import mybir

F32 = mybir.dt.float32
I32 = mybir.dt.int32
ALU = mybir.AluOpType
ACT = mybir.ActivationFunctionType
AX_X = mybir.AxisListType.X

P = 128
D = 1024
KC = D // P
G = 2
NT = G * P
L = 2
EPS = 1e-6

MLA_H, NOPE, ROPE, VD = 8, 64, 32, 64
QK = NOPE + ROPE
Q_LORA, KV_LORA = 384, 256
D_RNN = 512
RC = D_RNN // P
DIFF_H, DH, DV = 4, 64, 128
N_EXP, D_EXP, TOP_K = 32, 512, 4
SLOTS = 64
LIMIT, ALPHA = 7.0, 1.702
FIRST = 3
MAX_EXTRA = 16

OFF_KVA = Q_LORA
OFF_LRU = OFF_KVA + KV_LORA + ROPE
OFF_DQ = OFF_LRU + 2 * D_RNN
M_COLS = OFF_LRU

V_ADAB, V_N1, V_N2, V_BM, V_QA, V_SUB = 0, 48, 56, 64, 88, 91
V_CW, V_CB, V_GB, V_LAM, V_ST, V_LI, V_OML = 92, 108, 112, 128, 136, 144, 145
NV = 146
R_KVA, R_QN, R_KN, R_DQN, R_DKN, R_DL, R_RB = 0, 256, 352, 448, 512, 576, 832
NR = 864
C_ID, C_UT, C_ONE, C_IOTA = 0, 128, 256, 384
C_CM, C_SM, C_CD, C_SD = 512, 544, 576, 640
C_PIDX, C_KK, C_EIDX, C_EPS, C_FOLD = 704, 705, 721, 753, 754
NC = 786

RING = 6
SLOT = 4096
S_ADA = (0, 15, 25)
S_IN = (4, 5, 6, 7, 10, 11, 12)
S_QB, S_KVB = 8, 9
S_WM = {1: (13, 14), 0: (20, 21), 2: (22, 24)}
S_WO = {1: 19, 0: 23, 2: 29}
S_OUT = 30
PRE = 32
IN_SLICES = ((0, 512), (512, 160), (OFF_LRU, 512), (OFF_LRU + 512, 512), (OFF_DQ, 512), (OFF_DQ + 512, 512),
             (OFF_DQ + 1024, 512))
BRANCHES = (1, 0, 2)
MERGE = [("gate", 1, ch) for ch in range(KC)]
for _b, _next in ((1, 0), (0, 2)):
    for _ch in range(KC):
        MERGE += [("proj", _b, _ch), ("gate", _next, _ch)]
MERGE += [("proj", 2, ch) for ch in range(KC)] + [("out", 0, ch) for ch in range(KC)]


def merge_slot(kind, b, ch):
    return {"gate": S_WM[b][ch // 4], "proj": S_WO[b], "out": S_OUT + ch // 4}[kind]


def later_uses(s):
    return len(range(s, PRE, RING)) - 1


def build(nc, x_in, cond_in, consts, vecs, rows, ada_w, w_in, w_q_b, w_kv_b, lru_gate_w, w_o_mla, w_o_lru,
          w_o_diff, w_merge, w_out, router_w, exp_w1, exp_b1, exp_w2, exp_b2, cache_ckv, cache_krope,
          cache_dk, cache_dv, y_out, new_ckv, new_krope, new_lru, new_dk, new_dv):
    ctx = ExitStack()
    with ctx:
        def sb(name, shape, dt=F32):
            return ctx.enter_context(nc.sbuf_tensor(name, shape, dt))

        sems = []

        def sem(name):
            s = ctx.enter_context(nc.semaphore(name))
            sems.append(s)
            return s

        cst = sb("cst", [P, NC])
        vec = sb("vec", [P, NV])
        row = sb("row", [P, NR])
        cT = sb("cT", [P, KC, 32])
        modT = sb("modT", [P, 48, G])
        A1 = sb("A1", [P, KC, G])
        A2 = sb("A2", [P, KC, G])
        g1h = sb("g1h", [P, KC, G])
        gbh = sb("gbh", [P, 16])
        bmh = sb("bmh", [P, 24])
        sp = sb("sp", [P, 32])
        clh = sb("clh", [P, 8])
        lam = sb("lam", [P, 8])
        lprod = sb("lprod", [P, 128])
        subg = sb("subg", [P, 1])
        ss = sb("ss", [P, 32])
        nwt = sb("nwt", [P, 2, 32])
        krs = sb("krs", [P, 4])
        nm = sb("nm", [P, 2, 4])
        sums = sb("sums", [P, 2, 4])
        rcp = sb("rcp", [P, 2, 4])
        nl = sb("nl", [P, 2])
        rs = sb("rs", [P, NT])
        fin = sb("fin", [P, 8])
        xT = sb("xT", [P, KC, NT])
        hT = sb("hT", [P, KC, NT])
        rw = sb("rw", [P, KC, N_EXP])
        ring = sb("ring", [P, RING, SLOT])
        arena = sb("arena", [P, 21344])
        meta = sb("meta", [P, 2], I32)
        both = sb("both", [P, MAX_EXTRA // 2], I32)
        eidi = sb("eidi", [P, MAX_EXTRA], I32)
        ps = ctx.enter_context(nc.psum_tensor("ps", [P, 8, 512], F32))

        def at(off, *dims):
            n = 1
            for d in dims:
                n *= d
            v = arena[:, off:off + n]
            if len(dims) == 2:
                return v.rearrange("p (a b) -> p a b", a=dims[0])
            if len(dims) == 3:
                return v.rearrange("p (a b c) -> p a b c", a=dims[0], b=dims[1])
            if len(dims) == 4:
                return v.rearrange("p (a b c d) -> p a b c d", a=dims[0], b=dims[1], c=dims[2])
            return v

        merged = at(0, KC, NT)
        qaT = at(0, 3, NT)
        ckvT = at(768, 2, 384)
        lru_u = at(1536, 2, NT)
        tg = at(2048, KC, NT)
        lruw = at(2048, 16, P)
        projm = at(4096, G, M_COLS)
        projd = at(5440, 3, G, 512)
        E0 = 8512
        xpad = at(E0, RC, G, P + 3)
        lru_a = at(E0, RC, NT)
        lru_t = at(E0 + 1024, RC, NT)
        lru_h = [at(E0 + 2048, RC, NT), at(E0 + 3072, RC, NT)]
        xr = at(E0 + 4096, RC, NT)
        gel = at(E0 + 5120, RC, NT)
        scratch = at(0, 768)
        qkT = [at(E0, 640), at(E0 + 640, 640)]
        probs = [at(E0 + 1280, 2, 384), at(E0 + 2048, 2, 384)]
        probsT = [at(E0 + 2816, 384), at(E0 + 3200, 384)]
        on = at(E0 + 3584, G, DV)
        mtmp = at(E0 + 3840, NT)
        omla = at(E0 + 4096, 4, NT)
        odif = at(E0 + 5120, 4, NT)
        Q0 = E0 + 6144
        q_tok = at(Q0, G, MLA_H, QK)
        onsq = at(Q0, G, DV)
        msb = (at(Q0, 512), at(768, 512), at(Q0 + 512, 512))
        v_tok = at(Q0 + 1536, 3, 512)
        k_tok = at(Q0 + 3072, 3, MLA_H, QK)
        sq = at(Q0 + 3072, KC, NT)
        assert Q0 + 3072 + 2304 == 20032
        c_ckv = at(20032, KV_LORA)
        c_kr = at(20288, ROPE)
        c_dk = at(20320, 512)
        c_dv = at(20832, 512)
        more = [at(0, SLOT), at(SLOT, SLOT)]
        b1 = at(E0 + 2048, D)
        b2 = at(19776, D)
        X2 = at(E0, G, D)
        xTg = at(E0 + 3072, KC, P)
        gate_s, up_s, sig_s, act_s = (at(E0 + 4096 + 512 * i, 512) for i in range(4))
        actT = at(E0 + 6144, 4, P)
        O_s = at(E0 + 6656, D)
        SCT = at(E0 + 7680, NT)
        S_s = at(E0 + 7936, G, P)
        SC_s = at(E0 + 8192, G, P)
        oh = at(E0 + 8448, P)
        T0 = E0 + 8576
        lgt, rep, msk, exl, cmb = (at(T0 + 64 * i, G, N_EXP) for i in range(5))
        pm1 = at(T0 + 320, G, N_EXP)
        top8 = at(T0 + 384, G, 8)
        nv1 = at(T0 + 400, G)
        den = at(T0 + 402, G)
        cnt = at(T0 + 404, N_EXP)
        xtra = at(T0 + 436, N_EXP)
        tend = at(T0 + 468, N_EXP)
        tbeg = at(T0 + 500, N_EXP)
        npf = at(T0 + 532, 2)
        cmp8 = at(T0 + 534, 8)
        psub = at(T0 + 542, MAX_EXTRA)
        NTAB = N_EXP + MAX_EXTRA + 2
        pmT = at(T0 + 558, G, NTAB)
        cwT = at(T0 + 658, G, NTAB)
        eidf = at(T0 + 758, NTAB)
        ctT = at(T0 + 808, NT)
        lpart = ctT
        K0 = T0 + 1064
        sel, tmpx, tmpy = (at(K0 + 512 * i, MAX_EXTRA, N_EXP) for i in range(3))
        assert K0 + 3 * 512 <= 19776

        ident = cst[:, C_ID:C_ID + P]
        ustrict = cst[:, C_UT:C_UT + P]
        ones = cst[:, C_ONE:C_ONE + P]
        one_col = cst[:, C_ONE:C_ONE + 1]

        arr = [sem(f"slot{s}_arrived") for s in range(RING)]
        ld_lruw = sem("lruw_in")
        more_arr = [sem(f"more{i}_arrived") for i in range(2)]
        ld_ckv, ld_kr, ld_dk, ld_dv = sem("cckv_in"), sem("ckr_in"), sem("cdk_in"), sem("cdv_in")
        ld_rw, ld_b1, ld_b2 = sem("rw_in"), sem("b1_in"), sem("b2_in")
        out_done, y_done = sem("out_done"), sem("y_done")
        lruw_zero = sem("lruw_zero")
        v_step, a_step = sem("dve_step"), sem("act_step")
        x_upd, lp_v, fold_mm = sem("x_updated"), sem("logit_parts"), sem("logits_mm")
        sq_rdy = sem("sq_rdy")
        nrm_mm, nrm_sq, hraw, h_v, h_a = (
            [sem(f"{n}{i}") for i in range(2)] for n in ("nrm_mm", "nrm_sqrt", "hraw", "h_dve", "h_act"))
        ada_mm, ada_sb, ada_tr, prep, mod_rdy = (sem(n) for n in
                                                 ("ada_mm", "ada_sb", "ada_tr", "prep", "mod_rdy"))
        sp_abs, sp_ln, lam_exp = sem("sp_abs"), sem("sp_ln"), sem("lam_exp")
        win_mm, win_v, win_a = sem("win_mm"), sem("win_evac_v"), sem("win_evac_a")
        mla_n, conv_rdy = sem("mla_norm"), sem("conv_rdy")
        p3_mm, p3_ev, p4_mm, p4_ev = sem("lat_tr"), sem("lat_evac"), sem("exp_mm"), sem("exp_evac")
        lg_mm, lg_ev, lru_at, lru_w, lru_sq, lru_fr, lru_rdy = (
            sem(n) for n in ("lru_mm", "lru_evac", "lru_at", "lru_w", "lru_sqrt", "lru_free", "lru_rdy"))
        qn_rdy, kn_rdy, dn_rdy = sem("qn_rdy"), sem("kn_rdy"), sem("dn_rdy")
        f_mm, f_ac, f_dv = sem("merge_mm"), sem("merge_act"), sem("merge_dve")
        t_mm, qk_v, qk_a, s_mm, nm_v, ex_a = (sem(n) for n in ("qk_tr", "qk_evac_v", "qk_evac_a", "score_mm",
                                                              "negmax", "exp_done"))
        pn_v, pt_mm, ptc, pv_mm, om_ev, on_v, ot_mm, od_ev = (
            sem(n) for n in ("probs_rdy", "pt_tr", "pt_evac", "pv_mm", "omla_rdy", "on_rdy", "on_tr", "odif_rdy"))
        rt_mm, x2_mm, x2_ev, nv_v, exl_a, msk_v, pos_mm, cmb_v, ct_mm, ct_ev, routed = (
            sem(n) for n in ("router_mm", "x2_tr", "x2_evac", "negtop", "exl_rdy", "mask_rdy", "pos_mm", "cmb_rdy",
                             "ct_mm", "ct_evac", "routed"))
        disp, xt_a, xt_v = (sem(n) for n in ("disp_rdy", "xt_evac_a", "xt_evac_v"))
        ga_mm = [sem(f"gather_mm{i}") for i in range(2)]
        g1_mm = [sem(f"w1_mm{i}") for i in range(2)]
        gate_v, up_v, prod_v, sig_a, act_v, at_mm, at_ev = (
            sem(n) for n in ("gate_rdy", "up_rdy", "prod_rdy", "sig_rdy", "act_rdy", "act_tr",
                             "act_evac"))
        g2_mm, o_a, o_v, sct_mm, sct_ev = (sem(n) for n in ("w2_mm", "o_evac_a", "o_evac_v", "sct_tr",
                                                            "sct_evac"))
        sc_mm = [sem(f"scatter_mm{i}") for i in range(4)]
        early_vec, early_row = (ctx.enter_context(nc.semaphore(n)) for n in ("vec_early", "row_early"))
        early = [ctx.enter_context(nc.semaphore(f"slot{s}_early")) for s in range(RING)]
        s_set = [ctx.enter_context(nc.semaphore(f"setup{i}")) for i in range(5)]

        def consumed(pos):
            for r in range(3):
                if S_ADA[r] <= pos < S_ADA[r] + 4:
                    return ada_mm, r + 1
            if pos in S_IN:
                return win_mm, 2 * (S_IN.index(pos) + 1)
            if pos in (S_QB, S_KVB):
                return p4_mm, {S_QB: 4, S_KVB: 10}[pos]
            return f_mm, max(f for f, m in enumerate(MERGE) if merge_slot(*m) == pos) + 1

        def arrived(eng, pos):
            if pos < RING:
                eng.wait_ge(early[pos], l * 16 + 16)
            else:
                eng.wait_ge(arr[pos % RING], 16 * (pos // RING))
            return ring[:, pos % RING, :]

        def merge_evac(eng, f):
            gates = sum(m[0] == "gate" for m in MERGE[:f - 1])
            if MERGE[f - 2][0] == "gate":
                eng.wait_ge(f_ac, gates)
            else:
                eng.wait_ge(f_dv, f - 1 - gates)

        def merge_ps(f):
            return ps[:, 6 + f % 2, 0:NT]

        def rows_of(w, layer, nk, c0, nc_):
            return w[bass.ds(layer, 1), 0:nk * P, c0:c0 + nc_].rearrange("o (k p) n -> p (o k) n", p=P)

        def ada_or_in(layer, pos):
            for r in range(3):
                if S_ADA[r] <= pos < S_ADA[r] + 4:
                    return rows_of(ada_w, layer, KC, (4 * r + pos - S_ADA[r]) * 512, 512), 512
            c0, w = IN_SLICES[S_IN.index(pos)]
            return rows_of(w_in, layer, KC, c0, w), w

        def load_early(eng, layer, pos):
            src, w = ada_or_in(layer, pos)
            eng.dma_start(ring[:, pos, 0:KC * w].rearrange("p (k n) -> p k n", n=w), src).then_inc(early[pos], 16)

        def load_vectors(eng, layer):
            eng.dma_start(vec[:, :], vecs[bass.ds(layer, 1), :, :].rearrange("o p n -> (o p) n")).then_inc(
                early_vec, 16)
            eng.dma_start(row[:, :], rows[bass.ds(layer, 1), :].broadcast_to((P, NR))).then_inc(early_row, 16)

        with nc.Block() as block:
            @block.sync
            def _(sp_):
                sp_.dma_start(xT[:, :, :], x_in).then_inc(s_set[2], 16)
                sp_.dma_start(cT[:, :, 0:G], cond_in).then_inc(s_set[0], 16)
                sp_.dma_start(cst[:, :], consts).then_inc(s_set[1], 16)
                for pos in range(RING):
                    load_early(sp_, 0, pos)
                    if pos == 3:
                        load_vectors(sp_, 0)
                sp_.wait_ge(s_set[1], 16)
                sp_.wait_ge(s_set[2], 16)

            @block.scalar
            def _(act):
                act.wait_ge(s_set[2], 16)
                nc.scalar.activation(sq[:, :, :], xT[:, :, :], ACT.Square)
                act.wait_ge(s_set[0], 16)
                nc.scalar.activation(cT[:, :, G:2 * G], cT[:, :, 0:G], ACT.Tanh, scale=0.5).then_inc(s_set[3], 1)

            @block.vector
            def _(dve):
                dve.wait_ge(s_set[3], 1)
                nc.vector.tensor_scalar(cT[:, :, G:2 * G], cT[:, :, G:2 * G], 0.5, 0.5, ALU.mult,
                                        ALU.add).then_inc(s_set[4], 1)
                dve.wait_ge(s_set[4], 1)
                nc.vector.tensor_tensor(cT[:, :, 0:G], cT[:, :, 0:G], cT[:, :, G:2 * G],
                                        ALU.mult).then_inc(s_set[4], 1)
                dve.wait_ge(s_set[4], 2)
                nc.vector.memset(cT[:, :, G:32], 0.0).then_inc(s_set[4], 1)

        with nc.Fori(0, L) as l:
            with nc.Block() as block:
                @block.sync
                def _(sp_):
                    def load(pos, src, n):
                        dst = ring[:, pos % RING, 0:n]
                        s, v = consumed(pos - RING)
                        sp_.wait_ge(s, v)
                        shape = src.shape
                        sp_.dma_start(dst.rearrange("p (a b) -> p a b", b=shape[2]), src).then_inc(
                            arr[pos % RING], 16)

                    wo = {0: w_o_mla, 1: w_o_lru, 2: w_o_diff}
                    for pos in range(RING, PRE):
                        for b in BRANCHES:
                            if pos in S_WM[b]:
                                load(pos, rows_of(w_merge, l, KC, b * D + S_WM[b].index(pos) * 512, 512), SLOT)
                            if pos == S_WO[b]:
                                load(pos, rows_of(wo[b], l, 4, 0, D), SLOT)
                        if pos == S_QB:
                            load(pos, rows_of(w_q_b, l, 3, 0, 768), 3 * 768)
                        elif pos == S_KVB:
                            load(pos, rows_of(w_kv_b, l, 2, 0, 1024), 2048)
                        elif pos >= S_OUT:
                            load(pos, rows_of(w_out, l, KC, (pos - S_OUT) * 512, 512), SLOT)
                        elif pos in S_IN or any(r <= pos < r + 4 for r in S_ADA):
                            src, w = ada_or_in(l, pos)
                            load(pos, src, KC * w)

                    def expert_parts(e):
                        b = bass.ds(l * N_EXP + e, 1)
                        return exp_w1[b, 0:512, :], exp_w1[b, 512:1024, :], exp_w2[b, :, :]

                    def load_part(slot, src, dst=None, signal=None):
                        dst = ring[:, slot, :] if dst is None else dst
                        sp_.dma_start(dst.rearrange("p (k n) -> p k n", n=D),
                                      src.rearrange("o (k p) n -> p (o k) n", p=P)).then_inc(
                                          arr[slot] if signal is None else signal, 16)

                    def pair(experts, waits, order=range(RING)):
                        srcs = [expert_parts(e) for e in experts]
                        for j in order:
                            s, v = waits[j]
                            sp_.wait_ge(s, v)
                            load_part(j, srcs[j % 2][j // 2])

                    def freed(pairs_before):
                        return [(g1_mm[0], pairs_before)] * 2 + [(g1_mm[1], pairs_before)] * 2 + \
                            [(g2_mm, pairs_before * 2)] * 2

                    last_pos = [s + RING * later_uses(s) for s in range(RING)]
                    order = sorted(range(RING), key=last_pos.__getitem__)
                    free = [consumed(pos) for pos in last_pos]
                    pair((0, 1), free, order[:3])
                    sp_.wait_ge(pv_mm, 12)
                    sp_.wait_ge(out_done, 16 * 5)
                    load_part(1, expert_parts(3)[0], more[1], more_arr[1])
                    pair((0, 1), free, order[3:])
                    sp_.wait_ge(f_mm, len(MERGE))
                    sp_.wait_ge(f_dv, 32)
                    load_part(0, expert_parts(2)[0], more[0], more_arr[0])
                    pair((4, 5), freed(1), (0, 1))
                    pair((2, 3), freed(1), range(2, RING))
                    pair((4, 5), freed(2), range(2, RING))
                    sp_.wait_ge(routed, 1)
                    n_extra = sp_.value_load(meta[0:1, 0:1], min_val=0, max_val=MAX_EXTRA // 2)
                    with sp_.If(n_extra > 0):
                        with sp_.Fori(0, n_extra) as q:
                            e = [sp_.value_load(eidi[0:1, bass.ds(q * 2 + i, 1)], min_val=0, max_val=N_EXP - 1)
                                 for i in range(2)]
                            two = sp_.value_load(both[0:1, bass.ds(q, 1)], min_val=0, max_val=1)
                            with sp_.If(two > 0):
                                pair(e, freed(q + FIRST))
                            with sp_.Else():
                                srcs = expert_parts(e[0])
                                for j, (s, v) in enumerate(freed(q + FIRST)):
                                    sp_.wait_ge(s, v)
                                    if j % 2 == 0:
                                        load_part(j, srcs[j // 2])
                                    else:
                                        sp_.sem_inc(arr[j], 16)
                    with sp_.Else():
                        sp_.nop()
                    with sp_.Fori(FIRST, N_EXP // 2) as q:
                        pair((q * 2, q * 2 + 1), freed(n_extra + q))
                    with sp_.If(l < L - 1):
                        following = nc.s_assert_within(
                            l + 1, 1, L - 1, skip_runtime_bounds_check_because="this is the branch l < L - 1")
                        load_vectors(sp_, following)
                        for slot, (s, v) in enumerate(freed(n_extra + N_EXP // 2)):
                            sp_.wait_ge(s, v)
                            load_early(sp_, following, slot)
                    with sp_.Else():
                        for h in range(2):
                            sp_.wait_ge(x_upd, 4 * h + 4)
                            c = slice(4 * h, 4 * h + 4)
                            sp_.dma_start(y_out[:, c, :], xT[:, c, :]).then_inc(y_done, 16)
                        sp_.wait_ge(y_done, 32)
                    sp_.nop()

                @block.gpsimd
                def _(pool):
                    nc.gpsimd.memset(lruw[:, :, :], 0.0).then_inc(lruw_zero, 1)

                @block.tensor
                def _(pe):
                    mm = nc.tensor.matmul
                    tr = nc.tensor.transpose

                    def norm(i, bank):
                        for k in range(KC):
                            if i == 1:
                                pe.wait_ge(sq_rdy, k + 1)
                            last = mm(ps[:, bank, 0:NT], ones, sq[:, k, :], start=k == 0, stop=k == KC - 1)
                        last.then_inc(nrm_mm[i], 1)

                    norm(0, 7)
                    def ada_products(r, bank):
                        slots = [arrived(pe, S_ADA[r] + j) for j in range(4)]
                        for k in range(KC):
                            for j in range(4):
                                last = mm(ps[32 * j:32 * j + 32, bank, :], cT[:, k, :],
                                          slots[j][:, k * 512:(k + 1) * 512], start=k == 0, stop=k == KC - 1)
                        last.then_inc(ada_mm, 1)

                    def ada_transposes(r, bank):
                        pe.wait_ge(ada_sb, r + 1)
                        for b in range(4):
                            last = tr(ps[:, bank, b * P:(b + 1) * P], msb[r][:, b * P:(b + 1) * P], ident)
                        last.then_inc(ada_tr, 1)

                    ada_products(0, 0)
                    ada_transposes(0, 3)

                    def lru_products(d):
                        for i in range(8 * d, 8 * d + 8):
                            if d and i % 2 == 0:
                                pe.wait_ge(lg_ev, i - 6)
                            mm(ps[:, 2 + (i % 8) // 2, (i % 2) * NT:(i % 2 + 1) * NT], lruw[:, i, :],
                               xr[:, i % 4, :], start=True, stop=True).then_inc(lg_mm, 1)

                    def latent_products():
                        pe.wait_ge(win_a, 2)
                        pe.wait_ge(mla_n, 1)
                        for b in range(3):
                            for g in range(G):
                                last = tr(ps[:, b // 2, (b % 2) * NT + g * P:(b % 2) * NT + (g + 1) * P],
                                          projm[:, g, b * P:(b + 1) * P], ident)
                            last.then_inc(p3_mm, 1)
                        pe.wait_ge(ld_ckv, 16)
                        for b in range(2):
                            for s in range(3):
                                src = c_ckv[:, b * P:(b + 1) * P] if s == 1 else \
                                    projm[:, s // 2, OFF_KVA + b * P:OFF_KVA + (b + 1) * P]
                                last = tr(ps[:, 6 + b, s * P:(s + 1) * P], src, ident)
                            last.then_inc(p3_mm, 1)
                        pe.wait_ge(conv_rdy, 1)
                        pe.wait_ge(ld_lruw, 32)
                        lru_products(0)
                        for v in range(10):
                            if v == 0:
                                pe.wait_ge(p3_ev, 5)
                                slot = arrived(pe, S_QB)[:, 0:3 * 768].rearrange("p (k n) -> p k n", n=768)
                            if v == 4:
                                slot = arrived(pe, S_KVB)[:, 0:2048].rearrange("p (k n) -> p k n", n=1024)
                            if v >= 2:
                                pe.wait_ge(p4_ev, v - 1)
                            half = v % 2
                            if v < 4:
                                for k in range(3):
                                    last = mm(ps[:, half, 0:384], qaT[:, k, (v // 2) * P:(v // 2 + 1) * P],
                                              slot[:, k, half * 384:(half + 1) * 384], start=k == 0, stop=k == 2)
                            else:
                                s = v // 2 - 2
                                for k in range(2):
                                    last = mm(ps[:, half, :], ckvT[:, k, s * P:(s + 1) * P],
                                              slot[:, k, half * 512:(half + 1) * 512], start=k == 0, stop=k == 1)
                            last.then_inc(p4_mm, 1)

                    u = 0
                    for n, (kind, w) in enumerate((("tok", 512), ("tok", 160), ("feat", 512), ("feat", 512),
                                                   ("tok", 512), ("tok", 512), ("tok", 512))):
                        if n == 4:
                            latent_products()
                        slot = arrived(pe, S_IN[n])[:, 0:KC * w].rearrange("p (k n) -> p k n", n=w)
                        for half in range(2):
                            bank = u if u < 6 else u % 2
                            if 6 <= u < 8:
                                pe.wait_ge(win_v, u - 5)
                            elif u >= 8:
                                pe.wait_ge(p4_ev, min(u + 1, 10))
                                if u >= 10:
                                    pe.wait_ge(win_a, u - 7)
                            if kind == "tok":
                                for k in range(KC):
                                    if u == 0:
                                        pe.wait_ge(h_v[0], k + 1)
                                    if u == 1:
                                        pe.wait_ge(h_a[0], k + 1)
                                    last = mm(ps[:, bank, 0:w], hT[:, k, half * P:(half + 1) * P],
                                              slot[:, k, :], start=k == 0, stop=k == KC - 1)
                            else:
                                for c in range(2):
                                    for k in range(KC):
                                        ch = 2 * half + c
                                        last = mm(ps[:, bank, c * NT:(c + 1) * NT],
                                                  slot[:, k, ch * P:(ch + 1) * P], hT[:, k, :],
                                                  start=k == 0, stop=k == KC - 1)
                            last.then_inc(win_mm, 1)
                            u += 1
                            if u == 10:
                                lru_products(1)

                    done = [0]

                    def merge(n):
                        for _ in range(n):
                            f = done[0]
                            done[0] += 1
                            kind, b, ch = MERGE[f]
                            if f >= 2:
                                merge_evac(pe, f)
                            out = merge_ps(f)
                            slot = arrived(pe, merge_slot(kind, b, ch))
                            if kind == "proj":
                                slot = slot.rearrange("p (k n) -> p k n", n=D)
                                cols = slice(ch * P, (ch + 1) * P)
                                if ch == 0:
                                    pe.wait_ge(*{1: (lru_rdy, 1), 0: (om_ev, 4), 2: (od_ev, 4)}[b])
                                src, nk = {1: gel, 0: omla, 2: odif}[b], 4
                            else:
                                slot = slot.rearrange("p (k n) -> p k n", n=512)
                                cols = slice((ch % 4) * P, (ch % 4 + 1) * P)
                                src, nk = (merged if kind == "out" else hT), KC
                                if kind == "out" and ch == 0:
                                    pe.wait_ge(f_dv, 24)
                            for k in range(nk):
                                last = mm(out, slot[:, k, cols], src[:, k, :], start=k == 0, stop=k == nk - 1)
                            last.then_inc(f_mm, 1)

                    pe.wait_ge(p3_ev, 5)
                    merge(8)
                    pe.wait_ge(win_a, 8)
                    ada_products(1, 0)
                    ada_transposes(1, 1)
                    merge(1)

                    def qk_transposes(u):
                        if u == 0:
                            pe.wait_ge(mod_rdy, 2)
                            pe.wait_ge(qn_rdy, 2)
                            pe.wait_ge(kn_rdy, 3)
                        if u == 8:
                            pe.wait_ge(dn_rdy, 4)
                            pe.wait_ge(ld_dk, 16)
                        if u < 8:
                            rows_, srcs = QK, [q_tok[:, 0, u, :], q_tok[:, 1, u, :]] + \
                                [k_tok[:, s, u, :] for s in range(3)]
                        else:
                            c = slice((u - 8) * P, (u - 7) * P)
                            rows_, srcs = P, [projd[:, 0, 0, c], projd[:, 0, 1, c], projd[:, 1, 0, c],
                                              c_dk[:, c], projd[:, 1, 1, c]]
                        for n in range(3):
                            last = tr(ps[0:rows_, 0, n * P:(n + 1) * P], srcs[n], ident)
                        last.then_inc(t_mm, 1)
                        for n in range(2):
                            last = tr(ps[0:rows_, 1, n * P:(n + 1) * P], srcs[3 + n], ident)
                        last.then_inc(t_mm, 1)

                    def odif_transposes(u):
                        pe.wait_ge(on_v, u - 7)
                        for g in range(G):
                            last = tr(ps[:, 5, NT + g * P:NT + (g + 1) * P], on[:, g, :], ident)
                        last.then_inc(ot_mm, 1)

                    qk_transposes(0)
                    for u in range(12):
                        b = qkT[u % 2]
                        pe.wait_ge(qk_v, u + 1)
                        pe.wait_ge(qk_a, u + 1)
                        if u == 0:
                            pe.wait_ge(lg_ev, 16)
                        if u >= 2:
                            pe.wait_ge(ex_a, u if u >= 8 else u - 1)
                        if u < 8:
                            bank = 2 + u % 2
                            mm(ps[:, bank, 0:128], b[0:QK, 0:128], b[0:QK, 256:384], start=True, stop=True)
                            mm(ps[:, bank, 128:384], b[0:QK, 128:256], b[0:QK, 384:640], start=True,
                               stop=True).then_inc(s_mm, 1)
                        else:
                            for c in range(2):
                                r = slice(64 * c, 64 * c + 64)
                                mm(ps[:, 2 + c, 0:128], b[r, 0:128], b[r, 256:384], start=True, stop=True)
                            for c in range(2):
                                r = slice(64 * c, 64 * c + 64)
                                last = mm(ps[:, 2 + c, 128:384], b[r, 128:256], b[r, 384:640], start=True,
                                          stop=True)
                            last.then_inc(s_mm, 1)
                        if u < 11:
                            qk_transposes(u + 1)
                        merge(1 if u < 8 else 2)
                        pe.wait_ge(pn_v, u + 1)
                        if u >= 1:
                            pe.wait_ge(ptc, u)
                        for n in range(3):
                            last = tr(ps[:, 4, n * P:(n + 1) * P], probs[u % 2][:, 0, n * P:(n + 1) * P], ident)
                        last.then_inc(pt_mm, 1)
                        if u > 8:
                            odif_transposes(u - 1)
                        if u != 7:
                            merge(1)
                        pe.wait_ge(ptc, u + 1)
                        t = probsT[u % 2]
                        if u < 8:
                            if u % 2 == 0 and u:
                                pe.wait_ge(om_ev, u // 2)
                            r = slice(64 * (u % 2), 64 * (u % 2) + 64)
                            c = slice(u * VD, (u + 1) * VD)
                            mm(ps[r, 5, 0:P], v_tok[:, 0, c], t[:, 0:P], start=True, stop=True)
                            mm(ps[r, 5, P:NT], v_tok[:, 1, c], t[:, P:2 * P], start=True, stop=False)
                            mm(ps[r, 5, P:NT], v_tok[:, 2, c], t[:, 2 * P:3 * P], start=False,
                               stop=True).then_inc(pv_mm, 1)
                        else:
                            if u == 8:
                                pe.wait_ge(om_ev, 4)
                                pe.wait_ge(ld_dv, 16)
                            else:
                                pe.wait_ge(od_ev, u - 8)
                            c = slice((u - 8) * P, (u - 7) * P)
                            mm(ps[:, 5, 0:P], t[:, 0:P], projd[:, 2, 0, c], start=True, stop=True)
                            mm(ps[:, 5, P:NT], t[:, P:2 * P], c_dv[:, c], start=True, stop=False)
                            mm(ps[:, 5, P:NT], t[:, 2 * P:3 * P], projd[:, 2, 1, c], start=False,
                               stop=True).then_inc(pv_mm, 1)
                            merge(1)
                    ada_products(2, 0)
                    odif_transposes(11)
                    merge(8)
                    ada_transposes(2, 1)
                    merge(8)

                    norm(1, 0)
                    pe.wait_ge(ld_rw, 16)
                    for k in range(KC):
                        pe.wait_ge(h_v[1], k + 1)
                        pe.wait_ge(h_a[1], k + 1)
                        c = slice(32 * (k % 4), 32 * (k % 4) + 32)
                        last = mm(ps[c, 1, 0:NT], rw[:, k, :], hT[:, k, :], start=k < 4, stop=k >= 4)
                    last.then_inc(rt_mm, 1)

                    def h2_transposes(n):
                        for j in range(4):
                            k = (n % 2) * 4 + j
                            last = tr(ps[:, 2 + n, j * P:(j + 1) * P], hT[:, k, (n // 2) * P:(n // 2 + 1) * P],
                                      ident)
                        last.then_inc(x2_mm, 1)

                    h2_transposes(0)
                    pe.wait_ge(lp_v, 1)
                    for g in range(G):
                        last = mm(ps[:, 1, 256 + g * N_EXP:256 + (g + 1) * N_EXP], lpart[:, g * P:(g + 1) * P],
                                  cst[:, C_FOLD:C_FOLD + N_EXP], start=True, stop=True)
                    last.then_inc(fold_mm, 1)
                    for n in range(1, 4):
                        h2_transposes(n)
                    pe.wait_ge(msk_v, 1)
                    mm(ps[:, 1, 64:96], ustrict, msk[:, 0, :], start=True, stop=True)
                    mm(ps[:, 1, 96:128], ones, msk[:, 0, :], start=True, stop=False)
                    mm(ps[:, 1, 96:128], ustrict, msk[:, 1, :], start=False, stop=True)
                    mm(ps[:, 1, 128:160], ones, msk[:, 0, :], start=True, stop=False)
                    mm(ps[:, 1, 128:160], ones, msk[:, 1, :], start=False, stop=True).then_inc(pos_mm, 1)

                    def gather(chunks):
                        for k in chunks:
                            for g in range(G):
                                last = mm(ps[:, 2 + k // 4, (k % 4) * P:(k % 4 + 1) * P],
                                          X2[:, g, k * P:(k + 1) * P], S_s[:, g, :], start=g == 0, stop=g == 1)
                            if k % 4 == 3:
                                last.then_inc(ga_mm[k // 4], 1)

                    def biases():
                        for h in range(2):
                            mm(ps[:, h, :], oh[0:N_EXP, :], b1[0:N_EXP, h * 512:(h + 1) * 512], start=True,
                               stop=True, skip_group_check=True)

                    pe.wait_ge(disp, 1)
                    pe.wait_ge(x2_ev, 4)
                    gather(range(KC))
                    pe.wait_ge(cmb_v, 1)
                    for g in range(G):
                        last = mm(ps[0:N_EXP, 0, g * P:(g + 1) * P], cmb[:, g, :], ident, start=True, stop=True)
                    last.then_inc(ct_mm, 1)
                    pe.wait_ge(ld_b1, 16)
                    pe.wait_ge(ct_ev, 1)
                    biases()

                    def pair(q, first=False, second=False):
                        for part in range(2):
                            w = []
                            for i in range(2):
                                s = 2 * part + i
                                slot = ring[:, s, :]
                                if part == 1 or first:
                                    pe.wait_ge(arr[s], q * 16 + 16 * (later_uses(s) + 1))
                                elif second:
                                    pe.wait_ge(more_arr[i], 16)
                                    slot = more[i]
                                else:
                                    pe.wait_ge(arr[s], q * 16 + 16 * later_uses(s))
                                w.append(slot.rearrange("p (k n) -> p k n", k=4))
                            for k in range(4):
                                for h in range(2):
                                    for i in range(2):
                                        c = slice(64 * i, 64 * i + 64)
                                        last = mm(ps[c, h, :], xTg[:, 4 * part + k, c],
                                                  w[i][:, k, h * 512:(h + 1) * 512], start=False,
                                                  stop=True, skip_group_check=True)
                            last.then_inc(g1_mm[part], 1)
                        pe.wait_ge(disp, q + 2)
                        gather(range(6))
                        pe.wait_ge(act_v, q + 1)
                        for b in range(4):
                            last = tr(ps[:, 0, b * P:(b + 1) * P], act_s[:, b * P:(b + 1) * P], ident)
                        last.then_inc(at_mm, 1)
                        gather(range(6, KC))
                        for g in range(G):
                            last = tr(ps[:, 1, g * P:(g + 1) * P], SC_s[:, g, :], ident)
                        last.then_inc(sct_mm, 1)
                        w = []
                        for i in range(2):
                            s = 4 + i
                            pe.wait_ge(arr[s], q * 16 + 16 * (later_uses(s) + 1))
                            w.append(ring[:, s, :].rearrange("p (f n) -> p f n", f=4))
                        pe.wait_ge(at_ev, q + 1)
                        for h in range(2):
                            pe.wait_ge((xt_a, xt_v)[h], q + 2)
                            for f in range(4):
                                for i in range(2):
                                    c = slice(64 * i, 64 * i + 64)
                                    last = mm(ps[c, 2 + h, :], actT[:, f, c], w[i][:, f, h * 512:(h + 1) * 512],
                                              start=f == 0, stop=f == 3)
                            last.then_inc(g2_mm, 1)
                        pe.wait_ge(sct_ev, q + 1)
                        for k in range(KC):
                            if k % 4 == 0:
                                pe.wait_ge((o_a, o_v)[k // 4], q + 1)
                            last = mm(ps[:, 4 + k // 2, (k % 2) * NT:(k % 2 + 1) * NT],
                                      O_s[:, k * P:(k + 1) * P], SCT[:, :], start=first and k % 2 == 0, stop=True,
                                      skip_group_check=True)
                            if k % 2:
                                last.then_inc(sc_mm[k // 2], 1)
                        biases()

                    pe.wait_ge(xt_a, 1)
                    pe.wait_ge(xt_v, 1)
                    pair(0, first=True)
                    pe.wait_ge(ld_b2, 16)
                    for k in range(KC):
                        mm(ps[:, 4 + k // 2, (k % 2) * NT:(k % 2 + 1) * NT], b2[0:N_EXP, k * P:(k + 1) * P],
                           ctT[0:N_EXP, :], start=False, stop=True, skip_group_check=True)
                    pair(1, second=True)
                    pe.wait_ge(routed, 1)
                    pairs = pe.value_load(meta[0:1, 1:2], min_val=N_EXP // 2, max_val=(N_EXP + MAX_EXTRA) // 2)
                    with pe.Fori(2, pairs) as q:
                        pair(q)

                @block.scalar
                def _(act):
                    A = nc.scalar.activation
                    a_n = [0]

                    def link(ins):
                        a_n[0] += 1
                        ins.then_inc(a_step, 1)
                        act.wait_ge(a_step, a_n[0])

                    def root_mean_square(i, bank):
                        act.wait_ge(nrm_mm[i], 1)
                        A(rs[:, :], ps[:, bank, 0:NT], ACT.Sqrt, bias=cst[:, C_EPS:C_EPS + 1],
                          scale=1.0 / D).then_inc(nrm_sq[i], 1)

                    def cache(dst, src, s):
                        act.dma_start(dst, src[bass.ds(l, 1), :, :].rearrange("o p n -> (o p) n")).then_inc(s, 16)

                    def store(dst, src):
                        act.dma_start(dst[bass.ds(l, 1), :, :].rearrange("o p n -> (o p) n"), src).then_inc(
                            out_done, 16)

                    root_mean_square(0, 7)
                    act.wait_ge(sp_abs, 1)
                    link(A(sp[:, 8:16], sp[:, 0:8], ACT.Exp, scale=-1.0))
                    A(sp[:, 16:24], sp[:, 8:16], ACT.Ln, bias=one_col).then_inc(sp_ln, 1)
                    act.wait_ge(lruw_zero, 1)
                    for j in range(2):
                        src = lru_gate_w[bass.ds(l, 1), bass.ds(j, 16, step=2), :, :]
                        act.dma_start(lruw[64 * j:64 * j + 64, :, 64 * j:64 * j + 64],
                                      src.rearrange("o b c e -> c (o b) e")).then_inc(ld_lruw, 16)
                    cache(c_ckv[:, :], cache_ckv, ld_ckv)
                    cache(c_kr[:, :], cache_krope, ld_kr)
                    cache(c_dk[:, :], cache_dk, ld_dk)
                    cache(c_dv[:, :], cache_dv, ld_dv)
                    act.dma_start(rw[:, :, :], router_w[bass.ds(l, 1), :, :].rearrange(
                        "o (k p) n -> p (o k) n", p=P)).then_inc(ld_rw, 16)

                    def modulate(i, scale, shift):
                        act.wait_ge(mod_rdy, 1 + 2 * i)
                        for k in range(KC):
                            act.wait_ge(hraw[i], k + 1)
                            A(hT[:, k, P:NT], hT[:, k, P:NT], ACT.Identity, bias=modT[:, shift + k, 1:2],
                              scale=scale[:, k, 1:2]).then_inc(h_a[i], 1)

                    modulate(0, A1, 0)

                    def win_evac(u):
                        act.wait_ge(win_mm, u + 1)
                        if u < 8:
                            A(gel[:, 2 * (u - 6):2 * (u - 6) + 2, :],
                              ps[:, u % 2, :].rearrange("p (c n) -> p c n", c=2),
                              ACT.Gelu_apprx_tanh).then_inc(win_a, 1)
                        else:
                            A(projd[:, (u - 8) // 2, u % 2, :], ps[:, u % 2, :], ACT.Copy).then_inc(win_a, 1)

                    def lru_tanh(i):
                        act.wait_ge(lg_mm, i // 2 * 2 + 2)
                        dst = lru_t if i % 8 < 4 else lru_h[i // 8]
                        A(dst[:, i % 4, :], ps[:, 2 + (i % 8) // 2, (i % 2) * NT:(i % 2 + 1) * NT], ACT.Tanh,
                          bias=gbh[:, i:i + 1], scale=0.5).then_inc(lg_ev, 1)

                    def lru_decay(d):
                        act.wait_ge(lg_ev, 8 * d + 4)
                        for c in range(RC):
                            z = clh[:, 4 * d + c:4 * d + c + 1]
                            last = A(lru_a[:, c, :], lru_t[:, c, :], ACT.Exp, bias=z, scale=z)
                        link(last)
                        for c in range(RC):
                            z = clh[:, 4 * d + c:4 * d + c + 1]
                            A(lru_t[:, c, :], lru_t[:, c, :], ACT.Tanh, bias=z, scale=z).then_inc(lru_at, 1)

                    def lru_roots(d):
                        for half in range(2):
                            c = slice(2 * half, 2 * half + 2)
                            act.wait_ge(lru_w, 2 * d + half + 1)
                            A(lru_t[:, c, :], lru_t[:, c, :], ACT.Sqrt).then_inc(lru_sq, 1)

                    act.wait_ge(prep, 2)
                    A(lam[:, 4:6], lam[:, 0:2], ACT.Exp).then_inc(lam_exp, 1)
                    for u in (6, 7):
                        win_evac(u)
                    for v in range(10):
                        act.wait_ge(p4_mm, v + 1)
                        half = v % 2
                        if v < 4:
                            A(q_tok[:, v // 2, 4 * half:4 * half + 4, :],
                              ps[:, half, 0:384].rearrange("p (h n) -> p h n", h=4), ACT.Copy).then_inc(p4_ev, 1)
                        else:
                            s = v // 2 - 2
                            src = ps[:, half, :].rearrange("p (h n) -> p h n", h=4)
                            A(k_tok[:, s, 4 * half:4 * half + 4, 0:NOPE], src[:, :, 0:NOPE], ACT.Copy)
                            A(v_tok[:, s, 256 * half:256 * half + 256].rearrange("p (h n) -> p h n", h=4),
                              src[:, :, NOPE:128], ACT.Copy).then_inc(p4_ev, 1)
                        if v < 8:
                            lru_tanh(v)
                    lru_decay(0)
                    act.wait_ge(mla_n, 1)
                    store(new_ckv, projm[:, 0, OFF_KVA:OFF_KVA + KV_LORA])
                    store(new_krope, projm[:, 0, OFF_KVA + KV_LORA:M_COLS])
                    win_evac(8)
                    win_evac(9)
                    lru_roots(0)
                    win_evac(10)
                    act.wait_ge(lru_fr, 1)
                    for i in range(8, 16):
                        lru_tanh(i)
                    lru_decay(1)
                    win_evac(11)
                    lru_roots(1)
                    win_evac(12)
                    win_evac(13)
                    act.wait_ge(win_a, 7)
                    store(new_dv, projd[:, 2, 0, :])

                    done = [0]

                    def merge_gates(n):
                        for _ in range(n):
                            j = done[0]
                            done[0] += 1
                            b, ch = BRANCHES[j // 8], j % 8
                            f = MERGE.index(("gate", b, ch))
                            act.wait_ge(f_mm, f + 1)
                            if j >= 8:
                                act.wait_ge(f_dv, j - 8 + 1)
                            A(tg[:, ch, :], merge_ps(f), ACT.Tanh, bias=bmh[:, 8 * b + ch:8 * b + ch + 1],
                              scale=0.5).then_inc(f_ac, 1)

                    def modulation(r, bank):
                        act.wait_ge(ada_mm, r + 1)
                        A(msb[r], ps[:, bank, :], ACT.Copy).then_inc(ada_sb, 1)

                    merge_gates(8)
                    modulation(1, 0)
                    act.wait_ge(lru_rdy, 1)
                    store(new_lru, fin[:, :])
                    act.wait_ge(dn_rdy, 3)
                    store(new_dk, projd[:, 1, 0, :])

                    def qk_copy(u):
                        n = QK if u < 8 else P
                        act.wait_ge(t_mm, 2 * u + 2)
                        A(qkT[u % 2][0:n, 384:640], ps[0:n, 1, 0:256], ACT.Copy).then_inc(qk_a, 1)

                    def odif_evac(u):
                        act.wait_ge(ot_mm, u - 7)
                        A(odif[:, u - 8, :], ps[:, 5, NT:2 * NT], ACT.Copy, scale=subg[:, 0:1]).then_inc(od_ev, 1)

                    qk_copy(0)
                    for u in range(12):
                        act.wait_ge(nm_v, u + 1)
                        j = u % 2
                        if u < 8:
                            for n, c in enumerate((slice(0, 128), slice(128, 384))):
                                last = A(probs[j][:, 0, c], ps[:, 2 + j, c], ACT.Exp, bias=nm[:, j, n:n + 1],
                                         accum_out=sums[:, j, n:n + 1])
                        else:
                            for n, c in enumerate((slice(0, 128), slice(128, 384))):
                                for m in range(2):
                                    e = 2 * n + m
                                    last = A(probs[j][:, m, c], ps[:, 2 + m, c], ACT.Exp, bias=nm[:, j, e:e + 1],
                                             accum_out=sums[:, j, e:e + 1])
                        last.then_inc(ex_a, 1)
                        if u < 11:
                            qk_copy(u + 1)
                        merge_gates(1)
                        act.wait_ge(pt_mm, u + 1)
                        A(probsT[j], ps[:, 4, 0:384], ACT.Copy).then_inc(ptc, 1)
                        if u > 8:
                            odif_evac(u - 1)
                        if u >= 8:
                            merge_gates(1)
                    modulation(2, 0)
                    odif_evac(11)

                    act.wait_ge(pv_mm, 12)
                    act.wait_ge(out_done, 16 * 5)
                    cache(b1[0:N_EXP, :], exp_b1, ld_b1)
                    cache(b2[0:N_EXP, :], exp_b2, ld_b2)
                    for k in range(KC):
                        act.wait_ge(f_dv, 24 + k + 1)
                        A(sq[:, k, :], xT[:, k, :], ACT.Square).then_inc(sq_rdy, 1)
                    root_mean_square(1, 0)
                    modulate(1, A2, 24)
                    for n in range(4):
                        act.wait_ge(x2_mm, n + 1)
                        A(X2[:, n // 2, (n % 2) * 512:(n % 2 + 1) * 512], ps[:, 2 + n, :],
                          ACT.Copy).then_inc(x2_ev, 1)
                    act.wait_ge(nv_v, 1)
                    for g in range(G):
                        last = A(exl[:, g, :], lgt[:, g, :], ACT.Exp, bias=nv1[:, g:g + 1])
                    last.then_inc(exl_a, 1)
                    act.wait_ge(ct_mm, 1)
                    A(ctT[0:N_EXP, :], ps[0:N_EXP, 0, 0:NT], ACT.Copy).then_inc(ct_ev, 1)

                    def gathered(n):
                        act.wait_ge(ga_mm[0], n + 1)
                        A(xTg[:, 0:4, :], ps[:, 2, :].rearrange("p (a b) -> p a b", a=4), ACT.Copy).then_inc(xt_a, 1)

                    gathered(0)

                    def pair(q):
                        act.wait_ge(gate_v, q + 1)
                        A(sig_s, gate_s, ACT.Sigmoid, scale=ALPHA).then_inc(sig_a, 1)
                        gathered(q + 1)
                        act.wait_ge(sct_mm, q + 1)
                        A(SCT[:, :], ps[:, 1, 0:NT], ACT.Copy).then_inc(sct_ev, 1)
                        act.wait_ge(g2_mm, q * 2 + 1)
                        A(O_s[:, 0:512], ps[:, 2, :], ACT.Copy).then_inc(o_a, 1)

                    pair(0)
                    act.wait_ge(routed, 1)
                    pairs = act.value_load(meta[0:1, 1:2], min_val=N_EXP // 2, max_val=(N_EXP + MAX_EXTRA) // 2)
                    with act.Fori(1, pairs) as q:
                        pair(q)
                    for k in range(KC):
                        act.wait_ge(x_upd, k + 1)
                        A(sq[:, k, :], xT[:, k, :], ACT.Square)

                @block.vector
                def _(dve):
                    V = nc.vector
                    v_n = [0]

                    def link(ins):
                        v_n[0] += 1
                        ins.then_inc(v_step, 1)
                        dve.wait_ge(v_step, v_n[0])

                    dve.wait_ge(early_vec, l * 16 + 16)
                    lmb = vec[:, V_LAM:V_LAM + 8]
                    V.scalar_tensor_tensor(out=sp[:, 0:8], in0=lmb, scalar=-1.0, in1=lmb, op0=ALU.mult,
                                           op1=ALU.max).then_inc(sp_abs, 1)

                    def rsqrt(x):
                        n = x.shape[1]
                        y, t = nwt[:, 0, 0:n], nwt[:, 1, 0:n]
                        link(V.tensor_scalar(y.bitcast(I32), x.bitcast(I32), 1, None, ALU.logical_shift_right))
                        link(V.tensor_scalar(y.bitcast(I32), y.bitcast(I32), -1.0, float(0x5f3759df), ALU.mult,
                                             ALU.add))
                        for it in range(4):
                            link(V.tensor_tensor(t, y, y, ALU.mult))
                            link(V.scalar_tensor_tensor(out=t, in0=t, scalar=-0.5, in1=x, op0=ALU.mult,
                                                        op1=ALU.mult))
                            link(V.scalar_tensor_tensor(out=y if it < 3 else x, in0=t, scalar=1.5, in1=y,
                                                        op0=ALU.add, op1=ALU.mult))

                    def norm_scale(i):
                        dve.wait_ge(nrm_sq[i], 1)
                        link(V.reciprocal(rs[:, :], rs[:, :]))

                    def scaled_x(i, k):
                        V.tensor_tensor(hT[:, k, :], xT[:, k, :], rs[:, :], ALU.mult).then_inc(hraw[i], 1)

                    norm_scale(0)
                    for k in range(KC):
                        scaled_x(0, k)

                    V.tensor_scalar(gbh[:, :], vec[:, V_GB:V_GB + 16], 0.5, None, ALU.mult)
                    V.tensor_scalar(bmh[:, :], vec[:, V_BM:V_BM + 24], 0.5, None, ALU.mult)
                    V.tensor_tensor(subg[:, :], vec[:, V_SUB:V_SUB + 1], vec[:, V_OML:V_OML + 1], ALU.mult)
                    link(V.tensor_scalar(sp[:, 24:32], vec[:, V_LAM:V_LAM + 8], -1.0, 0.0, ALU.mult, ALU.max))
                    dve.wait_ge(sp_ln, 1)
                    link(V.tensor_tensor(clh[:, :], sp[:, 24:32], sp[:, 16:24], ALU.add))
                    V.tensor_scalar(clh[:, :], clh[:, :], -4.0, None, ALU.mult).then_inc(prep, 1)
                    dve.wait_ge(early_row, l * 16 + 16)
                    dl = row[:, R_DL:R_DL + 256].rearrange("p (a b n) -> p a b n", a=2, b=2)
                    link(V.tensor_tensor(lprod[:, :].rearrange("p (a n) -> p a n", a=2), dl[:, :, 0, :], dl[:, :, 1, :],
                                         ALU.mult))
                    V.tensor_reduce(lam[:, 0:2], lprod[:, :].rearrange("p (a n) -> p a n", a=2), AX_X,
                                    ALU.add).then_inc(prep, 1)

                    def modulation(r, bank):
                        dve.wait_ge(ada_tr, r + 1)
                        src = ps[:, bank, :].rearrange("p (b j z) -> p j b z", b=4, j=4)[:, :, :, 0:G]
                        dst = modT[:, 16 * r:16 * r + 16, :].rearrange("p (j b) z -> p j b z", j=4)
                        bias = vec[:, V_ADAB + 16 * r:V_ADAB + 16 * r + 16].rearrange("p (j b) -> p j b", j=4)
                        link(V.tensor_tensor(dst, src, bias[:, :, :, None].broadcast_to((P, 4, 4, G)), ALU.add))
                        if r == 1:
                            V.tensor_scalar(g1h[:, :, :], modT[:, 16:24, :], 0.5, None, ALU.mult).then_inc(mod_rdy, 1)
                        else:
                            out, sc, nrm = ((A1, 8, V_N1), None, (A2, 32, V_N2))[r]
                            V.scalar_tensor_tensor(out=out[:, :, :], in0=modT[:, sc:sc + 8, :], scalar=1.0,
                                                   in1=vec[:, nrm:nrm + 8][:, :, None].broadcast_to((P, KC, G)),
                                                   op0=ALU.add, op1=ALU.mult).then_inc(mod_rdy, 1)

                    dve.wait_ge(ada_mm, 1)
                    V.tensor_copy(msb[0], ps[:, 0, :]).then_inc(ada_sb, 1)
                    modulation(0, 3)

                    def modulate(i, scale, shift, ahead):
                        dve.wait_ge(mod_rdy, 1 + 2 * i)
                        for k in range(KC):
                            if k + 1 >= ahead and k + 1 < KC:
                                scaled_x(i, k + 1)
                            dve.wait_ge(hraw[i], k + 1)
                            V.tensor_scalar(hT[:, k, 0:P], hT[:, k, 0:P], scale[:, k, 0:1],
                                            modT[:, shift + k, 0:1], ALU.mult, ALU.add).then_inc(h_v[i], 1)

                    modulate(0, A1, 0, KC)

                    for u in range(4):
                        dve.wait_ge(win_mm, u + 1)
                        c0, w = (0, 512) if u < 2 else (512, 160)
                        V.tensor_copy(projm[:, u % 2, c0:c0 + w], ps[:, u, 0:w]).then_inc(win_v, 1)
                    dve.wait_ge(win_v, 4)
                    spare = at(E0 + 2048, G, 640)
                    for g in range(G):
                        V.tensor_tensor_reduce(out=spare[:, g, 0:Q_LORA], in0=projm[:, g, 0:Q_LORA],
                                               in1=projm[:, g, 0:Q_LORA], scale=1.0, scalar=0.0, op0=ALU.mult,
                                               op1=ALU.add, accum_out=ss[:, g:g + 1])
                        kv = projm[:, g, OFF_KVA:OFF_KVA + KV_LORA]
                        last = V.tensor_tensor_reduce(out=spare[:, g, 384:640], in0=kv, in1=kv, scale=1.0, scalar=0.0,
                                                      op0=ALU.mult, op1=ALU.add, accum_out=ss[:, 2 + g:3 + g])
                    link(last)
                    V.tensor_scalar(ss[:, 0:2], ss[:, 0:2], 1.0 / Q_LORA, EPS, ALU.mult, ALU.add)
                    link(V.tensor_scalar(ss[:, 2:4], ss[:, 2:4], 1.0 / KV_LORA, EPS, ALU.mult, ALU.add))
                    rsqrt(ss[:, 0:4])
                    for g in range(G):
                        V.tensor_scalar(projm[:, g, 0:Q_LORA], projm[:, g, 0:Q_LORA], ss[:, g:g + 1], None,
                                        ALU.mult)
                        kv = projm[:, g, OFF_KVA:OFF_KVA + KV_LORA]
                        last = V.scalar_tensor_tensor(out=kv, in0=kv, scalar=ss[:, 2 + g:3 + g],
                                                      in1=row[:, R_KVA:R_KVA + KV_LORA], op0=ALU.mult, op1=ALU.mult)
                    last.then_inc(mla_n, 1)

                    V.memset(xpad[:, :, :, 0:2], 0.0)
                    V.memset(xpad[:, :, :, P + 2:P + 3], 0.0)
                    for u in (4, 5):
                        dve.wait_ge(win_mm, u + 1)
                        V.tensor_copy(xpad[:, 2 * (u - 4):2 * (u - 4) + 2, :, 2:P + 2],
                                      ps[:, u, :].rearrange("p (c g n) -> p c g n", c=2, g=G)).then_inc(win_v, 1)
                    dve.wait_ge(win_v, 6)
                    for j in range(4):
                        for c in range(RC):
                            w = vec[:, V_CW + 4 * j + c:V_CW + 4 * j + c + 1]
                            o = xr[:, c, :].rearrange("p (g n) -> p g n", g=G)
                            if j == 0:
                                last = V.tensor_scalar(o, xpad[:, c, :, 0:P], w, vec[:, V_CB + c:V_CB + c + 1],
                                                       ALU.mult, ALU.add)
                            else:
                                last = V.scalar_tensor_tensor(out=o, in0=xpad[:, c, :, j:j + P], scalar=w, in1=o,
                                                              op0=ALU.mult, op1=ALU.add)
                        if j < 3:
                            link(last)
                    last.then_inc(conv_rdy, 1)

                    for b in range(3):
                        dve.wait_ge(p3_mm, 2 if b < 2 else 3)
                        V.tensor_scalar(qaT[:, b, :], ps[:, b // 2, (b % 2) * NT:(b % 2 + 1) * NT],
                                        vec[:, V_QA + b:V_QA + b + 1], None, ALU.mult).then_inc(p3_ev, 1)
                    for b in range(2):
                        dve.wait_ge(p3_mm, 4 + b)
                        V.tensor_copy(ckvT[:, b, :], ps[:, 6 + b, 0:384]).then_inc(p3_ev, 1)

                    def rotate(x, n, w, cos, sin):
                        swapped = scratch[:, 0:n * 4 * w].rearrange("p (h a b c) -> p h a b c", h=n, a=2, b=2)
                        for b in range(2):
                            s = sin.rearrange("p (a b c) -> p a b c", a=2, b=2)[:, :, b, :]
                            last_ = V.tensor_tensor(swapped[:, :, :, b, :], x[:, :, :, 1 - b, :],
                                                    s[:, None, :, :].broadcast_to((P, n, 2, w)), ALU.mult)
                        link(last_)
                        flat = x.rearrange("p h a b c -> p h (a b c)")
                        link(V.tensor_tensor(flat, flat, cos[:, None, :].broadcast_to((P, n, 4 * w)), ALU.mult))
                        return V.tensor_tensor(flat, flat, swapped.rearrange("p h a b c -> p h (a b c)"), ALU.add)

                    def axes(x, w):
                        return x.rearrange("p h (a b c) -> p h a b c", a=2, b=2)

                    def squares(x, n, w, dst):
                        s2 = scratch[:, 0:n * w].rearrange("p (h n) -> p h n", h=n)
                        link(V.tensor_tensor(s2, x, x, ALU.mult))
                        link(V.tensor_reduce(dst, s2, AX_X, ALU.add))

                    def scaled(x, n, w, r, gain, factor):
                        link(V.tensor_tensor(x, x, r[:, :, None].broadcast_to((P, n, w)), ALU.mult))
                        return V.scalar_tensor_tensor(out=x, in0=x, scalar=factor,
                                                      in1=gain[:, None, :].broadcast_to((P, n, w)), op0=ALU.mult,
                                                      op1=ALU.mult)

                    cosm, sinm = cst[:, C_CM:C_CM + ROPE], cst[:, C_SM:C_SM + ROPE]
                    cosd, sind = cst[:, C_CD:C_CD + DH], cst[:, C_SD:C_SD + DH]
                    dve.wait_ge(p4_ev, 4)
                    for g in range(G):
                        squares(q_tok[:, g, :, :], MLA_H, QK, ss[:, 8 * g:8 * g + 8])
                    link(V.tensor_scalar(ss[:, 0:16], ss[:, 0:16], 1.0 / QK, EPS, ALU.mult, ALU.add))
                    rsqrt(ss[:, 0:16])
                    for g in range(G):
                        last = scaled(q_tok[:, g, :, :], MLA_H, QK, ss[:, 8 * g:8 * g + 8], row[:, R_QN:R_QN + QK],
                                      float(QK) ** -0.5)
                        if g == 1:
                            link(last)
                            last = rotate(axes(q_tok[:, 1, :, NOPE:QK], 8), MLA_H, 8, cosm, sinm)
                        last.then_inc(qn_rdy, 1)
                        dve.wait_ge(qn_rdy, g + 1)
                    dve.wait_ge(ld_kr, 16)
                    kr = (projm[:, 0, 640:M_COLS], c_kr[:, :], projm[:, 1, 640:M_COLS])
                    for s in range(3):
                        dve.wait_ge(p4_ev, 2 * s + 6)
                        V.tensor_tensor_reduce(out=scratch[:, 512:544], in0=kr[s], in1=kr[s], scale=1.0,
                                               scalar=0.0, op0=ALU.mult, op1=ALU.add, accum_out=krs[:, s:s + 1])
                        r8 = ss[:, 8 * s:8 * s + 8]
                        squares(k_tok[:, s, :, 0:NOPE], MLA_H, NOPE, r8)
                        link(V.tensor_scalar(r8, r8, krs[:, s:s + 1], 1.0 / QK, ALU.add, ALU.mult))
                        link(V.tensor_scalar(r8, r8, EPS, None, ALU.add))
                    rsqrt(ss[:, 0:24])
                    for s in range(3):
                        r8 = ss[:, 8 * s:8 * s + 8]
                        link(V.tensor_copy(k_tok[:, s, :, NOPE:QK],
                                      kr[s][:, None, :].broadcast_to((P, MLA_H, ROPE))))
                        last = scaled(k_tok[:, s, :, :], MLA_H, QK, r8, row[:, R_KN:R_KN + QK], 1.0)
                        if s == 2:
                            link(last)
                            last = rotate(axes(k_tok[:, 2, :, NOPE:QK], 8), MLA_H, 8, cosm, sinm)
                        last.then_inc(kn_rdy, 1)
                        dve.wait_ge(kn_rdy, s + 1)
                    dve.wait_ge(conv_rdy, 1)
                    for d in range(2):
                        h = lru_h[d]
                        for half in range(2):
                            c = slice(2 * half, 2 * half + 2)
                            dve.wait_ge(lru_at, 4 * d + 2 * half + 2)
                            V.scalar_tensor_tensor(out=h[:, c, :], in0=h[:, c, :], scalar=1.0, in1=xr[:, c, :],
                                                   op0=ALU.add, op1=ALU.mult)
                            link(V.tensor_tensor(lru_u[:, :, :], lru_a[:, c, :], lru_a[:, c, :], ALU.mult))
                            link(V.scalar_tensor_tensor(out=lru_u[:, :, :], in0=lru_u[:, :, :], scalar=1.0,
                                                        in1=lru_t[:, c, :], op0=ALU.add, op1=ALU.mult))
                            V.tensor_scalar(lru_t[:, c, :], lru_u[:, :, :], -0.25, 2.0 ** -116, ALU.mult,
                                            ALU.max).then_inc(lru_w, 1)
                            dve.wait_ge(lru_w, 2 * d + half + 1)
                        for half in range(2):
                            c = slice(2 * half, 2 * half + 2)
                            dve.wait_ge(lru_sq, 2 * d + half + 1)
                            link(V.tensor_tensor(h[:, c, :], h[:, c, :], lru_t[:, c, :], ALU.mult))
                            for ch in (2 * half, 2 * half + 1):
                                for g in range(G):
                                    init = 0.0 if g == 0 else vec[:, V_ST + 4 * d + ch:V_ST + 4 * d + ch + 1]
                                    lo, hi = g * P, (g + 1) * P
                                    if d == 0:
                                        aa, bb = lru_a[:, ch, lo:hi], h[:, ch, lo:hi]
                                    else:
                                        aa, bb = lru_a[:, ch, lo:hi][:, ::-1], h[:, ch, lo:hi][:, ::-1]
                                    last = V.tensor_tensor_scan(bb, aa, bb, init, ALU.mult, ALU.add)
                        last.then_inc(lru_fr, 1)
                    dve.wait_ge(lru_fr, 2)
                    V.tensor_copy(fin[:, 0:4], lru_h[0][:, :, P - 1])
                    V.tensor_copy(fin[:, 4:8], lru_h[1][:, :, 0])
                    link(V.tensor_tensor(xr[:, :, :], lru_h[0][:, :, :], lru_h[1][:, :, :], ALU.add))
                    V.tensor_tensor(gel[:, :, :], xr[:, :, :], gel[:, :, :], ALU.mult).then_inc(lru_rdy, 1)

                    dve.wait_ge(win_a, 8)
                    for n in range(4):
                        squares(projd[:, n // 2, n % 2, :].rearrange("p (h n) -> p h n", n=DH), 8, DH,
                                ss[:, 8 * n:8 * n + 8])
                    link(V.tensor_scalar(ss[:, :], ss[:, :], 1.0 / DH, EPS, ALU.mult, ALU.add))
                    rsqrt(ss[:, :])
                    for n in range(4):
                        x = projd[:, n // 2, n % 2, :].rearrange("p (h n) -> p h n", n=DH)
                        gain = row[:, R_DQN:R_DQN + DH] if n < 2 else row[:, R_DKN:R_DKN + DH]
                        last = scaled(x, 8, DH, ss[:, 8 * n:8 * n + 8], gain, float(DH) ** -0.5 if n < 2 else 1.0)
                        if n % 2:
                            link(last)
                            last = rotate(axes(x, 16), 8, 16, cosd, sind)
                        last.then_inc(dn_rdy, 1)
                        dve.wait_ge(dn_rdy, n + 1)
                    dve.wait_ge(lam_exp, 1)
                    link(V.tensor_tensor(lam[:, 6:7], lam[:, 5:6], lam[:, 4:5], ALU.subtract))
                    link(V.tensor_tensor(lam[:, 7:8], lam[:, 6:7], vec[:, V_LI:V_LI + 1], ALU.subtract))
                    nlam = lam[:, 7:8]

                    done = [0]

                    def merge(n):
                        for _ in range(n):
                            j = done[0]
                            done[0] += 1
                            ch = j % 8
                            if j < 24:
                                f = MERGE.index(("proj", BRANCHES[j // 8], ch))
                                dve.wait_ge(f_mm, f + 1)
                                dve.wait_ge(f_ac, j + 1)
                                if j < 8:
                                    V.scalar_tensor_tensor(out=merged[:, ch, :], in0=tg[:, ch, :], scalar=1.0,
                                                           in1=merge_ps(f), op0=ALU.add,
                                                           op1=ALU.mult).then_inc(f_dv, 1)
                                else:
                                    dve.wait_ge(f_dv, j)
                                    link(V.scalar_tensor_tensor(out=mtmp, in0=tg[:, ch, :], scalar=1.0,
                                                                in1=merge_ps(f), op0=ALU.add, op1=ALU.mult))
                                    V.tensor_tensor(merged[:, ch, :], merged[:, ch, :], mtmp,
                                                    ALU.add).then_inc(f_dv, 1)
                            else:
                                f = MERGE.index(("out", 0, ch))
                                dve.wait_ge(f_mm, f + 1)
                                for g in range(G):
                                    c = slice(g * P, (g + 1) * P)
                                    last = V.scalar_tensor_tensor(out=xT[:, ch, c], in0=merge_ps(f)[:, c],
                                                                  scalar=g1h[:, ch, g:g + 1], in1=xT[:, ch, c],
                                                                  op0=ALU.mult, op1=ALU.add)
                                last.then_inc(f_dv, 1)

                    modulation(1, 1)
                    dve.wait_ge(mod_rdy, 2)
                    merge(1)

                    def qk_copy(u):
                        n = QK if u < 8 else P
                        dve.wait_ge(t_mm, 2 * u + 1)
                        V.tensor_copy(qkT[u % 2][0:n, 0:384], ps[0:n, 0, 0:384]).then_inc(qk_v, 1)

                    qk_copy(0)
                    for u in range(12):
                        j = u % 2
                        dve.wait_ge(s_mm, u + 1)
                        if u < 8:
                            V.tensor_reduce(nm[:, j, 0:1], ps[:, 2 + j, 0:128], AX_X, ALU.max, negate=True)
                            V.tensor_reduce(nm[:, j, 1:2], ps[:, 2 + j, 128:384], AX_X, ALU.max,
                                            negate=True).then_inc(nm_v, 1)
                        else:
                            V.tensor_reduce(nm[:, j, 0:2], ps[:, 2:4, 0:128], AX_X, ALU.max, negate=True)
                            V.tensor_reduce(nm[:, j, 2:4], ps[:, 2:4, 128:384], AX_X, ALU.max,
                                            negate=True).then_inc(nm_v, 1)
                        if u < 11:
                            qk_copy(u + 1)
                        dve.wait_ge(ex_a, u + 1)
                        if u < 8:
                            link(V.reciprocal(rcp[:, j, 0:2], sums[:, j, 0:2]))
                            for n, c in enumerate((slice(0, 128), slice(128, 384))):
                                last = V.tensor_scalar(probs[j][:, 0, c], probs[j][:, 0, c], rcp[:, j, n:n + 1],
                                                       None, ALU.mult)
                        else:
                            link(V.reciprocal(rcp[:, j, :], sums[:, j, :]))
                            V.tensor_scalar(nl[:, :], rcp[:, j, :].rearrange("p (n m) -> p n m", m=2)[:, :, 1], nlam,
                                            None, ALU.mult)
                            for n, c in enumerate((slice(0, 128), slice(128, 384))):
                                last = V.tensor_scalar(probs[j][:, 0, c], probs[j][:, 0, c],
                                                       rcp[:, j, 2 * n:2 * n + 1], None, ALU.mult)
                            link(last)
                            for n, c in enumerate((slice(0, 128), slice(128, 384))):
                                last = V.scalar_tensor_tensor(out=probs[j][:, 0, c], in0=probs[j][:, 1, c],
                                                              scalar=nl[:, n:n + 1], in1=probs[j][:, 0, c],
                                                              op0=ALU.mult, op1=ALU.add)
                        last.then_inc(pn_v, 1)
                        if u != 7:
                            merge(1 if u < 7 else 2)
                        if u < 8 and u % 2:
                            dve.wait_ge(pv_mm, u + 1)
                            V.tensor_copy(omla[:, u // 2, :], ps[:, 5, 0:NT]).then_inc(om_ev, 1)
                        if u >= 8:
                            dve.wait_ge(pv_mm, u + 1)
                            if u > 8:
                                dve.wait_ge(ot_mm, u - 8)
                            link(V.tensor_copy(on[:, :, :], ps[:, 5, 0:NT].rearrange("p (g n) -> p g n", g=G)))
                            for g in range(G):
                                last = V.tensor_tensor_reduce(out=onsq[:, g, :], in0=on[:, g, :],
                                                              in1=on[:, g, :], scale=1.0, scalar=0.0, op0=ALU.mult,
                                                              op1=ALU.add, accum_out=ss[:, g:g + 1])
                            link(last)
                            link(V.tensor_scalar(ss[:, 0:2], ss[:, 0:2], 1.0 / DV, EPS, ALU.mult, ALU.add))
                            rsqrt(ss[:, 0:2])
                            for g in range(G):
                                last = V.tensor_scalar(on[:, g, :], on[:, g, :], ss[:, g:g + 1], None, ALU.mult)
                            last.then_inc(on_v, 1)
                    merge(8)
                    modulation(2, 1)
                    merge(8)

                    dve.wait_ge(f_dv, 32)
                    norm_scale(1)
                    scaled_x(1, 0)
                    modulate(1, A2, 24, 1)

                    V.memset(pmT[:, :, :], -1.0)
                    V.memset(cwT[:, :, :], 0.0)
                    link(V.memset(eidf[:, :], 0.0))
                    V.tensor_copy(eidf[:, 0:2 * FIRST], cst[:, C_EIDX:C_EIDX + 2 * FIRST])
                    dve.wait_ge(rt_mm, 1)
                    V.tensor_copy(lpart[:, :], ps[:, 1, 0:NT]).then_inc(lp_v, 1)
                    dve.wait_ge(fold_mm, 1)
                    rb = row[:, R_RB:R_RB + N_EXP]
                    link(V.tensor_tensor(lgt[:, :, :], ps[:, 1, 256:320].rearrange("p (g e) -> p g e", g=G),
                                         rb[:, None, :].broadcast_to((P, G, N_EXP)), ALU.add))
                    for g in range(G):
                        last = V.max(top8[:, g, :], lgt[:, g, :])
                    link(last)
                    V.tensor_scalar(nv1[:, :], top8[:, :, 0], -1.0, None, ALU.mult).then_inc(nv_v, 1)
                    link(V.memset(top8[:, :, TOP_K:8], -3e38))
                    for g in range(G):
                        last = V.match_replace(rep[:, g, :], top8[:, g, :], lgt[:, g, :], 3e38)
                    link(last)
                    V.tensor_tensor(msk[:, :, :], rep[:, :, :], lgt[:, :, :], ALU.not_equal).then_inc(msk_v, 1)

                    dve.wait_ge(msk_v, 1)
                    dve.wait_ge(pos_mm, 1)
                    V.tensor_copy(cnt[:, :], ps[:, 1, 128:160])
                    link(V.scalar_tensor_tensor(out=pm1[:, :, :], in0=ps[:, 1, 64:128].rearrange(
                        "p (g e) -> p g e", g=G), scalar=1.0, in1=msk[:, :, :], op0=ALU.add, op1=ALU.mult))
                    link(V.tensor_scalar(pmT[:, :, 0:2 * FIRST], pm1[:, :, 0:2 * FIRST], -1.0, None, ALU.add))

                    def tokens_onehot(t):
                        for i in range(2):
                            c = slice(SLOTS * i, SLOTS * (i + 1))
                            for g in range(G):
                                V.tensor_scalar(S_s[:, g, c], cst[:, C_IOTA:C_IOTA + SLOTS],
                                                pmT[:, g, bass.ds(t + i, 1)], None, ALU.is_equal)
                            last = V.tensor_scalar(oh[0:N_EXP, c],
                                                   cst[0:N_EXP, C_PIDX:C_PIDX + 1].broadcast_to((N_EXP, SLOTS)),
                                                   eidf[0:N_EXP, bass.ds(t + i, 1)], None, ALU.is_equal)
                        return last

                    def combine_onehot(t):
                        for i in range(2):
                            for g in range(G):
                                V.tensor_scalar(SC_s[:, g, SLOTS * i:SLOTS * (i + 1)],
                                                cst[:, C_IOTA:C_IOTA + SLOTS], pmT[:, g, bass.ds(t + i, 1)],
                                                cwT[:, g, bass.ds(t + i, 1)], ALU.is_equal, ALU.mult)

                    def gathered(n):
                        dve.wait_ge(ga_mm[1], n + 1)
                        V.tensor_copy(xTg[:, 4:8, :], ps[:, 3, :].rearrange("p (a b) -> p a b", a=4)).then_inc(xt_v, 1)

                    tokens_onehot(0).then_inc(disp, 1)
                    dve.wait_ge(exl_a, 1)
                    for g in range(G):
                        last = V.tensor_tensor_reduce(out=cmb[:, g, :], in0=exl[:, g, :], in1=msk[:, g, :], scale=1.0,
                                                      scalar=0.0, op0=ALU.mult, op1=ALU.add,
                                                      accum_out=den[:, g:g + 1])
                    link(last)
                    link(V.reciprocal(den[:, :], den[:, :]))
                    V.tensor_tensor(cmb[:, :, :], cmb[:, :, :], den[:, :, None].broadcast_to((P, G, N_EXP)),
                                    ALU.mult).then_inc(cmb_v, 1)
                    dve.wait_ge(cmb_v, 1)
                    V.tensor_copy(cwT[:, :, 0:2 * FIRST], cmb[:, :, 0:2 * FIRST])
                    gathered(0)
                    XT = 2 * FIRST
                    link(V.tensor_scalar(xtra[:, :], cnt[:, :], 64.5, None, ALU.is_gt))
                    for m in (128.5, 192.5):
                        link(V.scalar_tensor_tensor(out=xtra[:, :], in0=cnt[:, :], scalar=m, in1=xtra[:, :],
                                                    op0=ALU.is_gt, op1=ALU.add))
                    link(V.tensor_tensor_scan(tend[:, :], ones[:, 0:N_EXP], xtra[:, :], 0.0, ALU.mult, ALU.add))
                    link(V.tensor_tensor(tbeg[:, :], tend[:, :], xtra[:, :], ALU.subtract))
                    kk = cst[:, C_KK:C_KK + MAX_EXTRA][:, :, None].broadcast_to((P, MAX_EXTRA, N_EXP))

                    def over_e(v):
                        return v[:, None, :].broadcast_to((P, MAX_EXTRA, N_EXP))

                    V.tensor_tensor(sel[:, :, :], kk, over_e(tbeg), ALU.is_ge)
                    link(V.tensor_tensor(tmpx[:, :, :], kk, over_e(tend), ALU.is_lt))
                    link(V.tensor_tensor(sel[:, :, :], sel[:, :, :], tmpx[:, :, :], ALU.mult))
                    V.tensor_tensor(tmpx[:, :, :], sel[:, :, :], over_e(cst[:, C_EIDX:C_EIDX + N_EXP]), ALU.mult)
                    link(V.tensor_tensor(tmpy[:, :, :], kk, over_e(tbeg), ALU.subtract))
                    V.tensor_reduce(eidf[:, XT:XT + MAX_EXTRA], tmpx[:, :, :], AX_X, ALU.add)
                    link(V.scalar_tensor_tensor(out=tmpy[:, :, :], in0=tmpy[:, :, :], scalar=1.0, in1=sel[:, :, :],
                                                op0=ALU.add, op1=ALU.mult))
                    link(V.tensor_reduce(psub[:, :], tmpy[:, :, :], AX_X, ALU.add))
                    for g in range(G):
                        link(V.tensor_tensor(tmpx[:, :, :], sel[:, :, :], over_e(pm1[:, g, :]), ALU.mult))
                        link(V.tensor_tensor(tmpy[:, :, :], sel[:, :, :], over_e(cmb[:, g, :]), ALU.mult))
                        dst = pmT[:, g, XT:XT + MAX_EXTRA]
                        V.tensor_reduce(cwT[:, g, XT:XT + MAX_EXTRA], tmpy[:, :, :], AX_X, ALU.add)
                        link(V.tensor_reduce(dst, tmpx[:, :, :], AX_X, ALU.add))
                        link(V.scalar_tensor_tensor(out=dst, in0=psub[:, :], scalar=-float(SLOTS), in1=dst,
                                                    op0=ALU.mult, op1=ALU.add))
                        link(V.tensor_scalar(dst, dst, -1.0, None, ALU.add))
                    link(V.tensor_scalar(cmp8[:, :], cst[:, C_KK:C_KK + 8], 2.0, tend[:, N_EXP - 1:N_EXP], ALU.mult,
                                         ALU.is_lt))
                    link(V.tensor_reduce(npf[:, 0:1], cmp8[:, :], AX_X, ALU.add))
                    link(V.tensor_scalar(npf[:, 1:2], npf[:, 0:1], float(N_EXP // 2), None, ALU.add))
                    link(V.tensor_scalar(cmp8[:, :], cst[:, C_KK:C_KK + 8], 2.0, 1.0, ALU.mult, ALU.add))
                    link(V.tensor_scalar(cmp8[:, :], cmp8[:, :], tend[:, N_EXP - 1:N_EXP], None, ALU.is_lt))
                    V.tensor_copy(both[:, :], cmp8[:, :])
                    V.tensor_copy(eidi[:, :], eidf[:, XT:XT + MAX_EXTRA])
                    V.tensor_copy(meta[:, :], npf[:, :]).then_inc(routed, 1)
                    dve.wait_ge(routed, 1)
                    n_extra = dve.value_load(meta[0:1, 0:1], min_val=0, max_val=MAX_EXTRA // 2)
                    rest = bass.ds(n_extra * 2 + XT, N_EXP - XT)
                    V.tensor_copy(eidf[:, rest], cst[:, C_EIDX + XT:C_EIDX + N_EXP])
                    V.tensor_copy(cwT[:, :, rest], cmb[:, :, XT:N_EXP])
                    link(V.tensor_scalar(pmT[:, :, rest], pm1[:, :, XT:N_EXP], -1.0, None, ALU.add))

                    def pair(q):
                        dve.wait_ge(g1_mm[0], q + 1)
                        combine_onehot(q * 2)
                        tokens_onehot(q * 2 + 2).then_inc(disp, 1)
                        dve.wait_ge(g1_mm[1], q + 1)
                        V.tensor_scalar(gate_s, ps[:, 0, :], LIMIT, None, ALU.min).then_inc(gate_v, 1)
                        V.tensor_scalar(up_s, ps[:, 1, :], LIMIT, -LIMIT, ALU.min, ALU.max).then_inc(up_v, 1)
                        dve.wait_ge(up_v, q + 1)
                        V.scalar_tensor_tensor(out=up_s, in0=up_s, scalar=1.0, in1=gate_s, op0=ALU.add,
                                               op1=ALU.mult).then_inc(prod_v, 1)
                        dve.wait_ge(prod_v, q + 1)
                        dve.wait_ge(sig_a, q + 1)
                        V.tensor_tensor(act_s, up_s, sig_s, ALU.mult).then_inc(act_v, 1)
                        dve.wait_ge(at_mm, q + 1)
                        V.tensor_copy(actT.rearrange("p a b -> p (a b)"), ps[:, 0, :]).then_inc(at_ev, 1)
                        gathered(q + 1)
                        dve.wait_ge(g2_mm, q * 2 + 2)
                        V.tensor_copy(O_s[:, 512:1024], ps[:, 3, :]).then_inc(o_v, 1)
                    pair(0)
                    dve.wait_ge(routed, 1)
                    pairs = dve.value_load(meta[0:1, 1:2], min_val=N_EXP // 2, max_val=(N_EXP + MAX_EXTRA) // 2)
                    with dve.Fori(1, pairs) as q:
                        pair(q)
                    for k in range(KC):
                        if k % 2 == 0:
                            dve.wait_ge(sc_mm[k // 2], pairs)
                        for g in range(G):
                            c = slice(g * P, (g + 1) * P)
                            last = V.scalar_tensor_tensor(
                                out=xT[:, k, c], in0=ps[:, 4 + k // 2, (k % 2) * NT + g * P:(k % 2) * NT + (g + 1) * P],
                                scalar=modT[:, 40 + k, g:g + 1], in1=xT[:, k, c], op0=ALU.mult, op1=ALU.add)
                        last.then_inc(x_upd, 1)
            for i, s in enumerate(sems):
                (nc.gpsimd, nc.vector, nc.scalar, nc.tensor, nc.sync)[i % 5].sem_clear(s)
            nc.all_engine_barrier()


def constants(np):
    c = np.zeros((P, NC), np.float32)
    c[:, C_ID:C_ID + P] = np.eye(P)
    c[:, C_UT:C_UT + P] = np.triu(np.ones((P, P)), 1)
    c[:, C_ONE:C_ONE + P] = 1.0
    c[:, C_IOTA:C_IOTA + P] = np.tile(np.arange(SLOTS), 2)
    for dim, cc, cs in ((ROPE, C_CM, C_SM), (DH, C_CD, C_SD)):
        half = dim // 2
        inv = (1.0 / (np.float32(10000.0) ** (np.arange(0, half, 2, dtype=np.float32) / np.float32(half))))
        inv = inv.astype(np.float32)
        t = np.arange(P)
        ang = [((pos.astype(np.float32))[:, None] * inv[None, :]).astype(np.float32) for pos in (t // 64, t % 64)]
        ang = np.concatenate([ang[0], ang[0], ang[1], ang[1]], axis=1)
        sign = np.tile(np.repeat([-1.0, 1.0], half // 2), 2)
        c[:, cc:cc + dim] = np.cos(ang)
        c[:, cs:cs + dim] = np.sin(ang) * sign
    c[:, C_PIDX] = np.arange(P)
    c[:, C_EPS] = EPS
    c[:, C_FOLD:C_FOLD + N_EXP] = np.tile(np.eye(N_EXP), (P // N_EXP, 1))
    c[:, C_KK:C_KK + MAX_EXTRA] = np.arange(MAX_EXTRA)
    c[:, C_EIDX:C_EIDX + N_EXP] = np.arange(N_EXP)
    return c


def kernel(**inputs):
    import math

    import numpy as np
    import concourse.bacc as _bacc
    from concourse import mybir as _mybir
    from concourse.bass_utils import run_bass_kernel_spmd as _run

    a = {k: np.asarray(v) for k, v in inputs.items()}

    def columns(x):
        return x.reshape(L, -1, P).transpose(0, 2, 1)

    x = np.concatenate([a["x_prompt"][0], a["x_sample"][0]], axis=0)
    cond = np.stack([a["c_ctx"], a["c"][0]], axis=0)
    lam_init = np.array([0.8 - 0.6 * math.exp(-0.3 * i) for i in range(L)])
    li = np.zeros((L, P, 2), np.float32)
    li[:, :, 0] = lam_init[:, None]
    li[:, :, 1] = 1.0 - lam_init[:, None]
    vecs = np.concatenate([columns(v) for v in (
        a["ada_b"], a["norm1_g"], a["norm2_g"], a["b_merge"], a["mla_qa_norm"], a["diff_subln"],
        a["lru_conv_w"].reshape(L, -1), a["lru_conv_b"], a["lru_gate_b"].reshape(L, -1),
        a["lru_lambda"].reshape(L, -1), a["state_lru"][0].reshape(L, -1))] + [li], axis=2)
    rows = np.concatenate([a["mla_kva_norm"], a["mla_qn"], a["mla_kn"], a["diff_qn"], a["diff_kn"],
                           a["diff_lambda"].reshape(L, -1), a["router_b"]], axis=1)
    arrays = {
        "x_in": x.T.reshape(KC, P, NT).transpose(1, 0, 2),
        "cond_in": cond.T.reshape(KC, P, G).transpose(1, 0, 2),
        "consts": constants(np), "vecs": vecs, "rows": rows,
        "ada_w": a["ada_w"], "w_in": a["w_in"], "w_q_b": a["w_q_b"], "w_kv_b": a["w_kv_b"],
        "lru_gate_w": a["lru_gate_w"].reshape(L, 32, 64, 64),
        "w_o_mla": a["w_o_mla"], "w_o_lru": a["w_o_lru"], "w_o_diff": a["w_o_diff"],
        "w_merge": a["w_merge"], "w_out": a["w_out"], "router_w": a["router_w"],
        "exp_w1": a["exp_w1"].reshape(L * N_EXP, D, 2 * D_EXP), "exp_b1": a["exp_b1"],
        "exp_w2": a["exp_w2"].reshape(L * N_EXP, D_EXP, D), "exp_b2": a["exp_b2"],
        "cache_ckv": a["cache_mla_ckv"][0], "cache_krope": a["cache_mla_krope"][0],
        "cache_dk": a["cache_diff_k"][0].reshape(L, P, 512), "cache_dv": a["cache_diff_v"][0].reshape(L, P, 512),
    }
    outs = {"y_out": (P, KC, NT), "new_ckv": (L, P, KV_LORA), "new_krope": (L, P, ROPE), "new_lru": (L, P, 8),
            "new_dk": (L, P, 512), "new_dv": (L, P, 512)}
    nc = _bacc.Bacc("TRN2", target_bir_lowering=False, num_devices=1)
    given, args = {}, []
    for name, v in arrays.items():
        given[f"{name}_dram"] = np.ascontiguousarray(v)
        args.append(nc.dram_tensor(f"{name}_dram", v.shape, _mybir.dt.float32, kind="ExternalInput").ap())
    for name, shape in outs.items():
        args.append(nc.dram_tensor(f"{name}_dram", shape, _mybir.dt.float32, kind="ExternalOutput").ap())
    build(nc, *args)
    r = _run(nc, [given], core_ids=[0]).results[0]
    y = r["y_out_dram"].transpose(1, 0, 2).reshape(D, NT).T
    return (np.ascontiguousarray(y[:P])[None], np.ascontiguousarray(y[P:])[None],
            r["new_ckv_dram"][None], r["new_krope_dram"][None],
            np.ascontiguousarray(r["new_lru_dram"].transpose(0, 2, 1)).reshape(1, L, 2, D_RNN),
            r["new_dk_dram"].reshape(1, L, P, DIFF_H, 2, DH), r["new_dv_dram"].reshape(1, L, P, DIFF_H, DV))
```
